# Optimizing a Trainium2 kernel written in Bass

```python
import math
import jax, jax.numpy as jnp
from jax import lax
import numpy as np

D_MODEL = 2048
BATCH = 1
SEQ = 512
DEPTH = 1
DEC_BATCH = 1
DEC_SEQ = 32
PAST_LEN = 512

CHUNK = 64
MIX_WIDTH = D_MODEL
A_DK = 64
A_DV = 2 * A_DK
A_HEADS = (MIX_WIDTH // 2) // A_DV
B_DH = 64
B_HEADS = (MIX_WIDTH // 2) // B_DH
B_KV_HEADS = B_HEADS // 4
B_GROUP = B_HEADS // B_KV_HEADS
WINDOW = 128
WINDOW_CHUNKS = WINDOW // CHUNK
D_FF = ((11 * D_MODEL // 4) + 127) // 128 * 128
CONV_W = 3
Q_BLOCK = 128
EPS = 1e-6
NEG = -1e30

A_QW = A_HEADS * 2 * A_DK
A_KW = A_HEADS * 2 * A_DK
A_VW = A_HEADS * A_DV
B_QW = B_HEADS * B_DH
B_KW = B_KV_HEADS * B_DH
B_VW = B_KV_HEADS * B_DH
IN_WIDTH = A_QW + A_KW + A_VW + B_QW + B_KW + B_VW
IN_SPLITS = [A_QW, A_QW + A_KW, A_QW + A_KW + A_VW, A_QW + A_KW + A_VW + B_QW,
             A_QW + A_KW + A_VW + B_QW + B_KW]

kernel_name = 'hybrid_diffattn_sinkswa_convffn_stream'

def rmsnorm(x, g):
    xf = x.astype(jnp.float32)
    y = xf * lax.rsqrt(jnp.mean(xf * xf, axis=-1, keepdims=True) + EPS)
    return (y * g.astype(jnp.float32)).astype(x.dtype)

def alibi_slopes(n):
    return jnp.asarray(np.array([2.0 ** (-8.0 * (i + 1) / n) for i in range(n)], dtype=np.float32))

def diff_attention(q, k, v, q_pos, k_pos, lam, slopes):
    b, tq = q.shape[0], q.shape[1]
    qb = Q_BLOCK if tq % Q_BLOCK == 0 else tq
    nb = tq // qb
    q_blocks = jnp.moveaxis(q.reshape(b, nb, qb, A_HEADS, 2, A_DK), 1, 0)
    p_blocks = q_pos.reshape(nb, qb)
    k_chunk = k_pos // CHUNK
    scale = A_DK ** -0.5

    def one_block(args):
        qblk, pblk = args
        s = jnp.einsum('bqhmd,bkhmd->bhmqk', qblk, k).astype(jnp.float32) * scale
        dist = jnp.abs(pblk[:, None] - k_pos[None, :]).astype(jnp.float32)
        s = s - slopes[None, :, None, None, None] * dist
        allowed = k_chunk[None, :] <= (pblk // CHUNK)[:, None]
        s = jnp.where(allowed, s, NEG)
        p = jax.nn.softmax(s, axis=-1)
        w = p[:, :, 0] - lam * p[:, :, 1]
        return jnp.einsum('bhqk,bkhd->bqhd', w.astype(v.dtype), v)

    out = lax.map(one_block, (q_blocks, p_blocks))
    return jnp.moveaxis(out, 0, 1).reshape(b, tq, A_HEADS, A_DV)

def sink_band_attention(q, k, v, q_pos, k_pos, sinks, slopes):
    b, n, tq = q.shape[0], q.shape[1], q.shape[2]
    qg = q.reshape(b, n, tq, B_KV_HEADS, B_GROUP, B_DH)
    s = jnp.einsum('bnqhgd,bnkhd->bnhgqk', qg, k).astype(jnp.float32) * (B_DH ** -0.5)
    dq = q_pos[:, :, None]
    dk = k_pos[:, None, :]
    cdiff = dq // CHUNK - dk // CHUNK
    allowed = (cdiff >= 0) & (cdiff <= WINDOW_CHUNKS) & (dk >= 0)
    dist = jnp.abs(dq - dk).astype(jnp.float32)
    sl = slopes.reshape(1, 1, B_KV_HEADS, B_GROUP, 1, 1)
    s = s - sl * dist[None, :, None, None]
    s = jnp.where(allowed[None, :, None, None], s, NEG)
    sk = sinks.astype(jnp.float32).reshape(1, 1, B_KV_HEADS, B_GROUP, 1, 1)
    m = jnp.maximum(jnp.max(s, axis=-1, keepdims=True), sk)
    e = jnp.exp(s - m)
    p = e / (jnp.sum(e, axis=-1, keepdims=True) + jnp.exp(sk - m))
    o = jnp.einsum('bnhgqk,bnkhd->bnqhgd', p.astype(v.dtype), v)
    return o.reshape(b, n, tq, B_HEADS, B_DH)

def band_prompt(qb, kb, vb, sinks, slopes):
    b, t = qb.shape[0], qb.shape[1]
    nc = t // CHUNK
    pad = WINDOW_CHUNKS * CHUNK
    idx = jnp.arange(nc)[:, None] + jnp.arange(WINDOW_CHUNKS + 1)[None, :]

    def band(a):
        ap = jnp.pad(a, ((0, 0), (pad, 0), (0, 0), (0, 0)))
        ac = ap.reshape(b, nc + WINDOW_CHUNKS, CHUNK, B_KV_HEADS, B_DH)[:, idx]
        return ac.reshape(b, nc, (WINDOW_CHUNKS + 1) * CHUNK, B_KV_HEADS, B_DH)

    kpos = (jnp.arange(t + pad) - pad).reshape(nc + WINDOW_CHUNKS, CHUNK)[idx].reshape(nc, -1)
    qpos = jnp.arange(t).reshape(nc, CHUNK)
    o = sink_band_attention(qb.reshape(b, nc, CHUNK, B_HEADS, B_DH), band(kb), band(vb),
                            qpos, kpos, sinks, slopes)
    return o.reshape(b, t, B_HEADS, B_DH)

def band_sample(qb, kb, vb, cache_k, cache_v, offset, sinks, slopes):
    b, t = qb.shape[0], qb.shape[1]
    wbuf = cache_k.shape[1]
    k_all = jnp.concatenate([cache_k, kb], axis=1)
    v_all = jnp.concatenate([cache_v, vb], axis=1)
    kpos = (offset - wbuf + jnp.arange(wbuf + t))[None]
    qpos = (offset + jnp.arange(t))[None]
    o = sink_band_attention(qb[:, None], k_all[:, None], v_all[:, None], qpos, kpos, sinks, slopes)[:, 0]
    return o, k_all[:, -wbuf:], v_all[:, -wbuf:]

def conv_ffn(h, conv_state, w_up, conv_w, conv_b, w_down):
    u = h @ w_up
    t = u.shape[1]
    ext = jnp.concatenate([conv_state, u], axis=1)
    y = conv_b + conv_w[0] * ext[:, 0:t]
    for j in range(1, CONV_W):
        y = y + conv_w[j] * ext[:, j:j + t]
    gate, val = jnp.split(y, 2, axis=-1)
    out = (jax.nn.silu(gate) * val) @ w_down
    return out, ext[:, -(CONV_W - 1):]

def run_group(x, c, past, w_mod, b_mod, g_attn, w_in, lambda_q1, lambda_k1, lambda_q2, lambda_k2,
              subln_g, sinks, w_out, g_ffn, w_up, conv_w, conv_b, w_down, g_final):
    b, t, _ = x.shape
    offset = 0 if past is None else past[0].shape[2]
    q_pos = offset + jnp.arange(t, dtype=jnp.int32)
    slopes_a = alibi_slopes(A_HEADS)
    slopes_b = alibi_slopes(B_HEADS)
    cs = jax.nn.silu(c)
    new_ak, new_av, new_bk, new_bv, new_conv = [], [], [], [], []
    for li in range(DEPTH):
        lambda_init = 0.8 - 0.6 * math.exp(-0.3 * li)
        mod = cs @ w_mod[li] + b_mod[li]
        sh_a, sc_a, gt_a, sh_f, sc_f, gt_f = [m[:, None, :] for m in jnp.split(mod, 6, axis=-1)]
        h = rmsnorm(x, g_attn[li]) * (1.0 + sc_a) + sh_a
        z = h @ w_in[li]
        za_q, za_k, za_v, zb_q, zb_k, zb_v = jnp.split(z, IN_SPLITS, axis=-1)
        ka_rows = za_k.reshape(b, t, A_HEADS, 2 * A_DK)
        va_rows = za_v.reshape(b, t, A_HEADS, A_DV)
        if past is None:
            ka_all, va_all = ka_rows, va_rows
            k_pos_a = q_pos
        else:
            ka_all = jnp.concatenate([past[0][li], ka_rows], axis=1)
            va_all = jnp.concatenate([past[1][li], va_rows], axis=1)
            k_pos_a = jnp.arange(offset + t, dtype=jnp.int32)
        lam = (jnp.exp(jnp.sum(lambda_q1[li].astype(jnp.float32) * lambda_k1[li].astype(jnp.float32)))
               - jnp.exp(jnp.sum(lambda_q2[li].astype(jnp.float32) * lambda_k2[li].astype(jnp.float32)))
               + lambda_init)
        oa = diff_attention(za_q.reshape(b, t, A_HEADS, 2, A_DK),
                            ka_all.reshape(b, -1, A_HEADS, 2, A_DK), va_all,
                            q_pos, k_pos_a, lam, slopes_a)
        oa = rmsnorm(oa, subln_g[li]) * (1.0 - lambda_init)
        new_ak.append(ka_rows)
        new_av.append(va_rows)
        qb = zb_q.reshape(b, t, B_HEADS, B_DH)
        kb = zb_k.reshape(b, t, B_KV_HEADS, B_DH)
        vb = zb_v.reshape(b, t, B_KV_HEADS, B_DH)
        if past is None:
            ob = band_prompt(qb, kb, vb, sinks[li], slopes_b)
            wkeep = min(WINDOW, t)
            kbuf, vbuf = kb[:, -wkeep:], vb[:, -wkeep:]
        else:
            ob, kbuf, vbuf = band_sample(qb, kb, vb, past[2][li], past[3][li], offset, sinks[li], slopes_b)
        new_bk.append(kbuf)
        new_bv.append(vbuf)
        o = jnp.concatenate([oa.reshape(b, t, A_VW), ob.reshape(b, t, B_QW)], axis=-1) @ w_out[li]
        x = x + gt_a * o
        h2 = rmsnorm(x, g_ffn[li]) * (1.0 + sc_f) + sh_f
        cstate = jnp.zeros((b, CONV_W - 1, 2 * D_FF), x.dtype) if past is None else past[4][li]
        f, cnew = conv_ffn(h2, cstate, w_up[li], conv_w[li], conv_b[li], w_down[li])
        new_conv.append(cnew)
        x = x + gt_f * f
    y = rmsnorm(x, g_final)
    return (y, jnp.stack(new_ak), jnp.stack(new_av), jnp.stack(new_bk), jnp.stack(new_bv), jnp.stack(new_conv))

def setup_inputs(seed: int = 0) -> dict:
    key = jax.random.key(seed)
    ks = jax.random.split(key, 32)
    f32 = jnp.float32

    def nrm(k, shape, s=1.0):
        return jax.random.normal(k, shape, f32) * s

    wbuf = min(WINDOW, PAST_LEN)
    return {
        'x_prompt': nrm(ks[0], (BATCH, SEQ, D_MODEL)),
        'x_sample': nrm(ks[1], (DEC_BATCH, DEC_SEQ, D_MODEL)),
        'cache_a_k': nrm(ks[2], (DEPTH, DEC_BATCH, PAST_LEN, A_HEADS, 2 * A_DK)),
        'cache_a_v': nrm(ks[3], (DEPTH, DEC_BATCH, PAST_LEN, A_HEADS, A_DV)),
        'cache_b_k': nrm(ks[4], (DEPTH, DEC_BATCH, wbuf, B_KV_HEADS, B_DH)),
        'cache_b_v': nrm(ks[5], (DEPTH, DEC_BATCH, wbuf, B_KV_HEADS, B_DH)),
        'state_conv': nrm(ks[6], (DEPTH, DEC_BATCH, CONV_W - 1, 2 * D_FF)),
        'c_prompt': nrm(ks[7], (BATCH, D_MODEL)),
        'c_sample': nrm(ks[8], (DEC_BATCH, D_MODEL)),
        'w_mod': nrm(ks[9], (DEPTH, D_MODEL, 6 * D_MODEL), 0.5 * D_MODEL ** -0.5),
        'b_mod': nrm(ks[10], (DEPTH, 6 * D_MODEL), 0.02),
        'g_attn': 1.0 + nrm(ks[11], (DEPTH, D_MODEL), 0.02),
        'w_in': nrm(ks[12], (DEPTH, D_MODEL, IN_WIDTH), D_MODEL ** -0.5),
        'lambda_q1': nrm(ks[13], (DEPTH, A_DK), 0.1),
        'lambda_k1': nrm(ks[14], (DEPTH, A_DK), 0.1),
        'lambda_q2': nrm(ks[15], (DEPTH, A_DK), 0.1),
        'lambda_k2': nrm(ks[16], (DEPTH, A_DK), 0.1),
        'subln_g': 1.0 + nrm(ks[17], (DEPTH, A_DV), 0.02),
        'sinks': nrm(ks[18], (DEPTH, B_HEADS), 0.5),
        'w_out': nrm(ks[19], (DEPTH, MIX_WIDTH, D_MODEL), MIX_WIDTH ** -0.5),
        'g_ffn': 1.0 + nrm(ks[20], (DEPTH, D_MODEL), 0.02),
        'w_up': nrm(ks[21], (DEPTH, D_MODEL, 2 * D_FF), D_MODEL ** -0.5),
        'conv_w': nrm(ks[22], (DEPTH, CONV_W, 2 * D_FF), CONV_W ** -0.5),
        'conv_b': nrm(ks[23], (DEPTH, 2 * D_FF), 0.02),
        'w_down': nrm(ks[24], (DEPTH, D_FF, D_MODEL), D_FF ** -0.5),
        'g_final': 1.0 + nrm(ks[25], (D_MODEL,), 0.02),
    }

def reference(x_prompt, x_sample, cache_a_k, cache_a_v, cache_b_k, cache_b_v, state_conv,
              c_prompt, c_sample, w_mod, b_mod, g_attn, w_in, lambda_q1, lambda_k1, lambda_q2,
              lambda_k2, subln_g, sinks, w_out, g_ffn, w_up, conv_w, conv_b, w_down, g_final):
    y_prompt, ak_p, av_p, bk_p, bv_p, conv_p = run_group(
        x_prompt, c_prompt, None, w_mod, b_mod, g_attn, w_in, lambda_q1, lambda_k1, lambda_q2,
        lambda_k2, subln_g, sinks, w_out, g_ffn, w_up, conv_w, conv_b, w_down, g_final)
    past = (cache_a_k, cache_a_v, cache_b_k, cache_b_v, state_conv)
    y_sample, ak_s, av_s, bk_s, bv_s, conv_s = run_group(
        x_sample, c_sample, past, w_mod, b_mod, g_attn, w_in, lambda_q1, lambda_k1, lambda_q2,
        lambda_k2, subln_g, sinks, w_out, g_ffn, w_up, conv_w, conv_b, w_down, g_final)
    return (y_prompt, y_sample, ak_p, av_p, bk_p, bv_p, conv_p, ak_s, av_s, bk_s, bv_s, conv_s)


_drawn_inputs = setup_inputs


def setup_inputs(seed=0):
    import zlib

    import numpy as np

    out = dict(_drawn_inputs(seed))
    spreads = {}
    factors = {'g_attn': 2.962,
     'lambda_q1': 6.235,
     'lambda_k1': 8.0,
     'lambda_q2': 6.141,
     'lambda_k2': 8.0,
     'subln_g': 23.526,
     'sinks': 64.0,
     'g_ffn': 8.034,
     'conv_b': 8.0,
     'g_final': 7.327,
     'cache_a_k': 4.114,
     'cache_a_v': 6.907}
    for name, (base, spread) in spreads.items():
        noise = np.random.default_rng([zlib.crc32(name.encode()), seed]).standard_normal(out[name].shape)
        drawn = base * np.exp(spread * noise) if base else spread * noise
        out[name] = __import__('jax').numpy.asarray(drawn.astype(out[name].dtype))
    for name, factor in factors.items():
        out[name] = (out[name] * factor).astype(out[name].dtype)
    return out
```

```python
from contextlib import ExitStack

import concourse.bass as bass
from concourse import mybir

F32 = mybir.dt.float32
F32R = mybir.dt.float32r
ALU = mybir.AluOpType
ACT = mybir.ActivationFunctionType
AX = mybir.AxisListType

P = 128
D = 2048
KT = D // P
TP, TS = 512, 32
T = TP + TS
QT = TP // P
H0 = T // 2
HALF = [(0, H0), (H0, T - H0)]
PIECES = [[(0, H0, 0)], [(H0, TP - H0, 0), (TP, TS, 1)]]
BLK = 8
CW = BLK * P
NR = 4
NW = 4
PAST = 512
CHUNK = 64
A_HEADS, A_DK, A_DV = 8, 64, 128
B_HEADS, B_DH, B_GROUP = 16, 64, 4
SCALE = A_DK ** -0.5
A_QW = A_HEADS * 2 * A_DK
DFF = 5632
FT = DFF // P
GRP = 4
NG = FT // GRP
EPS = 1e-6
LAMBDA_INIT = 0.2
NEG_LARGE = -2.0 ** 110
LOWEST = -3.0e38
ZSLABS = 36
ZH = 2 * ZSLABS
OH = 2 * KT
MOD_FIRST = 4
MOD_EARLY = 32
MOD_TILES = 96
SH_A, SC_A, GT_A, SH_F, SC_F, GT_F = range(0, MOD_TILES, KT)
MR = 4
TAB = 640


def slope_a(h):
    return 2.0 ** (-8.0 * (h + 1) / A_HEADS)


def slope_b(h):
    return 2.0 ** (-8.0 * (h + 1) / B_HEADS)


SLABS = [(x, h) for h in range(A_HEADS) for x in "qkv"]
for _m in range(2):
    SLABS += [("k", A_HEADS + _m), ("v", A_HEADS + _m)]
    SLABS += [("q", A_HEADS + 4 * _m + i) for i in range(4)]
SLAB_OF = {x: s for s, x in enumerate(SLABS)}


def kv_of(qi):
    return qi if qi < A_HEADS else A_HEADS + (qi - A_HEADS) // 4


TURNS = [(h, i) for h in range(A_HEADS) for i in range(6)]
TURNS += [(A_HEADS + u, i) for u in range(8) for i in range(4)]


def is_a(t):
    return TURNS[t][0] < A_HEADS


def has_out(t):
    return not (is_a(t) and TURNS[t][1] == 4)


def make_slots():
    turns = {6 * (h + 1) + i: [6 * h + i] for h in range(A_HEADS) for i in range(6)}
    items = {6 * (h + 1) + i: [(h, x)] for h in range(A_HEADS) for i, x in enumerate("vspk")}
    b = 6 * A_HEADS
    for u, first in ((0, 54), (1, 56), (2, 58), (4, 66), (5, 68), (6, 70)):
        for n in range(2):
            turns[first + n] = [b + 4 * u + 2 * n, b + 4 * u + 2 * n + 1]
    for n in range(4):
        turns[60 + n] = [b + 12 + n]
    items[52], items[53], items[54] = [(8, "v")], [(8, "s")], [(8, "p"), (8, "k")]
    items[64], items[65] = [(9, "v"), (9, "s")], [(9, "p"), (9, "k")]
    slots = []
    for hf in range(ZH):
        tt, ii = turns.get(hf, []), items.get(hf, [])
        n = max(1, len(tt), len(ii))
        for p in range(n):
            slots.append((hf, p, n, tt[p] if p < len(tt) else None, ii[p] if p < len(ii) else None))
    for t in range(b + 28, b + 32):
        slots.append((None, 0, 1, t, None))
    slots += [(None, 0, 1, None, None)] * 2
    return slots


SLOTS = make_slots()
TAIL = len(SLOTS) - 6
TAIL_SPLITS = [range(0, 4), range(4, 8), range(8, 11), range(11, 14), range(14, 15), range(15, 16)]


def segments(t):
    qi, i = TURNS[t]
    if qi < A_HEADS:
        if i < 4:
            n = P * (i + 1)
            return [(P, 512 * m, 512 * m, n, 512 - P * i, m, P * i, [("new", 0, n)], m) for m in range(2)]
        return [(TS, 0, 0, PAST + TS, 0, i - 4, TP, [("past", 0, PAST), ("new", TP, TS)], i - 4)]
    if i < 3:
        q0 = P * (i + 1)
        return [(P, 512 * e, 257 * e, 256, 256 * e, e, q0, [("new", q0 - P, 256)], e) for e in range(2)]
    out = [(P, 512 * e, 129 * e, P, 256 * e + P, e, 0, [("new", 0, P)], e) for e in range(2)]
    out += [(TS, 512 * e + P, 258 + 161 * e, P + TS, 256 * e, e, TP, [("past", 0, P), ("new", TP, TS)], 2 + e)
            for e in range(2)]
    return out


def pv_blocks(t):
    qi, i = TURNS[t]
    if qi < A_HEADS:
        if i < 4:
            return [(P, 0, P * i, [(P * j, P, "new", j, 0, P, 0, P * j) for j in range(i + 1)])]
        blocks = [(P * j, P, "past", j, 0, P, 0, TS * j) for j in range(4)]
        return [(TS, 0, TP, blocks + [(PAST, TS, "new", 4, 0, P, 0, P)])]
    if i < 3:
        return [(P, 0, P * (i + 1), [(257 * e + P * j, P, "new", i + j, 64 * e, 64, 64 * e, P * (2 * e + j))
                                     for e in range(2) for j in range(2)])]
    first = (P, 0, 0, [(129 * e, P, "new", 0, 64 * e, 64, 64 * e, P * e) for e in range(2)])
    blocks = []
    for e in range(2):
        blocks.append((258 + 161 * e, P, "past", 0, 64 * e, 64, P + 64 * e, 256 + 64 * e))
        blocks.append((258 + 161 * e + P, TS, "new", 4, 64 * e, 64, P + 64 * e, 256 + 64 * e + TS))
    return [first, (TS, P, TP, blocks)]


BANK6 = []
for _k, (_hf, _p, _n, _t, _x) in enumerate(SLOTS):
    if _k and SLOTS[_k - 1][3] is not None and has_out(SLOTS[_k - 1][3]):
        BANK6.append(("p", SLOTS[_k - 1][3]))
    if _x:
        BANK6.append(("x",) + _x)
USE6 = {x: n + 1 for n, x in enumerate(BANK6)}
OUTS = [t for t in range(len(TURNS)) if has_out(t)]
OUT_COUNT = {t: n + 1 for n, t in enumerate(OUTS)}
OUT_A = {t: n + 1 for n, t in enumerate([t for t in OUTS if is_a(t)])}
OUT_B = {t: n + 1 for n, t in enumerate([t for t in OUTS if not is_a(t)])}


def prev_out(k, back):
    t = SLOTS[k - back][3] if k >= back else None
    return t if t is not None and has_out(t) else None


STREAM = [("w", 0), ("w", 1)]
for _hf in range(ZH + OH):
    if MOD_FIRST <= _hf < MOD_FIRST + MOD_TILES - MOD_EARLY:
        STREAM += [("mod", _hf - MOD_FIRST, 0), ("mod", _hf - MOD_FIRST, 1)]
    if _hf + 2 < ZH + OH:
        STREAM.append(("w", _hf + 2))
RAW_OF = {x: r for r, x in enumerate(STREAM)}


def chunk_dmas(c):
    if c < ZH:
        x, qi = SLABS[c // 2]
        return 2 if x == "q" and qi >= A_HEADS else 1
    return 4 if c % 2 else 1


LOADED = {}
_count = [0] * NR
for _r, _x in enumerate(STREAM):
    _count[_r % NR] += 16 * (chunk_dmas(_x[1]) if _x[0] == "w" else 1)
    LOADED[_x] = _count[_r % NR]
FFN_RAW = list(_count)
FC0 = ZH + OH
assert len(STREAM) % NR == FC0 % NR == 0
LOOP_CHUNKS = 2 * GRP * 6
LAST_DOWN = 4 * GRP + LOOP_CHUNKS * (NG - 1) // 2
ROW_COUNTS = [2 * KT, MOD_TILES, 3 * KT] + [2 * FT] * 6
F_BANKS = (0, 6, 4)


def build(nc, A, O):
    w_in, w_out, w_mod = A["w_in"][0], A["w_out"][0], A["w_mod"][0]
    w_up, w_down = A["w_up"][0], A["w_down"][0]
    scratch = nc.dram_tensor("x_transposed", (KT, P, T), F32, kind="Internal").ap()

    ctx = ExitStack()
    with ctx:
        def on(stack, name, shape, dt=F32):
            return stack.enter_context(nc.sbuf_tensor(name, shape, dt))

        def sem(name):
            return ctx.enter_context(nc.semaphore(name))

        w_raw = [on(ctx, f"w_raw{i}", [P, CW]) for i in range(NR)]
        early = ExitStack()
        x_nat = [on(early, f"x_nat{i}", [P, D]) for i in range(QT)]
        early.close()
        w_hi = [on(ctx, f"w_hi{i}", [P, CW], F32R) for i in range(NW)]
        w_lo = [on(ctx, f"w_lo{i}", [P, CW], F32R) for i in range(NW)]
        cols = on(ctx, "cols", [P, 9, P])
        mod = on(ctx, "mod", [P, MOD_TILES, 2])
        cs = on(ctx, "cs", [P, KT, 2])
        ident = on(ctx, "ident", [P, P])
        ones = on(ctx, "ones", [P, P])
        tiny = on(ctx, "tiny", [P, 16])
        sinks = on(ctx, "sinks", [P, B_HEADS])
        stats = on(ctx, "stats", [P, 4, 20])
        eps, minus_half, neg_lam = tiny[:, 0:1], tiny[:, 1:2], tiny[:, 2:3]
        CT, BT, GT, CONV_W, CONV_B, STATE = 0, 1, 2, 3, 6, 7
        early = ExitStack()
        wm = [on(early, f"wm{i}", [P, KT, 256]) for i in range(MR)]
        early.close()
        y_nat = on(early, "y_nat", [P, QT + 1, D])
        early.close()
        x_hi = on(ctx, "x_hi", [P, KT, T], F32R)
        x_lo = on(ctx, "x_lo", [P, KT, T], F32R)
        st0 = ExitStack()
        xT = on(st0, "xT", [P, KT, T])
        x_nat.append(on(st0, "x_nat_sample", [P, D]))
        n0 = [on(st0, f"n0_{x}", [P, T]) for x in ("sq", "acc", "rstd", "t0", "t1", "h0", "h1")]
        rows = on(st0, "rows", [P, 9, P])
        st0.close()
        st1 = ExitStack()
        zq = [on(st1, f"zq{i}", [P, T]) for i in range(2)]
        zk = [on(st1, f"zk{i}", [P, T]) for i in range(2)]
        zv = on(st1, "zv", [P, T])
        v_nat = [on(st1, f"v_nat{i}", [P, 5 * P]) for i in range(2)]
        k_nat = on(st1, "k_nat", [P, 5 * P])
        past_k = on(st1, "past_k", [P, 4 * P])
        past_v = on(st1, "past_v", [P, 4 * P])
        past_kT = on(st1, "past_kT", [P, 4 * P])
        scores = [on(st1, f"scores{i}", [P, 1024]) for i in range(2)]
        probsT = on(st1, "probsT", [P, 512])
        o_raw = on(st1, "o_raw", [P, P])
        o_norm = on(st1, "o_norm", [P, 2 * P])
        square = on(st1, "square", [P, P])
        oT = on(st1, "oT", [P, KT, T])
        tab_a = on(st1, "tab_a", [P, TAB])
        tab_b = on(st1, "tab_b", [P, 256])
        tab = [on(st1, f"tab{i}", [P, TAB]) for i in range(2)]
        gsub = on(st1, "gsub", [P, P])
        st1.close()
        st2 = ExitStack()
        x1 = on(st2, "x1", [P, KT, T])
        st3 = st2
        ext = [on(st3, f"ext{i}", [P, TP + 2 * (TS + 2)]) for i in range(2)]
        cv = [on(st3, f"cv{i}", [P, T + 2]) for i in range(2)]
        n2_st = ExitStack()
        n2 = [on(n2_st, f"n2_{x}", [P, T]) for x in ("sq", "acc", "rstd")]
        n2_st.close()
        y_hi = [on(st3, f"y_hi{i}", [P, GRP, T], F32R) for i in range(2)]
        y_lo = [on(st3, f"y_lo{i}", [P, GRP, T], F32R) for i in range(2)]
        u_last = on(st3, "u_last", [P, 2 * FT, 4])
        u_rows = on(st3, "u_rows", [P, 4, P])
        st3.close()

        ps = ctx.enter_context(nc.psum_tensor("ps", [P, 8, 512], F32))
        psw = ps[:, :, :].rearrange("p b n -> p (b n)")

        def bank(b, n=1):
            return psw[:, 512 * b:512 * (b + n)]

        G = [bank(0), bank(1)]
        S = [bank(2, 2), bank(4, 2)]
        B6, B7 = bank(6), bank(7)

        ld_x, ld_rows, ld_small, scratch_out = sem("ld_x"), sem("ld_rows"), sem("ld_small"), sem("scratch_out")
        ld_m = [sem(f"ld_m{i}") for i in range(MR)]
        ld_raw = [sem(f"ld_raw{i}") for i in range(NR)]
        consts, rows_t, rows_ev, cs_ok = sem("consts"), sem("rows_t"), sem("rows_ev"), sem("cs_ok")
        xt_t, xt_ev = sem("xt_t"), sem("xt_ev")
        sq_ok, ss_ok, sd_ok, rs_ok = sem("sq_ok"), sem("ss_ok"), sem("sd_ok"), sem("rs_ok")
        m_used, m_late, mod_ok = sem("m_used"), sem("m_late"), sem("mod_ok")
        n_mul, n_aff, n_hi, x_ok = sem("n_mul"), sem("n_aff"), sem("n_hi"), sem("x_ok")
        act_own, dve_own, pool_own = sem("act_own"), sem("dve_own"), sem("pool_own")
        s_hi, s_lo = sem("s_hi"), sem("s_lo")
        g_done, g_free = sem("g_done"), sem("g_free")
        lam_dot, lam_exp, small_ok = sem("lam_dot"), sem("lam_exp"), sem("small_ok")
        tab_ok = sem("tab_ok")
        t_score, t_ttr, t_exp, t_comb = sem("t_score"), sem("t_ttr"), sem("t_exp"), sem("t_comb")
        b6_done, b6_free = sem("b6_done"), sem("b6_free")
        t_pv, t_o, t_rstd, t_on_a, t_on_b = sem("t_pv"), sem("t_o"), sem("t_rstd"), sem("t_on_a"), sem("t_on_b")
        t_ot, t_otev = sem("t_ot"), sem("t_otev")
        st_k, st_v, ld_pk, ld_pv = sem("st_k"), sem("st_v"), sem("ld_pk"), sem("ld_pv")
        xr = [sem(f"xr{i}") for i in range(4)]
        u_done, u_ev, c_gate, c_val, c_silu, y_mul, y_hi_ok, y_ok = (
            sem(x) for x in ("u_done", "u_ev", "c_gate", "c_val", "c_silu", "y_mul", "y_hi_ok", "y_ok"))
        d_done, d_ev = sem("d_done"), sem("d_ev")
        f_mul, f_t, f_eva, f_evd, store = sem("f_mul"), sem("f_t"), sem("f_eva"), sem("f_evd"), sem("store")
        uc_t, uc_ev = sem("uc_t"), sem("uc_ev")
        ld_sub, st_win, st_conv = sem("ld_sub"), sem("st_win"), sem("st_conv")
        ext_ok, cv_ok = sem("ext_ok"), sem("cv_ok")

        block = ctx.enter_context(nc.Block())

        def w_in_cols(s):
            x, i = SLABS[s]
            if i < A_HEADS:
                return [("qkv".index(x) * A_QW + P * i, P)]
            m, base = (i - A_HEADS) // 4 if x == "q" else i - A_HEADS, 3 * A_QW
            if x == "q":
                head = 2 * B_GROUP * m + (i - A_HEADS) % 4
                return [(base + B_DH * head, B_DH), (base + B_DH * (head + B_GROUP), B_DH)]
            return [(base + B_HEADS * B_DH + (256 if x == "v" else 0) + P * m, P)]

        @block.sync
        def _(sp):
            for t in range(QT):
                sp.dma_start(x_nat[t][:, :], A["x_prompt"][0, P * t:P * t + P, :]).then_inc(ld_x, 16)
            sp.dma_start(x_nat[QT][0:TS, :], A["x_sample"][0]).then_inc(ld_x, 16)
            for c in range(MOD_EARLY // 2):
                if c == 6:
                    sp.wait_ge(xt_ev, KT)
                    sp.dma_start(scratch.rearrange("k p t -> p k t"), xT[:, :, :]).then_inc(scratch_out, 16)
                if c >= MR:
                    sp.wait_ge(m_used, c - MR + 1)
                sp.dma_start(wm[c % MR][:, :, :],
                             w_mod[:, 256 * c:256 * c + 256].rearrange("(k p) n -> p k n", p=P)
                             ).then_inc(ld_m[c % MR], 16)
            for r, x in enumerate(STREAM):
                slot = r % NR
                if r >= NR:
                    old = STREAM[r - NR]
                    if old[0] == "w":
                        sp.wait_ge(s_lo, old[1] + 1)
                    else:
                        sp.wait_ge(m_late, old[1] + 1)
                dst = w_raw[slot][:, :].rearrange("p (k n) -> p k n", n=P)
                if x[0] == "mod":
                    c0 = P * (MOD_EARLY + x[1])
                    src = w_mod[1024 * x[2]:1024 * x[2] + 1024, c0:c0 + P]
                    sp.dma_start(dst, src.rearrange("(k p) n -> p k n", p=P)).then_inc(ld_raw[slot], 16)
                elif x[1] < ZH:
                    s, half = x[1] // 2, x[1] % 2
                    at = 0
                    for c0, n in w_in_cols(s):
                        src = w_in[1024 * half:1024 * half + 1024, c0:c0 + n]
                        sp.dma_start(dst[:, :, at:at + n], src.rearrange("(k p) n -> p k n", p=P)
                                     ).then_inc(ld_raw[slot], 16)
                        at += n
                else:
                    n, half = (x[1] - ZH) // 2, x[1] % 2
                    if half == 0:
                        sp.dma_start(dst, w_out[0:1024, P * n:P * n + P].rearrange("(k p) n -> p k n", p=P)
                                     ).then_inc(ld_raw[slot], 16)
                    else:
                        for u in range(2):
                            for m in range(2):
                                r0 = 1024 + 512 * m + 256 * u
                                src = w_out[r0:r0 + 256, P * n:P * n + P]
                                sp.dma_start(dst[64 * u:64 * u + 64, 4 * m:4 * m + 4, :],
                                             src.rearrange("(i p) n -> p i n", p=64)
                                             ).then_inc(ld_raw[slot], 16)

            def up(c, nth, j, k, base):
                slot = c % NR
                sp.wait_ge(s_lo, nth - NR + 1)
                sp.dma_start(w_raw[slot][:, :].rearrange("p (k n) -> p k n", n=P),
                             w_up[1024 * k:1024 * k + 1024, bass.ds(base + P * j, P)]
                             .rearrange("(k p) n -> p k n", p=P)).then_inc(ld_raw[slot], 16)

            def down(c, nth, g, n0_):
                slot = c % NR
                sp.wait_ge(s_lo, nth - NR + 1)
                sp.dma_start(w_raw[slot][:, :].rearrange("p (k n) -> p k n", n=256),
                             w_down[bass.ds(g * (GRP * P), GRP * P), P * n0_:P * n0_ + 256]
                             .rearrange("(k p) n -> p k n", p=P)).then_inc(ld_raw[slot], 16)

            for j in range(GRP):
                for n in range(4):
                    up(4 * j + n, FC0 + 4 * j + n, j, n % 2, DFF * (n // 2))
            with sp.Fori(0, NG - 1) as i:
                for jj in range(GRP):
                    for n in range(4):
                        up(6 * jj + n, i * 24 + (FC0 + 16 + 6 * jj + n), (i + 1) * GRP + jj, n % 2, DFF * (n // 2))
                    for n in range(2):
                        down(6 * jj + 4 + n, i * 24 + (FC0 + 16 + 6 * jj + 4 + n), i, 4 * jj + 2 * n)
            for n in range(8):
                down(n, FC0 + 16 + 24 * (NG - 1) + n, NG - 1, 2 * n)
            for q in range(4):
                sp.wait_ge(f_eva, 2 * (q + 1))
                sp.wait_ge(f_evd, 2 * (q + 1))
                sp.dma_start(O["y_p"][0, :, 512 * q:512 * q + 512].rearrange("(t p) n -> p t n", p=P),
                             y_nat[:, 0:QT, 512 * q:512 * q + 512]).then_inc(store, 16)
                sp.dma_start(O["y_s"][0, :, 512 * q:512 * q + 512],
                             y_nat[0:TS, QT, 512 * q:512 * q + 512]).then_inc(store, 16)
            sp.wait_ge(store, 16 * 8)

        @block.gpsimd
        def _(pool):
            own = [0]

            def step(ins):
                own[0] += 1
                ins.then_inc(pool_own, 1)
                pool.wait_ge(pool_own, own[0])

            pool.memset(ones[:, :], 1.0).then_inc(consts, 1)
            step(pool.memset(ident[:, :], 0.0))
            pool.affine_select(out=ident[:, :], in_=ident[:, :], compare_op=ALU.not_equal, fill=1.0, base=0,
                               pattern=[[-1, P]], channel_multiplier=1).then_inc(consts, 1)
            pool.memset(eps, EPS).then_inc(consts, 1)
            pool.memset(minus_half, -0.5).then_inc(consts, 1)

            def natural(ki, item):
                sem_, buf = (st_v, v_nat[ki % 2]) if item == "v" else (st_k, k_nat)
                pool.wait_ge(b6_free, USE6[("x", ki, item)])
                if item == "p":
                    return
                if item == "s":
                    lo = 0 if ki < A_HEADS else P - TS
                    for x, b, sm in (("v", v_nat[ki % 2], st_v), ("k", k_nat, st_k)):
                        if ki < A_HEADS:
                            dst = O[f"a{x}_s"][0, 0, :, ki, :]
                        else:
                            m = ki - A_HEADS
                            dst = O[f"b{x}_s"][0, 0, lo:, 2 * m:2 * m + 2, :].rearrange("t h d -> t (h d)")
                        pool.dma_start(dst, b[0:TS, 4 * P:5 * P]).then_inc(sm, 16)
                elif ki < A_HEADS:
                    dst = O[f"a{item}_p"][0, 0, :, ki, :].rearrange("(t p) d -> p t d", p=P)
                    pool.dma_start(dst, buf[:, 0:512].rearrange("p (t d) -> p t d", d=P)).then_inc(sem_, 16)
                else:
                    m = ki - A_HEADS
                    dst = O[f"b{item}_p"][0, 0, :, 2 * m:2 * m + 2, :].rearrange("t h d -> t (h d)")
                    pool.dma_start(dst, buf[:, 384:512]).then_inc(sem_, 16)

            def load_past(which, ki):
                buf, sm = (past_k, ld_pk) if which == "k" else (past_v, ld_pv)
                if ki < A_HEADS:
                    src = A[f"cache_a_{which}"][0, 0, :, ki, :].rearrange("(t p) d -> p t d", p=P)
                    pool.dma_start(buf[:, :].rearrange("p (t d) -> p t d", d=P), src).then_inc(sm, 16)
                else:
                    m = ki - A_HEADS
                    src = A[f"cache_b_{which}"][0, 0, :, 2 * m:2 * m + 2, :].rearrange("t h d -> t (h d)")
                    pool.dma_start(buf[:, 0:P], src).then_inc(sm, 16)

            for x in "kv":
                pool.dma_start(O[f"b{x}_s"][0, 0, 0:P - TS], A[f"cache_b_{x}"][0, 0, TS:P]).then_inc(st_win, 16)

            pool.wait_ge(x_ok, KT)
            pool.wait_ge(scratch_out, 16)
            load_past("k", 0)
            load_past("v", 0)
            pool.dma_start(gsub[:, :], A["subln_g"].partition_broadcast(P).rearrange("p a n -> p (a n)")
                           ).then_inc(ld_sub, 16)
            step(pool.iota(tab_a[:, :], pattern=[[1, TAB]], base=-512, channel_multiplier=-1,
                           allow_small_or_imprecise_dtypes=True))
            step(pool.tensor_scalar(tab[0][:, :], tab_a[:, :], -1.0, None, ALU.mult))
            step(pool.tensor_scalar(tab[1][:, :], tab_a[:, :], 0.0, -2.0, ALU.max, ALU.mult))
            step(pool.tensor_tensor(tab_a[:, :], tab_a[:, :], tab[1][:, :], ALU.add))
            step(pool.memset(tab_a[0:CHUNK, 512 + CHUNK:TAB], NEG_LARGE))
            step(pool.tensor_copy(tab_b[:, :], tab_a[:, 384:TAB]))
            step(pool.memset(tab_b[CHUNK:P, 0:CHUNK], NEG_LARGE))

            def table(qi):
                if qi >= 2:
                    last = max(t for t in range(len(TURNS)) if TURNS[t][0] == qi - 2)
                    pool.wait_ge(t_ttr, last + 1)
                if qi < A_HEADS:
                    pool.tensor_scalar(tab[qi % 2][:, :], tab_a[:, :], slope_a(qi), None, ALU.mult
                                       ).then_inc(tab_ok, 1)
                else:
                    m, i = (qi - A_HEADS) // 4, (qi - A_HEADS) % 4
                    for e in range(2):
                        ins = pool.tensor_scalar(tab[qi % 2][:, 256 * e:256 * e + 256], tab_b[:, :],
                                                 slope_b(8 * m + 4 * e + i), None, ALU.mult)
                    ins.then_inc(tab_ok, 1)

            def rstd(t):
                pool.wait_ge(t_o, OUT_A[t])
                n = pv_blocks(t)[0][0]
                s = stats[0:n, t % 4, :]
                step(pool.tensor_scalar(s[:, 18:19], s[:, 17:18], 1.0 / A_DV, EPS, ALU.mult, ALU.add))
                pool.tensor_tensor(s[:, 19:20], s[:, 18:19], minus_half[0:n, :], ALU.pow).then_inc(t_rstd, 1)

            table(0)
            next_table, next_pk, next_pv = 1, 1, 1
            for k, (hf, part, parts, t, item) in enumerate(SLOTS):
                pt = prev_out(k, 1)
                if pt is not None and is_a(pt):
                    rstd(pt)
                if t is not None and TURNS[t][1] == 0 and next_table < 16:
                    table(next_table)
                    next_table += 1
                if item:
                    natural(*item)
                    if item[1] == "p" and next_pk < 10:
                        load_past("k", next_pk)
                        next_pk += 1
                if pt is not None and TURNS[pt][1] == (5 if is_a(pt) else 3):
                    last_of_kv = pt + 1 == len(TURNS) or kv_of(TURNS[pt + 1][0]) != kv_of(TURNS[pt][0])
                    if last_of_kv and next_pv < 10:
                        pool.wait_ge(t_pv, OUT_COUNT[pt])
                        load_past("v", next_pv)
                        next_pv += 1
            pool.wait_ge(t_otev, len(OUTS))
            pool.wait_ge(st_k, 16 * 20)
            pool.wait_ge(st_v, 16 * 20)
            for q in range(4):
                pool.dma_start(x1[:, 4 * q:4 * q + 4, :], scratch[4 * q:4 * q + 4].rearrange("k p t -> p k t")
                               ).then_inc(xr[q], 16)
            pool.wait_ge(uc_ev, 1)
            for r in range(4):
                dst = O["conv_p" if r < 2 else "conv_s"][0, 0, r % 2, :].rearrange("(j p) -> j p", p=P)
                pool.dma_start(dst, u_rows[0:2 * FT, r, :]).then_inc(st_conv, 16)
            pool.wait_ge(st_conv, 64)
            pool.wait_ge(st_win, 32)

        @block.scalar
        def _(act):
            own = [0]

            def step(ins):
                own[0] += 1
                ins.then_inc(act_own, 1)
                act.wait_ge(act_own, own[0])

            tiled = lambda a: a.rearrange("(k p) -> k p", p=P)
            act.dma_start(rows[0:KT, 0, :], tiled(A["c_prompt"][0])).then_inc(ld_rows, 16)
            act.dma_start(rows[KT:2 * KT, 0, :], tiled(A["c_sample"][0])).then_inc(ld_rows, 16)
            act.dma_start(rows[0:MOD_TILES, BT, :], tiled(A["b_mod"][0])).then_inc(ld_rows, 16)
            act.dma_start(rows[0:KT, GT, :], tiled(A["g_attn"][0])).then_inc(ld_rows, 16)
            act.dma_start(rows[KT:2 * KT, GT, :], tiled(A["g_ffn"][0])).then_inc(ld_rows, 16)
            act.dma_start(rows[2 * KT:3 * KT, GT, :], tiled(A["g_final"])).then_inc(ld_rows, 16)
            for i in range(3):
                act.dma_start(rows[0:2 * FT, CONV_W + i, :], tiled(A["conv_w"][0, i])).then_inc(ld_rows, 16)
            act.dma_start(rows[0:2 * FT, CONV_B, :], tiled(A["conv_b"][0])).then_inc(ld_rows, 16)
            for i in range(2):
                act.dma_start(rows[0:2 * FT, STATE + i, :], tiled(A["state_conv"][0, 0, i])).then_inc(ld_rows, 16)
            bc = lambda a: a.partition_broadcast(P).rearrange("p a n -> p (a n)")
            act.dma_start(sinks[:, :], bc(A["sinks"])).then_inc(ld_small, 16)
            for i, x in enumerate(("q1", "k1", "q2", "k2")):
                act.dma_start(n0[2 + i][:, 0:A_DK], bc(A[f"lambda_{x}"])).then_inc(ld_small, 16)
            act.wait_ge(rows_ev, 1)
            act.activation(cs[:, :, :].rearrange("p k g -> p g k"),
                           cols[:, CT, 0:2 * KT].rearrange("p (g k) -> p g k", g=2), ACT.Silu).then_inc(cs_ok, 1)
            for kt in range(KT):
                act.wait_ge(xt_t, kt + 1)
                act.activation(xT[:, kt, :], bank(2 * (kt % 2), 2)[:, 0:T], ACT.Copy).then_inc(xt_ev, 1)
            act.wait_ge(lam_dot, 2)
            act.activation(tiny[:, 4:6], tiny[:, 6:8], ACT.Exp).then_inc(lam_exp, 1)

            def root(n, dst):
                act.wait_ge(ss_ok, n + 1)
                act.activation(dst, bank(4, 2)[:, 0:T], ACT.Sqrt, bias=eps, scale=1.0 / D).then_inc(sd_ok, 1)

            def affine(n, kt, src, h, scale_row, shift_row):
                act.wait_ge(n_mul, KT * n + kt + 1)
                if kt >= 2:
                    act.wait_ge(x_ok, KT * 2 * n + kt - 1)
                for a, c, g in ((0, TP, 0), (TP, TS, 1)):
                    ins = act.activation(h[:, a:a + c], src[:, a:a + c], ACT.Identity,
                                         bias=mod[:, shift_row + kt, g:g + 1],
                                         scale=mod[:, scale_row + kt, g:g + 1])
                step(ins)
                act.activation(x_hi[:, kt, :], h[:, 0:T], ACT.Copy).then_inc(n_hi, 1)

            act.wait_ge(consts, 4)
            root(0, n0[2][:, :])
            act.wait_ge(mod_ok, 1)
            for kt in range(KT):
                affine(0, kt, n0[3 + kt % 2], n0[5 + kt % 2], SC_A, SH_A)

            def hi(c, raw, count):
                act.wait_ge(ld_raw[raw], count)
                act.activation(w_hi[c % NW][:, :], w_raw[raw][:, :], ACT.Copy).then_inc(s_hi, 1)

            def hi_early(c):
                if c >= NW:
                    act.wait_ge(g_done, 2 * ((c - NW) // 2) + 2)
                hi(c, RAW_OF[("w", c)] % NR, LOADED[("w", c)])

            hi_early(0)
            hi_early(1)
            for k, (hf, part, parts, t, item) in enumerate(SLOTS):
                pt, pp = prev_out(k, 1), prev_out(k, 2)
                if pt is not None and is_a(pt):
                    act.wait_ge(b6_done, USE6[("p", pt)])
                    if pv_blocks(pt)[0][0] == P:
                        n = P * len(pv_blocks(pt)[0][3])
                        act.activation(probsT[:, 0:n], B6[:, 0:n], ACT.Copy).then_inc(b6_free, 1)
                    else:
                        act.activation(probsT[:, 0:P], B6[:, 0:P], ACT.Copy)
                        act.activation(probsT[0:TS, P:P + TS], B6[0:TS, P:P + TS], ACT.Copy).then_inc(b6_free, 1)
                if pp is not None:
                    act.wait_ge(t_ot, OUT_COUNT[pp])
                    for n, c, tok, _b in pv_blocks(pp):
                        ins = act.activation(oT[:, TURNS[pp][0], tok:tok + n],
                                             B7[:, 256 + c:256 + c + n], ACT.Copy)
                    ins.then_inc(t_otev, 1)
                if t is not None:
                    act.wait_ge(t_ttr, t + 1)
                    st = stats[:, t % 4, :]
                    for np_, _pc, sc, n, _tc, _e, _q, _k, i in segments(t):
                        n += 0 if is_a(t) else 1
                        sb = scores[t % 2][0:np_, sc:sc + n]
                        ins = act.activation(sb, sb, ACT.Exp, bias=st[0:np_, 4 + i:5 + i],
                                             accum_out=st[0:np_, 8 + i:9 + i])
                    ins.then_inc(t_exp, 1)
                if hf is not None and part == 0 and hf + 2 < FC0:
                    hi_early(hf + 2)
                if hf is None:
                    for kt in TAIL_SPLITS[k - TAIL]:
                        act.wait_ge(g_done, ZH)
                        act.wait_ge(t_otev, len(OUTS) if kt == KT - 1 else OUT_COUNT[4 * (kt - 8) + 51] if kt >= 8
                                    else OUT_COUNT[6 * kt + 5])
                        act.activation(x_hi[:, kt, :], oT[:, kt, :], ACT.Copy).then_inc(n_hi, 1)
                if pt is not None:
                    act.wait_ge(t_pv, OUT_COUNT[pt])
                    act.wait_ge(t_comb, OUT_COUNT[pt])
                    st = stats[:, pt % 4, :]
                    if is_a(pt):
                        n = pv_blocks(pt)[0][0]
                        inv = st[0:n, 12:13]
                        act.activation(o_raw[0:n, :], B7[0:n, 0:P], ACT.Copy, scale=inv)
                        act.activation(square[0:n, :], B7[0:n, 0:P], ACT.Square, scale=inv,
                                       accum_out=st[0:n, 17:18]).then_inc(t_o, 1)
                    else:
                        for o, (n, c, _tok, _b) in enumerate(pv_blocks(pt)):
                            for e in range(2):
                                a = c + 64 * e
                                ins = act.activation(o_norm[0:n, a:a + 64], B7[0:n, a:a + 64], ACT.Copy,
                                                     scale=st[0:n, 12 + 2 * o + e:13 + 2 * o + e])
                        ins.then_inc(t_on_b, 1)
                if item:
                    ki, x = item
                    act.wait_ge(b6_done, USE6[("x", ki, x)])
                    if x == "v":
                        if ki >= 2:
                            act.wait_ge(st_v, 32 * (ki - 1))
                        act.activation(v_nat[ki % 2][:, 0:512], B6[:, :], ACT.Copy).then_inc(b6_free, 1)
                    elif x == "s":
                        if ki:
                            act.wait_ge(st_k, 32 * ki)
                        act.activation(v_nat[ki % 2][0:TS, 4 * P:5 * P], B6[0:TS, 0:P], ACT.Copy)
                        act.activation(k_nat[0:TS, 4 * P:5 * P], B6[0:TS, P:2 * P], ACT.Copy).then_inc(b6_free, 1)
                    elif x == "p":
                        n = 4 * P if ki < A_HEADS else P
                        act.activation(past_kT[:, 0:n], B6[:, 0:n], ACT.Copy).then_inc(b6_free, 1)
                    else:
                        c0 = 0 if ki < A_HEADS else 3 * P
                        act.activation(k_nat[:, c0:512], B6[:, c0:512], ACT.Copy).then_inc(b6_free, 1)
            for hf in range(ZH, ZH + OH - 2):
                hi_early(hf + 2)

            def hi_ffn(f):
                n, i = f
                count = FFN_RAW[n % NR] + 16 * (n // NR + 1)
                hi(n, n % NR, count if i is None else i * (LOOP_CHUNKS // NR * 16) + count)

            act.wait_ge(g_done, ZH + OH)
            hi_ffn((0, None))
            hi_ffn((1, None))
            root(1, n2[2][:, :])
            for kt in range(KT):
                affine(1, kt, cv[kt % 2], ext[kt % 2], SC_F, SH_F)
            act.wait_ge(x_ok, 3 * KT)

            def u_copy(x, h, count):
                act.wait_ge(u_done, count)
                for a, n, g in PIECES[h]:
                    ins = act.activation(ext[x][:, a + 2 + 2 * g:a + 2 + 2 * g + n],
                                         bank(2 * x + h)[:, a - HALF[h][0]:a - HALF[h][0] + n], ACT.Copy)
                ins.then_inc(u_ev, 1)

            def hidden(J, par, jj, f, has_down, last):
                at = lambda n: (f[0] + n, f[1])
                act.wait_ge(u_done, J * 4 + 1)
                hi_ffn(at(2))
                hi_ffn(at(3))
                if not isinstance(J, int) or J:
                    act.wait_ge(c_gate, J)
                u_copy(0, 0, J * 4 + 1)
                u_copy(0, 1, J * 4 + 2)
                if has_down:
                    hi_ffn(at(4))
                    hi_ffn(at(5))
                if not isinstance(J, int) or J:
                    act.wait_ge(c_val, J)
                u_copy(1, 0, J * 4 + 3)
                u_copy(1, 1, J * 4 + 4)
                if not last:
                    nxt = 6 if has_down else 4
                    hi_ffn(at(nxt))
                    hi_ffn(at(nxt + 1))
                act.wait_ge(c_gate, J + 1)
                act.activation(cv[0][:, :], cv[0][:, :], ACT.Silu).then_inc(c_silu, 1)
                act.wait_ge(y_mul, J + 1)
                for a, n, g in ((0, TP, 0), (TP, TS, 1)):
                    ins = act.activation(y_hi[par][:, jj, a:a + n], cv[1][:, a + 2 * g:a + 2 * g + n], ACT.Copy)
                ins.then_inc(y_hi_ok, 1)

            for jj in range(GRP):
                hidden(jj, 0, jj, (4 * jj, None), False, False)
            with act.Fori(0, (NG - 1) // 2) as i:
                for gg in range(2):
                    for jj in range(GRP):
                        hidden(i * (2 * GRP) + (GRP * (gg + 1) + jj), (gg + 1) % 2, jj,
                               (4 * GRP + 24 * gg + 6 * jj, i), True, False)
            for n in range(2, 8):
                act.wait_ge(d_done, 8 * GRP * (NG - 1) + 4 * (n - 2) - 4 if n < 4 else
                            8 * GRP * (NG - 1) + 4 * (n - 3))
                hi_ffn((LAST_DOWN + n, None))
            act.wait_ge(uc_t, 1)
            act.activation(u_rows[0:2 * FT, :, :].rearrange("p r n -> p (r n)"), bank(3)[0:2 * FT, :], ACT.Copy
                           ).then_inc(uc_ev, 1)
            root(2, ext[0][:, 0:T])
            for kt in range(0, KT, 2):
                act.wait_ge(f_t, kt + 1)
                b = F_BANKS[kt % 3]
                act.activation(y_nat[:, 0:QT, P * kt:P * kt + P],
                               bank(b)[:, :].rearrange("p (t n) -> p t n", n=P), ACT.Copy)
                act.activation(y_nat[0:TS, QT, P * kt:P * kt + P], bank(b + 1)[0:TS, 0:P], ACT.Copy
                               ).then_inc(f_eva, 1)

        @block.vector
        def _(dve):
            own = [0]

            def step(ins):
                own[0] += 1
                ins.then_inc(dve_own, 1)
                dve.wait_ge(dve_own, own[0])

            dve.wait_ge(rows_t, len(ROW_COUNTS))
            for i, n in enumerate(ROW_COUNTS):
                dve.tensor_copy(cols[:, i, 0:n], psw[:, 2048 + P * i:2048 + P * i + n]).then_inc(rows_ev, 1)
            dve.wait_ge(ld_small, 80)
            for i in range(2):
                a, b = n0[2 + 2 * i], n0[3 + 2 * i]
                dve.tensor_tensor_reduce(a[:, 0:A_DK], a[:, 0:A_DK], b[:, 0:A_DK], 1.0, 0.0, ALU.mult, ALU.add,
                                         tiny[:, 6 + i:7 + i]).then_inc(lam_dot, 1)

            def add_square(kt, x, sq, acc):
                if kt == 0:
                    step(dve.tensor_tensor(acc, x[:, 0, :], x[:, 0, :], ALU.mult))
                    return
                step(dve.tensor_tensor(sq, x[:, kt, :], x[:, kt, :], ALU.mult))
                ins = dve.tensor_tensor(acc, acc, sq, ALU.add)
                if kt == KT - 1:
                    ins.then_inc(sq_ok, 1)
                else:
                    step(ins)

            for kt in range(KT):
                dve.wait_ge(xt_ev, kt + 1)
                add_square(kt, xT, n0[0][:, :], n0[1][:, :])
            dve.wait_ge(lam_exp, 1)
            step(dve.tensor_tensor(tiny[:, 3:4], tiny[:, 5:6], tiny[:, 4:5], ALU.subtract))
            step(dve.tensor_scalar(neg_lam, tiny[:, 3:4], -LAMBDA_INIT, None, ALU.add))

            def scales(row, g_row):
                for g in range(2):
                    ins = dve.scalar_tensor_tensor(out=mod[:, row:row + KT, g], in0=mod[:, row:row + KT, g], scalar=1.0,
                                                   in1=cols[:, GT, g_row:g_row + KT], op0=ALU.add, op1=ALU.mult)
                ins.then_inc(mod_ok, 1)

            dve.wait_ge(m_used, MOD_EARLY // 2)
            for g in range(2):
                ins = dve.tensor_tensor(mod[:, 0:MOD_EARLY, g], B7[:, g:2 * MOD_EARLY:2], cols[:, BT, 0:MOD_EARLY], ALU.add)
            step(ins)
            scales(SC_A, 0)

            def inverse(n, x):
                dve.wait_ge(sd_ok, n + 1)
                step(dve.reciprocal(x, x))

            def normalise(n, x, t, h, rstd):
                def mul(kt):
                    dve.tensor_tensor(t[kt % 2], x[:, kt, :], rstd, ALU.mult).then_inc(n_mul, 1)
                mul(0)
                for kt in range(KT):
                    if kt + 1 < KT:
                        mul(kt + 1)
                    dve.wait_ge(n_hi, KT * 2 * n + kt + 1)
                    dve.tensor_tensor(x_lo[:, kt, :], h[kt % 2], x_hi[:, kt, :].bitcast(F32), ALU.subtract
                                      ).then_inc(x_ok, 1)

            inverse(0, n0[2][:, :])
            normalise(0, xT, [n0[3][:, :], n0[4][:, :]], [n0[5][:, :], n0[6][:, :]], n0[2][:, :])
            dve.wait_ge(scratch_out, 16)
            dve.wait_ge(ld_sub, 16)
            dve.tensor_scalar(gsub[:, :], gsub[:, :], 1.0 - LAMBDA_INIT, None, ALU.mult).then_inc(small_ok, 1)
            dve.wait_ge(small_ok, 1)

            def lo(c, raw, nth):
                dve.wait_ge(s_hi, nth + 1)
                dve.tensor_tensor(w_lo[c % NW][:, :], w_raw[raw][:, :], w_hi[c % NW][:, :].bitcast(F32), ALU.subtract
                                  ).then_inc(s_lo, 1)

            def lo_early(c):
                lo(c, RAW_OF[("w", c)] % NR, c)

            def z_out(hf):
                dve.wait_ge(g_done, hf + 1)
                x, i = SLABS[hf // 2]
                buf = zq[i % 2] if x == "q" else zk[i % 2] if x == "k" else zv
                a, n = HALF[hf % 2]
                ins = dve.tensor_scalar(buf[:, a:a + n], G[hf % 2][:, 0:n], SCALE if x == "q" else 1.0, None, ALU.mult)
                j = hf - MOD_FIRST
                if 0 <= j < MOD_TILES - MOD_EARLY:
                    tile = MOD_EARLY + j
                    ins = dve.tensor_scalar(mod[:, tile, :], G[hf % 2][:, H0:H0 + 2], cols[:, BT, tile:tile + 1], None,
                                            ALU.add)
                ins.then_inc(g_free, 1)

            def softmax_max(t):
                qi, i = TURNS[t]
                dve.wait_ge(t_score, t + 1)
                dve.wait_ge(tab_ok, qi + 1)
                st, sb, segs = stats[:, t % 4, :], scores[t % 2], segments(t)
                head = lambda e: 8 * ((qi - A_HEADS) // 4) + (qi - A_HEADS) % 4 + 4 * e
                if not is_a(t):
                    for np_, c, w in ((P, 256, 257),) if i < 3 else ((P, P, 129), (TS, 258 + 160, 161)):
                        dve.tensor_copy(sb[0:np_, c:c + w + 1:w], sinks[0:np_, head(0):head(0) + 5:4])
                for np_, pc, sc, n, tc, e, _q, _k, c in segs:
                    first = LOWEST if is_a(t) else sinks[0:np_, head(e):head(e) + 1]
                    ins = dve.tensor_tensor_reduce(sb[0:np_, sc:sc + n], S[t % 2][0:np_, pc:pc + n],
                                                   tab[qi % 2][0:np_, tc:tc + n], 1.0, first, ALU.add, ALU.max,
                                                   st[0:np_, c:c + 1])
                step(ins)
                groups = ([(P, 0, 2)] if i < 4 else [(TS, i - 4, i - 3)]) if is_a(t) else \
                    [(P, 0, 2)] if i < 3 else [(P, 0, 2), (TS, 2, 4)]
                for np_, c0, c1 in groups:
                    ins = dve.tensor_scalar(st[0:np_, 4 + c0:4 + c1], st[0:np_, c0:c1], -1.0, None, ALU.mult)
                ins.then_inc(t_ttr, 1)

            def combine(t):
                qi, i = TURNS[t]
                dve.wait_ge(t_exp, t + 1)
                st = stats[:, t % 4, :]
                if not is_a(t):
                    ins = dve.reciprocal(st[:, 12:14], st[:, 8:10])
                    if i == 3:
                        ins = dve.reciprocal(st[0:TS, 14:16], st[0:TS, 10:12])
                    ins.then_inc(t_comb, 1)
                    return
                if i < 4:
                    n, np_, st0_, p0 = P * (i + 1), P, st, scores[t % 2][:, 0:P * (i + 1)]
                    p1, out = scores[t % 2][:, 512:512 + n], p0
                else:
                    n, np_, st0_, p0 = PAST + TS, TS, stats[:, (t - 1) % 4, :], scores[(t - 1) % 2][0:TS, 0:PAST + TS]
                    p1 = out = scores[t % 2][0:TS, 0:n]
                dve.reciprocal(st[0:np_, 12:13], st0_[0:np_, 8:9])
                step(dve.reciprocal(st[0:np_, 13:14], st[0:np_, 9:10]))
                step(dve.tensor_scalar(st[0:np_, 16:17], st0_[0:np_, 8:9], st[0:np_, 13:14], neg_lam[0:np_, :],
                                       ALU.mult, ALU.mult))
                dve.scalar_tensor_tensor(out=out, in0=p1, scalar=st[0:np_, 16:17], in1=p0, op0=ALU.mult, op1=ALU.add
                                         ).then_inc(t_comb, 1)

            lo_early(0)
            lo_early(1)
            for k, (hf, part, parts, t, item) in enumerate(SLOTS):
                pt = prev_out(k, 1)
                if (hf and part == 0) or k == TAIL:
                    z_out(hf - 1 if hf else ZH - 1)
                if t is not None:
                    softmax_max(t)
                if pt is not None and not is_a(pt):
                    dve.wait_ge(b6_done, USE6[("p", pt)])
                    if TURNS[pt][1] < 3:
                        dve.tensor_copy(probsT[:, :], B6[:, :]).then_inc(b6_free, 1)
                    else:
                        dve.tensor_copy(probsT[:, 0:2 * P], B6[:, 0:2 * P])
                        for e in range(2):
                            c = 256 + 64 * e
                            dve.tensor_copy(probsT[:, c:c + TS], B6[:, c:c + TS])
                            ins = dve.tensor_copy(probsT[0:TS, c + TS:c + 2 * TS], B6[0:TS, c + TS:c + 2 * TS])
                        ins.then_inc(b6_free, 1)
                if hf is not None and part == 0 and hf + 2 < FC0:
                    lo_early(hf + 2)
                if hf is None:
                    for kt in TAIL_SPLITS[k - TAIL]:
                        dve.wait_ge(n_hi, KT + kt + 1)
                        dve.tensor_tensor(x_lo[:, kt, :], oT[:, kt, :], x_hi[:, kt, :].bitcast(F32), ALU.subtract
                                          ).then_inc(x_ok, 1)
                if t is not None and has_out(t):
                    combine(t)
                if pt is not None and is_a(pt):
                    dve.wait_ge(t_rstd, OUT_A[pt])
                    n = pv_blocks(pt)[0][0]
                    dve.scalar_tensor_tensor(out=o_norm[0:n, 0:P], in0=o_raw[0:n, :], scalar=stats[0:n, pt % 4, 19:20],
                                             in1=gsub[0:n, :], op0=ALU.mult, op1=ALU.mult).then_inc(t_on_a, 1)
            scales(SC_F, KT)

            def gated(n, h, b, gate):
                for a, m, g in PIECES[h]:
                    ins = dve.scalar_tensor_tensor(out=x1[:, n, a:a + m], in0=b[:, a - HALF[h][0]:a - HALF[h][0] + m],
                                                   scalar=mod[:, gate + n, g:g + 1], in1=x1[:, n, a:a + m],
                                                   op0=ALU.mult, op1=ALU.add)
                return ins

            for hf in range(ZH, ZH + OH):
                if hf + 2 < FC0:
                    lo_early(hf + 2)
                n, h = (hf - ZH) // 2, hf % 2
                if h == 0 and n % 4 == 0:
                    dve.wait_ge(xr[n // 4], 16)
                dve.wait_ge(g_done, hf + 1)
                gated(n, h, G[h], GT_A).then_inc(g_free, 1)
                if h:
                    dve.wait_ge(g_free, hf + 1)
                    add_square(n, x1, n2[0][:, :], n2[1][:, :])

            def lo_ffn(f):
                n, i = f
                lo(n, n % NR, FC0 + n if i is None else i * LOOP_CHUNKS + (FC0 + n))

            lo_ffn((0, None))
            lo_ffn((1, None))
            inverse(1, n2[2][:, :])
            dve.wait_ge(mod_ok, 2)
            normalise(1, x1, [cv[0][:, 0:T], cv[1][:, 0:T]], [ext[0][:, 0:T], ext[1][:, 0:T]], n2[2][:, :])
            dve.wait_ge(x_ok, 3 * KT)
            for x in range(2):
                ins = dve.memset(ext[x][:, 0:2], 0.0)
            ins.then_inc(d_ev, 4)

            def conv(x, J, done):
                tile = J + FT * x
                dve.tensor_copy(ext[x][:, TP + 2:TP + 4], cols[:, STATE:STATE + 2, bass.ds(tile, 1)]
                                .rearrange("p a b -> p (a b)")).then_inc(ext_ok, 1)
                dve.wait_ge(ext_ok, J * 2 + (x + 1))
                dve.tensor_copy(u_last[:, bass.ds(tile, 1), :].rearrange("p o (a b) -> p (o a) b", b=2),
                                ext[x][:, TP:TP + 2 * (TS + 2)].rearrange("p (a b) -> p a b", b=TS + 2)[:, :, 0:2])
                w = lambda i: cols[:, CONV_W + i, bass.ds(tile, 1)]
                dve.tensor_scalar(cv[x][:, :], ext[x][:, 2:T + 4], w(2), cols[:, CONV_B, bass.ds(tile, 1)],
                                  ALU.mult, ALU.add).then_inc(cv_ok, 1)
                dve.wait_ge(cv_ok, J * 4 + (2 * x + 1))
                dve.scalar_tensor_tensor(out=cv[x][:, :], in0=ext[x][:, 1:T + 3], scalar=w(1), in1=cv[x][:, :],
                                         op0=ALU.mult, op1=ALU.add).then_inc(cv_ok, 1)
                dve.wait_ge(cv_ok, J * 4 + (2 * x + 2))
                dve.scalar_tensor_tensor(out=cv[x][:, :], in0=ext[x][:, 0:T + 2], scalar=w(0), in1=cv[x][:, :],
                                         op0=ALU.mult, op1=ALU.add).then_inc(done, 1)

            def down_out(q, jj, Jd):
                dve.wait_ge(d_done, Jd * 8 + (q + 1))
                gated(4 * jj + q // 2, q % 2, bank(4 + q % 4), GT_F).then_inc(d_ev, 1)

            def hidden(J, par, jj, f, has_down, last):
                at = lambda n: (f[0] + n, f[1])
                lo_ffn(at(2))
                lo_ffn(at(3))
                dve.wait_ge(u_ev, J * 4 + 2)
                conv(0, J, c_gate)
                if has_down:
                    lo_ffn(at(4))
                    lo_ffn(at(5))
                dve.wait_ge(u_ev, J * 4 + 4)
                conv(1, J, c_val)
                out = (lambda q: down_out(q, jj, J - GRP)) if has_down else (lambda q: None)
                dve.wait_ge(c_val, J + 1)
                dve.wait_ge(c_silu, J + 1)
                dve.tensor_tensor(cv[1][:, :], cv[0][:, :], cv[1][:, :], ALU.mult).then_inc(y_mul, 1)
                nxt = 6 if has_down else 4
                if not last:
                    lo_ffn(at(nxt))
                    lo_ffn(at(nxt + 1))
                out(0)
                dve.wait_ge(y_hi_ok, J + 1)
                for a, n, g in ((0, TP, 0), (TP, TS, 1)):
                    ins = dve.tensor_tensor(y_lo[par][:, jj, a:a + n], cv[1][:, a + 2 * g:a + 2 * g + n],
                                            y_hi[par][:, jj, a:a + n].bitcast(F32), ALU.subtract)
                ins.then_inc(y_ok, 1)
                for q in range(1, 8):
                    out(q)

            for jj in range(GRP):
                hidden(jj, 0, jj, (4 * jj, None), False, False)
            with dve.Fori(0, (NG - 1) // 2) as i:
                for gg in range(2):
                    for jj in range(GRP):
                        hidden(i * (2 * GRP) + (GRP * (gg + 1) + jj), (gg + 1) % 2, jj,
                               (4 * GRP + 24 * gg + 6 * jj, i), True, False)
            for n in range(8):
                if n >= 2:
                    lo_ffn((LAST_DOWN + n, None))
                for q in range(4 * (n % 2), 4 * (n % 2) + 4):
                    down_out(q, n // 2, GRP * (NG - 1) + n // 2)
                    if q % 2:
                        dve.wait_ge(d_ev, 4 + 8 * (GRP * (NG - 1) + n // 2) + q + 1)
                        add_square(4 * (n // 2) + q // 2, x1, cv[0][:, 0:T], cv[1][:, 0:T])
            inverse(2, ext[0][:, 0:T])
            for kt in range(KT):
                if kt >= 2:
                    dve.wait_ge(f_t, kt - 1)
                dve.scalar_tensor_tensor(out=cv[kt % 2][:, 0:T], in0=x1[:, kt, :], scalar=cols[:, GT, 2 * KT + kt:2 * KT + kt + 1],
                                         in1=ext[0][:, 0:T], op0=ALU.mult, op1=ALU.mult).then_inc(f_mul, 1)
                if kt >= 2 and kt % 2 == 0 or kt == KT - 1:
                    for o in ([kt - 1] if kt < KT - 1 else [kt]):
                        dve.wait_ge(f_t, o + 1)
                        b = F_BANKS[o % 3]
                        dve.tensor_copy(y_nat[:, 0:QT, P * o:P * o + P],
                                        bank(b)[:, :].rearrange("p (t n) -> p t n", n=P))
                        dve.tensor_copy(y_nat[0:TS, QT, P * o:P * o + P], bank(b + 1)[0:TS, 0:P]).then_inc(f_evd, 1)

        @block.tensor
        def _(pe):
            pe.wait_ge(consts, 2)
            pe.wait_ge(ld_rows, 16 * 12)
            for i, n in enumerate(ROW_COUNTS):
                pe.transpose(psw[:, 2048 + P * i:2048 + P * i + n], rows[0:n, i, :], ident[0:n, 0:n]).then_inc(rows_t, 1)
            pe.wait_ge(ld_x, 16 * (QT + 1))
            for kt in range(KT):
                if kt >= 2:
                    pe.wait_ge(xt_ev, kt - 1)
                b = bank(2 * (kt % 2), 2)
                for t in range(QT):
                    pe.transpose(b[:, P * t:P * t + P], x_nat[t][:, P * kt:P * kt + P], ident[:, :])
                pe.transpose(b[:, TP:T], x_nat[QT][0:TS, P * kt:P * kt + P], ident[0:TS, 0:TS]).then_inc(xt_t, 1)

            def sum_squares(n, acc):
                pe.wait_ge(sq_ok, n + 1)
                pe.matmul(bank(4), ones[:, :], acc[:, 0:TP], start=True, stop=True)
                pe.matmul(bank(5)[:, 0:TS], ones[:, :], acc[:, TP:T], start=True, stop=True).then_inc(ss_ok, 1)

            pe.wait_ge(cs_ok, 1)
            for c in range(MOD_EARLY // 2):
                if c == 10:
                    pe.wait_ge(rows_ev, 9)
                    sum_squares(0, n0[1])
                pe.wait_ge(ld_m[c % MR], 16 * (c // MR + 1))
                for j in range(2):
                    col = 2 * (2 * c + j)
                    for kt in range(KT):
                        mm = pe.matmul(B7[:, col:col + 2], wm[c % MR][:, kt, P * j:P * j + P], cs[:, kt, :],
                                       start=(kt == 0), stop=(kt == KT - 1))
                mm.then_inc(m_used, 1)

            def products(out, n, hi_w, lo_w, hi_x, lo_x, first, last):
                pe.matmul(out[:, 0:n], hi_w, hi_x, start=first, stop=False)
                pe.matmul(out[:, 0:n], hi_w, lo_x, start=False, stop=False)
                return pe.matmul(out[:, 0:n], lo_w, hi_x, start=False, stop=last)

            def late_mod(j, hf):
                for part in range(2):
                    x = ("mod", j, part)
                    raw = RAW_OF[x] % NR
                    pe.wait_ge(ld_raw[raw], LOADED[x])
                    for k in range(BLK):
                        mm = pe.matmul(G[hf % 2][:, H0:H0 + 2], w_raw[raw][:, P * k:P * k + P], cs[:, BLK * part + k, :],
                                       start=(part == 0 and k == 0), stop=(part == 1 and k == BLK - 1))
                mm.then_inc(m_late, 1)

            def tiles(hf, kts):
                s, h = hf // 2, hf % 2
                a, n = HALF[h]
                for kt in kts:
                    c = 2 * s + kt // BLK
                    if kt == 0:
                        if hf >= 2:
                            pe.wait_ge(g_free, hf - 1)
                        if MOD_FIRST <= hf < MOD_FIRST + MOD_TILES - MOD_EARLY:
                            late_mod(hf - MOD_FIRST, hf)
                    if kt % BLK == 0 and h == 0:
                        pe.wait_ge(s_lo, c + 1)
                    if hf in (0, ZH):
                        pe.wait_ge(x_ok, (KT if hf else 0) + kt + 1)
                    w = slice(P * (kt % BLK), P * (kt % BLK) + P)
                    mm = products(G[h], n, w_hi[c % NW][:, w], w_lo[c % NW][:, w], x_hi[:, kt, a:a + n],
                                  x_lo[:, kt, a:a + n], kt == 0, kt == KT - 1)
                    if kt == KT - 1:
                        mm.then_inc(g_done, 1)

            def z_ready(ki_or_qi, what):
                pe.wait_ge(g_free, 2 * SLAB_OF[(what, ki_or_qi)] + 2)

            def score(t):
                qi, i = TURNS[t]
                ki = kv_of(qi)
                z_ready(qi, "q")
                z_ready(ki, "k")
                if t >= 2:
                    pe.wait_ge(t_ttr, t - 1)
                for np_, pc, _sc, _n, _tc, e, q0, keys, _c in segments(t):
                    r = slice(64 * e, 64 * e + 64)
                    for src, k0, n in keys:
                        if src == "past":
                            pe.wait_ge(b6_free, USE6[("x", ki, "p")])
                        kk = (past_kT if src == "past" else zk[ki % 2])[r, k0:k0 + n]
                        mm = pe.matmul(S[t % 2][0:np_, pc:pc + n], zq[qi % 2][r, q0:q0 + np_], kk, start=True, stop=True)
                        pc += n
                mm.then_inc(t_score, 1)

            def bank6(use):
                if use > 1:
                    pe.wait_ge(b6_free, use - 1)

            def turn_probs(t):
                if is_a(t):
                    pe.wait_ge(t_comb, OUT_COUNT[t])
                else:
                    pe.wait_ge(t_exp, t + 1)
                bank6(USE6[("p", t)])
                for np_, _c, _tok, blocks in pv_blocks(t):
                    for sc, n, _src, _tile, _vc, _vn, _oc, tc in blocks:
                        mm = pe.transpose(B6[0:n, tc:tc + np_], scores[t % 2][0:np_, sc:sc + n], ident[0:np_, 0:np_])
                mm.then_inc(b6_done, 1)

            def values(t):
                ki = kv_of(TURNS[t][0])
                pe.wait_ge(b6_free, max(USE6[("p", t)], USE6[("x", ki, "s" if TURNS[t][1] >= 3 else "v")]))
                prev = OUT_COUNT[t] - 1
                if prev:
                    pe.wait_ge(t_otev, prev)
                for np_, _c, tok, blocks in pv_blocks(t):
                    if tok == TP:
                        pe.wait_ge(ld_pv, 16 * (ki + 1))
                    for j, (_sc, n, src, tile, vc, vn, oc, tc) in enumerate(blocks):
                        v = (past_v if src == "past" else v_nat[ki % 2])[0:n, P * tile + vc:P * tile + vc + vn]
                        first = j == 0 or blocks[j - 1][6] != oc
                        last = j == len(blocks) - 1 or blocks[j + 1][6] != oc
                        mm = pe.matmul(B7[0:np_, oc:oc + vn], probsT[0:n, tc:tc + np_], v, start=first, stop=last)
                mm.then_inc(t_pv, 1)

            def turn_output(t):
                if is_a(t):
                    pe.wait_ge(t_on_a, OUT_A[t])
                else:
                    pe.wait_ge(t_on_b, OUT_B[t])
                for np_, c, _tok, _b in pv_blocks(t):
                    mm = pe.transpose(B7[:, 256 + c:256 + c + np_], o_norm[0:np_, c:c + P], ident[0:np_, 0:np_])
                mm.then_inc(t_ot, 1)

            def kv_item(ki, x):
                z_ready(ki, "v" if x in "vs" else "k")
                bank6(USE6[("x", ki, x)])
                if x == "v":
                    for t in range(QT):
                        mm = pe.transpose(B6[:, P * t:P * t + P], zv[:, P * t:P * t + P], ident[:, :])
                elif x == "s":
                    pe.transpose(B6[0:TS, 0:P], zv[:, TP:T], ident[:, :])
                    mm = pe.transpose(B6[0:TS, P:2 * P], zk[ki % 2][:, TP:T], ident[:, :])
                elif x == "p":
                    pe.wait_ge(ld_pk, 16 * (ki + 1))
                    for t in range(4 if ki < A_HEADS else 1):
                        mm = pe.transpose(B6[:, P * t:P * t + P], past_k[:, P * t:P * t + P], ident[:, :])
                else:
                    for t in range(0 if ki < A_HEADS else 3, QT):
                        mm = pe.transpose(B6[:, P * t:P * t + P], zk[ki % 2][:, P * t:P * t + P], ident[:, :])
                mm.then_inc(b6_done, 1)

            for k, (hf, part, parts, t, item) in enumerate(SLOTS):
                pt, pp = prev_out(k, 1), prev_out(k, 2)
                if pt is not None:
                    turn_probs(pt)
                if pp is not None:
                    turn_output(pp)
                if t is not None:
                    score(t)
                n = KT // parts
                if hf is not None:
                    tiles(hf, range(n * part, n * part + n // 2))
                if pt is not None:
                    values(pt)
                if item:
                    kv_item(*item)
                if hf is not None:
                    tiles(hf, range(n * part + n // 2, n * part + n))
            for hf in range(ZH, ZH + OH):
                tiles(hf, range(KT))
            sum_squares(1, n2[1])
            pe.wait_ge(g_free, ZH + OH)

            def lo_ready(f):
                n, i = f
                pe.wait_ge(s_lo, FC0 + n + 1 if i is None else i * LOOP_CHUNKS + (FC0 + n + 1))

            def up(J, f, x):
                for h, (a, n) in enumerate(HALF):
                    if not isinstance(J, int) or J:
                        pe.wait_ge(u_ev, J * 4 + (2 * x + h - 3))
                    for kt in range(KT):
                        c = f[0] + 2 * x + kt // BLK
                        if kt % BLK == 0 and h == 0:
                            lo_ready((c, f[1]))
                        if isinstance(J, int) and J == 0 and x == 0 and h == 0:
                            pe.wait_ge(x_ok, 2 * KT + kt + 1)
                        w = slice(P * (kt % BLK), P * (kt % BLK) + P)
                        mm = products(bank(2 * x + h), n, w_hi[c % NW][:, w], w_lo[c % NW][:, w], x_hi[:, kt, a:a + n],
                                      x_lo[:, kt, a:a + n], kt == 0, kt == KT - 1)
                    mm.then_inc(u_done, 1)

            def down(Jd, f, par):
                for q in range(8):
                    c, nn, h = f[0] + q // 4, q % 4 // 2, q % 2
                    if q % 4 == 0:
                        lo_ready((c, f[1]))
                    pe.wait_ge(d_ev, Jd * 8 + (q + 1))
                    a, n = HALF[h]
                    for kt in range(GRP):
                        w = slice(256 * kt + P * nn, 256 * kt + P * nn + P)
                        mm = products(bank(4 + q % 4), n, w_hi[c % NW][:, w], w_lo[c % NW][:, w], y_hi[par][:, kt, a:a + n],
                                      y_lo[par][:, kt, a:a + n], kt == 0, kt == GRP - 1)
                    mm.then_inc(d_done, 1)

            for jj in range(GRP):
                up(jj, (4 * jj, None), 0)
                up(jj, (4 * jj, None), 1)
            with pe.Fori(0, (NG - 1) // 2) as i:
                for gg in range(2):
                    for jj in range(GRP):
                        J = i * (2 * GRP) + (GRP * (gg + 1) + jj)
                        f = (4 * GRP + 24 * gg + 6 * jj, i)
                        up(J, f, 0)
                        up(J, f, 1)
                        if jj == 0:
                            pe.wait_ge(y_ok, J)
                        down(J - GRP, (f[0] + 4, i), gg % 2)
            pe.wait_ge(y_ok, FT)
            for jj in range(GRP):
                down(GRP * (NG - 1) + jj, (LAST_DOWN + 2 * jj, None), (NG - 1) % 2)
            pe.wait_ge(c_val, FT)
            pe.wait_ge(u_ev, 4 * FT)
            for r in range(4):
                mm = pe.transpose(bank(3)[0:2 * FT, P * r:P * r + P], u_last[:, :, r], ident[:, :])
            mm.then_inc(uc_t, 1)
            sum_squares(2, cv[1])
            for kt in range(KT):
                pe.wait_ge(f_mul, kt + 1)
                if kt == 2:
                    pe.wait_ge(sd_ok, 3)
                if kt >= 3:
                    o = kt - 3
                    pe.wait_ge(f_evd if o % 2 else f_eva, o // 2 + 1)
                b = bank(F_BANKS[kt % 3], 2)
                for t in range(QT):
                    pe.transpose(b[:, P * t:P * t + P], cv[kt % 2][:, P * t:P * t + P], ident[:, :])
                pe.transpose(b[0:TS, 512:512 + P], cv[kt % 2][:, TP:T], ident[:, :]).then_inc(f_t, 1)


_INS = ["x_prompt", "x_sample", "cache_a_k", "cache_a_v", "cache_b_k", "cache_b_v", "state_conv", "c_prompt",
        "c_sample", "w_mod", "b_mod", "g_attn", "w_in", "lambda_q1", "lambda_k1", "lambda_q2", "lambda_k2",
        "subln_g", "sinks", "w_out", "g_ffn", "w_up", "conv_w", "conv_b", "w_down", "g_final"]
_OUTS = [("y_p", (1, TP, D)), ("y_s", (1, TS, D)), ("ak_p", (1, 1, TP, A_HEADS, 2 * A_DK)),
         ("av_p", (1, 1, TP, A_HEADS, A_DV)), ("bk_p", (1, 1, P, 4, B_DH)), ("bv_p", (1, 1, P, 4, B_DH)),
         ("conv_p", (1, 1, 2, 2 * DFF)), ("ak_s", (1, 1, TS, A_HEADS, 2 * A_DK)),
         ("av_s", (1, 1, TS, A_HEADS, A_DV)), ("bk_s", (1, 1, P, 4, B_DH)), ("bv_s", (1, 1, P, 4, B_DH)),
         ("conv_s", (1, 1, 2, 2 * DFF))]


def kernel(**inputs):
    import numpy as np
    import concourse.bacc as bacc
    from concourse.bass_utils import run_bass_kernel_spmd

    nc = bacc.Bacc("TRN2", target_bir_lowering=False, num_devices=1)
    arrays, A, O = {}, {}, {}
    for name in _INS:
        a = np.ascontiguousarray(inputs[name])
        arrays[f"in_{name}"] = a
        A[name] = nc.dram_tensor(f"in_{name}", a.shape, mybir.dt.from_np(a.dtype), kind="ExternalInput").ap()
    for name, shape in _OUTS:
        O[name] = nc.dram_tensor(f"out_{name}", shape, F32, kind="ExternalOutput").ap()
    build(nc, A, O)
    r = run_bass_kernel_spmd(nc, [arrays], core_ids=[0])
    return tuple(r.results[0][f"out_{name}"] for name, _ in _OUTS)
```

```python
from contextlib import ExitStack

import concourse.bass as bass
from concourse import mybir

F32 = mybir.dt.float32
F32R = mybir.dt.float32r
ALU = mybir.AluOpType
ACT = mybir.ActivationFunctionType
AX = mybir.AxisListType

P = 128
D = 2048
KT = D // P
TP, TS = 512, 32
T = TP + TS
QT = TP // P
H0 = T // 2
HALF = [(0, H0), (H0, T - H0)]
PIECES = [[(0, H0, 0)], [(H0, TP - H0, 0), (TP, TS, 1)]]
BLK = 8
CW = BLK * P
NR = 4
NW = 4
PAST = 512
CHUNK = 64
A_HEADS, A_DK, A_DV = 8, 64, 128
B_HEADS, B_DH, B_GROUP = 16, 64, 4
SCALE = A_DK ** -0.5
A_QW = A_HEADS * 2 * A_DK
DFF = 5632
FT = DFF // P
GRP = 4
NG = FT // GRP
EPS = 1e-6
LAMBDA_INIT = 0.2
NEG_LARGE = -2.0 ** 110
LOWEST = -3.0e38
ZSLABS = 36
ZH = 2 * ZSLABS
OH = 2 * KT
MOD_EARLY = 32
MOD_TILES = 96
SH_A, SC_A, GT_A, SH_F, SC_F, GT_F = range(0, MOD_TILES, KT)
LG = 256
LGT = LG // P
LK = CW // LG
LPG = KT // LK
EG = 512
EGT = EG // P
E_GROUPS = MOD_EARLY // EGT
EK = CW // EG
EPG = KT // EK
EC = E_GROUPS * EPG
TAB = 640


def slope_a(h):
    return 2.0 ** (-8.0 * (h + 1) / A_HEADS)


def slope_b(h):
    return 2.0 ** (-8.0 * (h + 1) / B_HEADS)


SLABS = [(x, h) for h in range(A_HEADS) for x in "qkv"]
for _m in range(2):
    SLABS += [("k", A_HEADS + _m), ("v", A_HEADS + _m)]
    SLABS += [("q", A_HEADS + 4 * _m + i) for i in range(4)]
SLAB_OF = {x: s for s, x in enumerate(SLABS)}


def kv_of(qi):
    return qi if qi < A_HEADS else A_HEADS + (qi - A_HEADS) // 4


TURNS = [(h, i) for h in range(A_HEADS) for i in range(6)]
TURNS += [(A_HEADS + u, i) for u in range(8) for i in range(4)]


def is_a(t):
    return TURNS[t][0] < A_HEADS


def has_out(t):
    return not (is_a(t) and TURNS[t][1] == 4)


def make_slots():
    turns = {6 * (h + 1) + i: [6 * h + i] for h in range(A_HEADS) for i in range(6)}
    items = {6 * (h + 1) + i: [(h, x)] for h in range(A_HEADS) for i, x in enumerate("vspk")}
    b = 6 * A_HEADS
    for u, first in ((0, 54), (1, 56), (2, 58), (4, 66), (5, 68), (6, 70)):
        for n in range(2):
            turns[first + n] = [b + 4 * u + 2 * n, b + 4 * u + 2 * n + 1]
    for n in range(4):
        turns[60 + n] = [b + 12 + n]
    items[52], items[53], items[54] = [(8, "v")], [(8, "s")], [(8, "p"), (8, "k")]
    items[64], items[65] = [(9, "v"), (9, "s")], [(9, "p"), (9, "k")]
    slots = []
    for hf in range(ZH):
        tt, ii = turns.get(hf, []), items.get(hf, [])
        n = max(1, len(tt), len(ii))
        for p in range(n):
            slots.append((hf, p, n, tt[p] if p < len(tt) else None, ii[p] if p < len(ii) else None))
    for t in range(b + 28, b + 32):
        slots.append((None, 0, 1, t, None))
    slots += [(None, 0, 1, None, None)] * 2
    return slots


SLOTS = make_slots()
TAIL = len(SLOTS) - 6
TAIL_SPLITS = [range(0, 4), range(4, 8), range(8, 11), range(11, 14), range(14, 15), range(15, 16)]


def segments(t):
    qi, i = TURNS[t]
    if qi < A_HEADS:
        if i < 4:
            n = P * (i + 1)
            return [(P, 512 * m, 512 * m, n, 512 - P * i, m, P * i, [("new", 0, n)], m) for m in range(2)]
        return [(TS, 0, 0, PAST + TS, 0, i - 4, TP, [("past", 0, PAST), ("new", TP, TS)], i - 4)]
    if i < 3:
        q0 = P * (i + 1)
        return [(P, 512 * e, 257 * e, 256, 256 * e, e, q0, [("new", q0 - P, 256)], e) for e in range(2)]
    out = [(P, 512 * e, 129 * e, P, 256 * e + P, e, 0, [("new", 0, P)], e) for e in range(2)]
    out += [(TS, 512 * e + P, 258 + 161 * e, P + TS, 256 * e, e, TP, [("past", 0, P), ("new", TP, TS)], 2 + e)
            for e in range(2)]
    return out


def pv_blocks(t):
    qi, i = TURNS[t]
    if qi < A_HEADS:
        if i < 4:
            return [(P, 0, P * i, [(P * j, P, "new", j, 0, P, 0, P * j) for j in range(i + 1)])]
        blocks = [(P * j, P, "past", j, 0, P, 0, TS * j) for j in range(4)]
        return [(TS, 0, TP, blocks + [(PAST, TS, "new", 4, 0, P, 0, P)])]
    if i < 3:
        return [(P, 0, P * (i + 1), [(257 * e + P * j, P, "new", i + j, 64 * e, 64, 64 * e, P * (2 * e + j))
                                     for e in range(2) for j in range(2)])]
    first = (P, 0, 0, [(129 * e, P, "new", 0, 64 * e, 64, 64 * e, P * e) for e in range(2)])
    blocks = []
    for e in range(2):
        blocks.append((258 + 161 * e, P, "past", 0, 64 * e, 64, P + 64 * e, 256 + 64 * e))
        blocks.append((258 + 161 * e + P, TS, "new", 4, 64 * e, 64, P + 64 * e, 256 + 64 * e + TS))
    return [first, (TS, P, TP, blocks)]


BANK6 = []
for _k, (_hf, _p, _n, _t, _x) in enumerate(SLOTS):
    if _k and SLOTS[_k - 1][3] is not None and has_out(SLOTS[_k - 1][3]):
        BANK6.append(("p", SLOTS[_k - 1][3]))
    if _x:
        BANK6.append(("x",) + _x)
USE6 = {x: n + 1 for n, x in enumerate(BANK6)}
OUTS = [t for t in range(len(TURNS)) if has_out(t)]
OUT_COUNT = {t: n + 1 for n, t in enumerate(OUTS)}
OUT_A = {t: n + 1 for n, t in enumerate([t for t in OUTS if is_a(t)])}
OUT_B = {t: n + 1 for n, t in enumerate([t for t in OUTS if not is_a(t)])}


def prev_out(k, back):
    t = SLOTS[k - back][3] if k >= back else None
    return t if t is not None and has_out(t) else None


X_AT = 8
SUM_AT = X_AT + KT + 2
LAG = NW
NORM_AT = {34 + 2 * k if k < 8 else 57 + 2 * (k - 8): k for k in range(12)}


LATE1 = 24 * LPG
LATE2 = (MOD_TILES - MOD_EARLY) // LGT * LPG - LATE1
LATE_AT = [3 + n * 60 // LATE1 for n in range(LATE1)] + [ZH + 1 + n * 28 // LATE2 for n in range(LATE2)]
SUM_OF = {LATE_AT[LPG * g + LPG - 1] + 2 + t: (g, t) for g in range((LATE1 + LATE2) // LPG) for t in range(LGT)}
assert len(SUM_OF) == (LATE1 + LATE2) // LPG * LGT and max(SUM_OF) < ZH + OH


def late_of(hf, part, parts):
    if hf is None:
        return [], []
    c = [n for n, h in enumerate(LATE_AT) if h == hf]
    if parts == 1:
        return c[:1], c[1:]
    return (c[:1] if part == 0 else c[1:] if part == 1 else []), []


def early_tile(g):
    return (SC_A if g % 2 else SH_A) + EGT * (g // 2)


STREAM = [("e", _e) for _e in range(EC)] + [("w", 0), ("w", 1)]
for _hf in range(ZH + OH):
    _late = [("mod", _n) for _n, _h in enumerate(LATE_AT) if _h == _hf]
    STREAM += _late[:1]
    if _hf + 2 < ZH + OH:
        STREAM.append(("w", _hf + 2))
    STREAM += _late[1:]
RAW_OF = {x: r for r, x in enumerate(STREAM)}


def chunk_dmas(c):
    if c < ZH:
        x, qi = SLABS[c // 2]
        return 2 if x == "q" and qi >= A_HEADS else 1
    return 4 if c % 2 else 1


LOADED = {}
_count = [0] * NR
for _r, _x in enumerate(STREAM):
    _count[_r % NR] += 16 * (chunk_dmas(_x[1]) if _x[0] == "w" else 1)
    LOADED[_x] = _count[_r % NR]
FFN_RAW = list(_count)
FC0 = ZH + OH
SC0 = EC + FC0
assert len(STREAM) % NR == FC0 % NR == EC % NR == 0
LOOP_CHUNKS = 2 * GRP * 6
LAST_DOWN = 4 * GRP + LOOP_CHUNKS * (NG - 1) // 2
ROW_COUNTS = [2 * KT, MOD_TILES, 3 * KT] + [2 * FT] * 6
F_BANKS = (0, 6, 4)


def build(nc, A, O):
    w_in, w_out, w_mod = A["w_in"][0], A["w_out"][0], A["w_mod"][0]
    w_up, w_down = A["w_up"][0], A["w_down"][0]
    scratch = nc.dram_tensor("x_transposed", (KT, P, T), F32, kind="Internal").ap()

    ctx = ExitStack()
    with ctx:
        def on(stack, name, shape, dt=F32):
            return stack.enter_context(nc.sbuf_tensor(name, shape, dt))

        def sem(name):
            return ctx.enter_context(nc.semaphore(name))

        w_raw = [on(ctx, f"w_raw{i}", [P, CW]) for i in range(NR)]
        w_hi = [on(ctx, f"w_hi{i}", [P, CW], F32R) for i in range(NW)]
        w_lo = [on(ctx, f"w_lo{i}", [P, CW], F32R) for i in range(NW)]
        cols = on(ctx, "cols", [P, 9, P])
        mod = on(ctx, "mod", [P, MOD_TILES, 2])
        cs = on(ctx, "cs", [P, KT, 2])
        ident = on(ctx, "ident", [P, P])
        ones = on(ctx, "ones", [P, P])
        tiny = on(ctx, "tiny", [P, 16])
        sinks = on(ctx, "sinks", [P, B_HEADS])
        stats = on(ctx, "stats", [P, 4, 20])
        eps, minus_half, neg_lam = tiny[:, 0:1], tiny[:, 1:2], tiny[:, 2:3]
        CT, BT, GT, CONV_W, CONV_B, STATE = 0, 1, 2, 3, 6, 7
        early = ExitStack()
        x_nat = [on(early, f"x_nat{i}", [P, D]) for i in range(QT + 1)]
        early.close()
        y_nat = on(early, "y_nat", [P, QT + 1, D])
        early.close()
        x_hi = on(ctx, "x_hi", [P, KT, T], F32R)
        x_lo = on(ctx, "x_lo", [P, KT, T], F32R)
        st0 = ExitStack()
        xT = on(st0, "xT", [P, KT, T])
        n0_sq = [on(st0, f"n0_sq{i}", [P, T]) for i in range(2)]
        n0_acc, n0_rstd = on(st0, "n0_acc", [P, T]), on(st0, "n0_rstd", [P, T])
        lam = [on(st0, f"lambda{i}", [P, A_DK]) for i in range(4)]
        c_parts = on(st0, "c_parts", [P, KT, 4], F32R)
        mod_rows = [on(st0, f"mod_rows{i}", [P, EG]) for i in range(2)]
        pair = on(st0, "pair", [P, 2])
        rows = on(st0, "rows", [P, 9, P])
        st0.close()
        st1 = ExitStack()
        zq = [on(st1, f"zq{i}", [P, T]) for i in range(2)]
        zk = [on(st1, f"zk{i}", [P, T]) for i in range(2)]
        zv = on(st1, "zv", [P, T])
        v_nat = [on(st1, f"v_nat{i}", [P, 5 * P]) for i in range(2)]
        k_nat = on(st1, "k_nat", [P, 5 * P])
        past_k = on(st1, "past_k", [P, 4 * P])
        past_v = on(st1, "past_v", [P, 4 * P])
        past_kT = on(st1, "past_kT", [P, 4 * P])
        scores = [on(st1, f"scores{i}", [P, 1024]) for i in range(2)]
        probsT = on(st1, "probsT", [P, 512])
        o_raw = on(st1, "o_raw", [P, P])
        o_norm = on(st1, "o_norm", [P, 2 * P])
        square = on(st1, "square", [P, P])
        oT = on(st1, "oT", [P, KT, T])
        late = oT[:, KT - 4:KT, :].rearrange("p k n -> p (k n)")
        acc_d, acc_p = ([late[:, LG * (2 * x + i):LG * (2 * x + i) + LG] for i in range(2)] for x in range(2))
        late_prod = late[:, 4 * LG:4 * LG + CW]
        tab_a = on(st1, "tab_a", [P, TAB])
        tab_b = on(st1, "tab_b", [P, 256])
        tab = [on(st1, f"tab{i}", [P, TAB]) for i in range(2)]
        gsub = on(st1, "gsub", [P, P])
        st1.close()
        st2 = ExitStack()
        x1 = on(st2, "x1", [P, KT, T])
        st3 = st2
        ext = [on(st3, f"ext{i}", [P, TP + 2 * (TS + 2)]) for i in range(2)]
        cv = [on(st3, f"cv{i}", [P, T + 2]) for i in range(2)]
        n2_st = ExitStack()
        n2 = [on(n2_st, f"n2_{x}", [P, T]) for x in ("sq", "acc", "rstd")]
        n2_st.close()
        y_hi = [on(st3, f"y_hi{i}", [P, GRP, T], F32R) for i in range(2)]
        y_lo = [on(st3, f"y_lo{i}", [P, GRP, T], F32R) for i in range(2)]
        u_last = on(st3, "u_last", [P, 2 * FT, 4])
        u_rows = on(st3, "u_rows", [P, 4, P])
        st3.close()

        ps = ctx.enter_context(nc.psum_tensor("ps", [P, 8, 512], F32))
        psw = ps[:, :, :].rearrange("p b n -> p (b n)")

        def bank(b, n=1):
            return psw[:, 512 * b:512 * (b + n)]

        G = [bank(0), bank(1)]
        S = [bank(2, 2), bank(4, 2)]

        def out_bank(hf):
            return bank(hf % (2 if hf < ZH else 4))

        B6, B7 = bank(6), bank(7)

        ld_x, ld_rows, ld_small, scratch_out = sem("ld_x"), sem("ld_rows"), sem("ld_small"), sem("scratch_out")
        ld_c, c_hi, c_lo = sem("ld_c"), sem("c_hi"), sem("c_lo")
        e_ev, e_t, e_tev = sem("e_ev"), sem("e_t"), sem("e_tev")
        sq_mul, sq_add = sem("sq_mul"), sem("sq_add")
        ld_raw = [sem(f"ld_raw{i}") for i in range(NR)]
        consts, rows_t, rows_ev, cs_ok = sem("consts"), sem("rows_t"), sem("rows_ev"), sem("cs_ok")
        xt_t, xt_ev = sem("xt_t"), sem("xt_ev")
        sq_ok, ss_ok, sd_ok, rs_ok = sem("sq_ok"), sem("ss_ok"), sem("sd_ok"), sem("rs_ok")
        m_used, m_late, mod_ok = sem("m_used"), sem("m_late"), sem("mod_ok")
        late_d, late_act, late_p, n_aff2 = sem("late_d"), sem("late_act"), sem("late_p"), sem("n_aff2")
        n_mul, n_aff, n_hi, x_ok = sem("n_mul"), sem("n_aff"), sem("n_hi"), sem("x_ok")
        act_own, dve_own, pool_own = sem("act_own"), sem("dve_own"), sem("pool_own")
        s_hi, s_lo = sem("s_hi"), sem("s_lo")
        g_done, g_free = sem("g_done"), sem("g_free")
        lam_dot, lam_exp, small_ok = sem("lam_dot"), sem("lam_exp"), sem("small_ok")
        tab_ok = sem("tab_ok")
        t_score, t_ttr, t_exp, t_comb = sem("t_score"), sem("t_ttr"), sem("t_exp"), sem("t_comb")
        b6_done, b6_free = sem("b6_done"), sem("b6_free")
        t_pv, t_o, t_rstd, t_on_a, t_on_b = sem("t_pv"), sem("t_o"), sem("t_rstd"), sem("t_on_a"), sem("t_on_b")
        t_ot, t_otev = sem("t_ot"), sem("t_otev")
        st_k, st_v, ld_pk, ld_pv = sem("st_k"), sem("st_v"), sem("ld_pk"), sem("ld_pv")
        xr = [sem(f"xr{i}") for i in range(4)]
        u_done, u_ev, c_gate, c_val, c_silu, y_mul, y_hi_ok, y_ok = (
            sem(x) for x in ("u_done", "u_ev", "c_gate", "c_val", "c_silu", "y_mul", "y_hi_ok", "y_ok"))
        d_done, d_ev = sem("d_done"), sem("d_ev")
        f_mul, f_t, f_eva, f_evd, store = sem("f_mul"), sem("f_t"), sem("f_eva"), sem("f_evd"), sem("store")
        uc_t, uc_ev = sem("uc_t"), sem("uc_ev")
        ld_sub, st_win, st_conv = sem("ld_sub"), sem("st_win"), sem("st_conv")
        ext_ok, cv_ok = sem("ext_ok"), sem("cv_ok")

        block = ctx.enter_context(nc.Block())

        def w_in_cols(s):
            x, i = SLABS[s]
            if i < A_HEADS:
                return [("qkv".index(x) * A_QW + P * i, P)]
            m, base = (i - A_HEADS) // 4 if x == "q" else i - A_HEADS, 3 * A_QW
            if x == "q":
                head = 2 * B_GROUP * m + (i - A_HEADS) % 4
                return [(base + B_DH * head, B_DH), (base + B_DH * (head + B_GROUP), B_DH)]
            return [(base + B_HEADS * B_DH + (256 if x == "v" else 0) + P * m, P)]

        @block.sync
        def _(sp):
            def slot_free(old):
                if old[0] != "mod":
                    sp.wait_ge(s_lo, old[1] + 1 + (EC if old[0] == "w" else 0))
                else:
                    sp.wait_ge(late_d, LK * (old[1] + 1))
                    sp.wait_ge(late_act, old[1] + 1)

            for r, x in enumerate(STREAM):
                slot = r % NR
                if r == SUM_AT + 2:
                    sp.wait_ge(xt_ev, KT)
                    sp.dma_start(scratch.rearrange("k p t -> p k t"), xT[:, :, :]).then_inc(scratch_out, 16)
                if r >= NR:
                    slot_free(STREAM[r - NR])
                dst = w_raw[slot][:, :].rearrange("p (k n) -> p k n", n=P)
                if x[0] == "e":
                    c0, r0 = P * early_tile(x[1] // EPG), EK * P * (x[1] % EPG)
                    sp.dma_start(w_raw[slot][:, :].rearrange("p (k n) -> p k n", n=EG),
                                 w_mod[r0:r0 + EK * P, c0:c0 + EG].rearrange("(k p) n -> p k n", p=P)
                                 ).then_inc(ld_raw[slot], 16)
                elif x[0] == "mod":
                    c0, r0 = P * MOD_EARLY + LG * (x[1] // LPG), LK * P * (x[1] % LPG)
                    sp.dma_start(w_raw[slot][:, :].rearrange("p (k n) -> p k n", n=LG),
                                 w_mod[r0:r0 + LK * P, c0:c0 + LG].rearrange("(k p) n -> p k n", p=P)
                                 ).then_inc(ld_raw[slot], 16)
                elif x[1] < ZH:
                    s, half = x[1] // 2, x[1] % 2
                    at = 0
                    for c0, n in w_in_cols(s):
                        src = w_in[1024 * half:1024 * half + 1024, c0:c0 + n]
                        sp.dma_start(dst[:, :, at:at + n], src.rearrange("(k p) n -> p k n", p=P)
                                     ).then_inc(ld_raw[slot], 16)
                        at += n
                else:
                    n, half = (x[1] - ZH) // 2, x[1] % 2
                    if half == 0:
                        sp.dma_start(dst, w_out[0:1024, P * n:P * n + P].rearrange("(k p) n -> p k n", p=P)
                                     ).then_inc(ld_raw[slot], 16)
                    else:
                        for u in range(2):
                            for m in range(2):
                                r0 = 1024 + 512 * m + 256 * u
                                src = w_out[r0:r0 + 256, P * n:P * n + P]
                                sp.dma_start(dst[64 * u:64 * u + 64, 4 * m:4 * m + 4, :],
                                             src.rearrange("(i p) n -> p i n", p=64)
                                             ).then_inc(ld_raw[slot], 16)

            def up(c, nth, j, k, base):
                slot = c % NR
                if isinstance(nth, int) and nth - SC0 < NR:
                    slot_free(STREAM[nth - SC0 - NR])
                else:
                    sp.wait_ge(s_lo, nth - NR + 1)
                sp.dma_start(w_raw[slot][:, :].rearrange("p (k n) -> p k n", n=P),
                             w_up[1024 * k:1024 * k + 1024, bass.ds(base + P * j, P)]
                             .rearrange("(k p) n -> p k n", p=P)).then_inc(ld_raw[slot], 16)

            def down(c, nth, g, n0_):
                slot = c % NR
                sp.wait_ge(s_lo, nth - NR + 1)
                sp.dma_start(w_raw[slot][:, :].rearrange("p (k n) -> p k n", n=256),
                             w_down[bass.ds(g * (GRP * P), GRP * P), P * n0_:P * n0_ + 256]
                             .rearrange("(k p) n -> p k n", p=P)).then_inc(ld_raw[slot], 16)

            for j in range(GRP):
                for n in range(4):
                    up(4 * j + n, SC0 + 4 * j + n, j, n % 2, DFF * (n // 2))
            with sp.Fori(0, NG - 1) as i:
                for jj in range(GRP):
                    for n in range(4):
                        up(6 * jj + n, i * 24 + (SC0 + 16 + 6 * jj + n), (i + 1) * GRP + jj, n % 2, DFF * (n // 2))
                    for n in range(2):
                        down(6 * jj + 4 + n, i * 24 + (SC0 + 16 + 6 * jj + 4 + n), i, 4 * jj + 2 * n)
            for n in range(8):
                down(n, SC0 + 16 + 24 * (NG - 1) + n, NG - 1, 2 * n)
            for q in range(4):
                sp.wait_ge(f_eva, 2 * (q + 1))
                sp.wait_ge(f_evd, 2 * (q + 1))
                sp.dma_start(O["y_p"][0, :, 512 * q:512 * q + 512].rearrange("(t p) n -> p t n", p=P),
                             y_nat[:, 0:QT, 512 * q:512 * q + 512]).then_inc(store, 16)
                sp.dma_start(O["y_s"][0, :, 512 * q:512 * q + 512],
                             y_nat[0:TS, QT, 512 * q:512 * q + 512]).then_inc(store, 16)
            sp.wait_ge(store, 16 * 8)

        @block.gpsimd
        def _(pool):
            own = [0]

            def step(ins):
                own[0] += 1
                ins.then_inc(pool_own, 1)
                pool.wait_ge(pool_own, own[0])

            pool.memset(ones[:, :], 1.0).then_inc(consts, 1)
            step(pool.memset(ident[:, :], 0.0))
            pool.affine_select(out=ident[:, :], in_=ident[:, :], compare_op=ALU.not_equal, fill=1.0, base=0,
                               pattern=[[-1, P]], channel_multiplier=1).then_inc(consts, 1)
            pool.memset(eps, EPS).then_inc(consts, 1)
            pool.memset(minus_half, -0.5).then_inc(consts, 1)
            pool.wait_ge(consts, 4)
            pool.tensor_tensor(pair[0:4, :], ident[0:4, 0:2], ident[0:4, 2:4], ALU.add).then_inc(consts, 1)
            for kt in range(KT):
                pool.wait_ge(xt_ev, kt + 1)
                if kt >= 2:
                    pool.wait_ge(sq_add, max(1, kt - 2))
                pool.tensor_tensor(n0_sq[kt % 2][:, :], xT[:, kt, :], xT[:, kt, :], ALU.mult).then_inc(sq_mul, 1)
            pool.wait_ge(scratch_out, 16)
            pool.wait_ge(rs_ok, 1)
            def scale_shift(kt):
                pool.wait_ge(mod_ok, kt // EGT + 1)
                pool.wait_ge(n_mul, kt + 1)
                for a, c, g in ((0, TP, 0), (TP, TS, 1)):
                    ins = pool.tensor_scalar(xT[:, kt, a:a + c], xT[:, kt, a:a + c], mod[:, SC_A + kt, g:g + 1],
                                             mod[:, SH_A + kt, g:g + 1], ALU.mult, ALU.add)
                ins.then_inc(n_aff, 1)

            for kt in range(KT):
                pool.tensor_tensor(xT[:, kt, :], xT[:, kt, :], n0_rstd[:, :], ALU.mult).then_inc(n_mul, 1)
                if kt < 2 * EGT:
                    scale_shift(kt)
            for kt in range(2 * EGT, 3 * EGT):
                scale_shift(kt)

            def natural(ki, item):
                sem_, buf = (st_v, v_nat[ki % 2]) if item == "v" else (st_k, k_nat)
                pool.wait_ge(b6_free, USE6[("x", ki, item)])
                if item == "p":
                    return
                if item == "s":
                    lo = 0 if ki < A_HEADS else P - TS
                    for x, b, sm in (("v", v_nat[ki % 2], st_v), ("k", k_nat, st_k)):
                        if ki < A_HEADS:
                            dst = O[f"a{x}_s"][0, 0, :, ki, :]
                        else:
                            m = ki - A_HEADS
                            dst = O[f"b{x}_s"][0, 0, lo:, 2 * m:2 * m + 2, :].rearrange("t h d -> t (h d)")
                        pool.dma_start(dst, b[0:TS, 4 * P:5 * P]).then_inc(sm, 16)
                elif ki < A_HEADS:
                    dst = O[f"a{item}_p"][0, 0, :, ki, :].rearrange("(t p) d -> p t d", p=P)
                    pool.dma_start(dst, buf[:, 0:512].rearrange("p (t d) -> p t d", d=P)).then_inc(sem_, 16)
                else:
                    m = ki - A_HEADS
                    dst = O[f"b{item}_p"][0, 0, :, 2 * m:2 * m + 2, :].rearrange("t h d -> t (h d)")
                    pool.dma_start(dst, buf[:, 384:512]).then_inc(sem_, 16)

            def load_past(which, ki):
                buf, sm = (past_k, ld_pk) if which == "k" else (past_v, ld_pv)
                if ki < A_HEADS:
                    src = A[f"cache_a_{which}"][0, 0, :, ki, :].rearrange("(t p) d -> p t d", p=P)
                    pool.dma_start(buf[:, :].rearrange("p (t d) -> p t d", d=P), src).then_inc(sm, 16)
                else:
                    m = ki - A_HEADS
                    src = A[f"cache_b_{which}"][0, 0, :, 2 * m:2 * m + 2, :].rearrange("t h d -> t (h d)")
                    pool.dma_start(buf[:, 0:P], src).then_inc(sm, 16)

            for x in "kv":
                pool.dma_start(O[f"b{x}_s"][0, 0, 0:P - TS], A[f"cache_b_{x}"][0, 0, TS:P]).then_inc(st_win, 16)

            pool.wait_ge(x_ok, KT)
            pool.wait_ge(scratch_out, 16)
            load_past("k", 0)
            load_past("v", 0)
            pool.dma_start(gsub[:, :], A["subln_g"].partition_broadcast(P).rearrange("p a n -> p (a n)")
                           ).then_inc(ld_sub, 16)
            step(pool.iota(tab_a[:, :], pattern=[[1, TAB]], base=-512, channel_multiplier=-1,
                           allow_small_or_imprecise_dtypes=True))
            step(pool.tensor_scalar(tab[0][:, :], tab_a[:, :], -1.0, None, ALU.mult))
            step(pool.tensor_scalar(tab[1][:, :], tab_a[:, :], 0.0, -2.0, ALU.max, ALU.mult))
            step(pool.tensor_tensor(tab_a[:, :], tab_a[:, :], tab[1][:, :], ALU.add))
            step(pool.memset(tab_a[0:CHUNK, 512 + CHUNK:TAB], NEG_LARGE))
            step(pool.tensor_copy(tab_b[:, :], tab_a[:, 384:TAB]))
            step(pool.memset(tab_b[CHUNK:P, 0:CHUNK], NEG_LARGE))

            def table(qi):
                if qi >= 2:
                    last = max(t for t in range(len(TURNS)) if TURNS[t][0] == qi - 2)
                    pool.wait_ge(t_ttr, last + 1)
                if qi < A_HEADS:
                    pool.tensor_scalar(tab[qi % 2][:, :], tab_a[:, :], slope_a(qi), None, ALU.mult
                                       ).then_inc(tab_ok, 1)
                else:
                    m, i = (qi - A_HEADS) // 4, (qi - A_HEADS) % 4
                    for e in range(2):
                        ins = pool.tensor_scalar(tab[qi % 2][:, 256 * e:256 * e + 256], tab_b[:, :],
                                                 slope_b(8 * m + 4 * e + i), None, ALU.mult)
                    ins.then_inc(tab_ok, 1)

            def rstd(t):
                pool.wait_ge(t_o, OUT_A[t])
                n = pv_blocks(t)[0][0]
                s = stats[0:n, t % 4, :]
                step(pool.tensor_scalar(s[:, 18:19], s[:, 17:18], 1.0 / A_DV, EPS, ALU.mult, ALU.add))
                pool.tensor_tensor(s[:, 19:20], s[:, 18:19], minus_half[0:n, :], ALU.pow).then_inc(t_rstd, 1)

            def late_add(n):
                g, p = n // LPG, n % LPG
                if p == 0 and g >= 2:
                    pool.wait_ge(m_late, LGT * (g - 1))
                if n == LATE1:
                    pool.wait_ge(x_ok, 2 * KT)
                pool.wait_ge(late_act, n + 1)
                acc, prod = acc_p[g % 2], lambda k: late_prod[:, LG * k:LG * k + LG]
                if n:
                    pool.wait_ge(late_p, n)
                for k in range(1 if p == 0 else 0, LK):
                    ins = pool.tensor_tensor(acc, prod(0) if p == 0 and k == 1 else acc, prod(k), ALU.add)
                    if k < LK - 1:
                        step(ins)
                ins.then_inc(late_p, 1)

            table(0)
            next_table, next_pk, next_pv = 1, 1, 1
            for k, (hf, part, parts, t, item) in enumerate(SLOTS):
                pt = prev_out(k, 1)
                begin, end = late_of(hf, part, parts)
                for n in begin:
                    late_add(n)
                if pt is not None and is_a(pt):
                    rstd(pt)
                if t is not None and TURNS[t][1] == 0 and next_table < 16:
                    table(next_table)
                    next_table += 1
                if item:
                    natural(*item)
                    if item[1] == "p" and next_pk < 10:
                        load_past("k", next_pk)
                        next_pk += 1
                if pt is not None and TURNS[pt][1] == (5 if is_a(pt) else 3):
                    last_of_kv = pt + 1 == len(TURNS) or kv_of(TURNS[pt + 1][0]) != kv_of(TURNS[pt][0])
                    if last_of_kv and next_pv < 10:
                        pool.wait_ge(t_pv, OUT_COUNT[pt])
                        load_past("v", next_pv)
                        next_pv += 1
                for n in end:
                    late_add(n)
            pool.wait_ge(t_otev, len(OUTS))
            pool.wait_ge(st_k, 16 * 20)
            pool.wait_ge(st_v, 16 * 20)
            for q in range(4):
                pool.dma_start(x1[:, 4 * q:4 * q + 4, :], scratch[4 * q:4 * q + 4].rearrange("k p t -> p k t")
                               ).then_inc(xr[q], 16)
            for n in range(LATE1, LATE1 + LATE2):
                late_add(n)
            pool.wait_ge(uc_ev, 1)
            for r in range(4):
                dst = O["conv_p" if r < 2 else "conv_s"][0, 0, r % 2, :].rearrange("(j p) -> j p", p=P)
                pool.dma_start(dst, u_rows[0:2 * FT, r, :]).then_inc(st_conv, 16)
            pool.wait_ge(st_conv, 64)
            pool.wait_ge(st_win, 32)

        @block.scalar
        def _(act):
            own = [0]

            def step(ins):
                own[0] += 1
                ins.then_inc(act_own, 1)
                act.wait_ge(act_own, own[0])

            tiled = lambda a: a.rearrange("(k p) -> k p", p=P)
            act.dma_start(rows[0:KT, 0, :], tiled(A["c_prompt"][0])).then_inc(ld_c, 16)
            act.dma_start(rows[KT:2 * KT, 0, :], tiled(A["c_sample"][0])).then_inc(ld_c, 16)
            act.dma_start(rows[0:MOD_TILES, BT, :], tiled(A["b_mod"][0])).then_inc(ld_rows, 16)
            act.dma_start(rows[0:KT, GT, :], tiled(A["g_attn"][0])).then_inc(ld_rows, 16)
            act.dma_start(rows[KT:2 * KT, GT, :], tiled(A["g_ffn"][0])).then_inc(ld_rows, 16)
            act.dma_start(rows[2 * KT:3 * KT, GT, :], tiled(A["g_final"])).then_inc(ld_rows, 16)
            for i in range(3):
                act.dma_start(rows[0:2 * FT, CONV_W + i, :], tiled(A["conv_w"][0, i])).then_inc(ld_rows, 16)
            act.dma_start(rows[0:2 * FT, CONV_B, :], tiled(A["conv_b"][0])).then_inc(ld_rows, 16)
            for i in range(2):
                act.dma_start(rows[0:2 * FT, STATE + i, :], tiled(A["state_conv"][0, 0, i])).then_inc(ld_rows, 16)
            bc = lambda a: a.partition_broadcast(P).rearrange("p a n -> p (a n)")
            act.dma_start(sinks[:, :], bc(A["sinks"])).then_inc(ld_small, 16)
            for i, x in enumerate(("q1", "k1", "q2", "k2")):
                act.dma_start(lam[i][:, :], bc(A[f"lambda_{x}"])).then_inc(ld_small, 16)
            for t in range(QT):
                act.dma_start(x_nat[t][:, :], A["x_prompt"][0, P * t:P * t + P, :]).then_inc(ld_x, 16)
            act.dma_start(x_nat[QT][0:TS, :], A["x_sample"][0]).then_inc(ld_x, 16)
            act.wait_ge(rows_ev, 1)
            act.activation(cs[:, :, :].rearrange("p k g -> p g k"),
                           cols[:, CT, 0:2 * KT].rearrange("p (g k) -> p g k", g=2), ACT.Silu).then_inc(cs_ok, 1)
            act.wait_ge(cs_ok, 1)
            act.activation(c_parts[:, :, 0:2], cs[:, :, :], ACT.Copy).then_inc(c_hi, 1)
            act.wait_ge(consts, 5)

            def root(n, dst):
                act.wait_ge(ss_ok, n + 1)
                act.activation(dst, bank(4 if n else 0, 2)[:, 0:T], ACT.Sqrt, bias=eps, scale=1.0 / D).then_inc(sd_ok, 1)

            def affine(n, kt, src, h, scale_row, shift_row):
                act.wait_ge(n_mul, KT * n + kt + 1)
                if kt >= 2:
                    act.wait_ge(x_ok, KT * 2 * n + kt - 1)
                for a, c, g in ((0, TP, 0), (TP, TS, 1)):
                    ins = act.activation(h[:, a:a + c], src[:, a:a + c], ACT.Identity,
                                         bias=mod[:, shift_row + kt, g:g + 1],
                                         scale=mod[:, scale_row + kt, g:g + 1])
                step(ins)
                act.activation(x_hi[:, kt, :], h[:, 0:T], ACT.Copy).then_inc(n_hi, 1)

            def hi(c, raw, count):
                act.wait_ge(ld_raw[raw], count)
                act.activation(w_hi[c % NW][:, :], w_raw[raw][:, :], ACT.Copy).then_inc(s_hi, 1)

            def hi_early(c):
                if c >= NW:
                    act.wait_ge(g_done, 2 * ((c - NW) // 2) + 2)
                else:
                    act.wait_ge(m_used, EC - NW + c + 1)
                hi(c, RAW_OF[("w", c)] % NR, LOADED[("w", c)])

            def group_out(g):
                act.wait_ge(m_used, EPG * (g + 1))
                if g >= 2:
                    act.wait_ge(e_t, g - 1)
                act.activation(mod_rows[g % 2][0:4, :], bank(7 - g % 2)[0:4, :], ACT.Copy).then_inc(e_ev, 1)

            def scale_shift(kt):
                act.wait_ge(n_mul, kt + 1)
                act.wait_ge(mod_ok, kt // EGT + 1)
                for a, c, g in ((0, TP, 0), (TP, TS, 1)):
                    ins = act.activation(xT[:, kt, a:a + c], xT[:, kt, a:a + c], ACT.Identity,
                                         bias=mod[:, SH_A + kt, g:g + 1], scale=mod[:, SC_A + kt, g:g + 1])
                ins.then_inc(n_aff2, 1)

            def h_hi(kt):
                if kt < len(NORM_AT):
                    act.wait_ge(n_aff, kt + 1)
                else:
                    act.wait_ge(n_aff2, kt - len(NORM_AT) + 1)
                act.activation(x_hi[:, kt, :], xT[:, kt, :], ACT.Copy).then_inc(n_hi, 1)

            for e in range(EC):
                if e >= NW:
                    act.wait_ge(m_used, e - NW + 1)
                hi(e, e % NR, LOADED[("e", e)])
                if e % EPG == LAG - 1 and e >= EPG:
                    group_out(e // EPG - 1)
                kt = e - X_AT - LAG + 1
                if 0 <= kt < KT:
                    act.wait_ge(xt_t, kt + 1)
                    act.activation(xT[:, kt, :], bank(2 * (kt % 2), 2)[:, 0:T], ACT.Copy).then_inc(xt_ev, 1)
                if e == X_AT:
                    act.wait_ge(lam_dot, 2)
                    act.activation(tiny[:, 4:6], tiny[:, 6:8], ACT.Exp).then_inc(lam_exp, 1)
                if e == SUM_AT + LAG:
                    root(0, n0_rstd[:, :])
                if e in NORM_AT:
                    h_hi(NORM_AT[e])
            def late_mul(n):
                x = ("mod", n)
                act.wait_ge(ld_raw[RAW_OF[x] % NR], LOADED[x])
                if n:
                    act.wait_ge(late_p, n)
                if n == LATE1:
                    act.wait_ge(x_ok, 2 * KT)
                for k in range(LK):
                    kt = LK * (n % LPG) + k
                    ins = act.activation(late_prod[:, LG * k:LG * k + LG], w_raw[RAW_OF[x] % NR][:, LG * k:LG * k + LG],
                                         ACT.Copy, scale=cs[:, kt, 1:2])
                ins.then_inc(late_act, 1)

            hi_early(0)
            hi_early(1)
            group_out(E_GROUPS - 1)
            for kt in range(len(NORM_AT), KT):
                scale_shift(kt)
                if kt > len(NORM_AT):
                    h_hi(kt - 1)
            h_hi(KT - 1)
            for k, (hf, part, parts, t, item) in enumerate(SLOTS):
                pt, pp = prev_out(k, 1), prev_out(k, 2)
                if pt is not None and is_a(pt):
                    act.wait_ge(b6_done, USE6[("p", pt)])
                    if pv_blocks(pt)[0][0] == P:
                        n = P * len(pv_blocks(pt)[0][3])
                        act.activation(probsT[:, 0:n], B6[:, 0:n], ACT.Copy).then_inc(b6_free, 1)
                    else:
                        act.activation(probsT[:, 0:P], B6[:, 0:P], ACT.Copy)
                        act.activation(probsT[0:TS, P:P + TS], B6[0:TS, P:P + TS], ACT.Copy).then_inc(b6_free, 1)
                if pp is not None:
                    act.wait_ge(t_ot, OUT_COUNT[pp])
                    if TURNS[pp][0] >= KT - 4:
                        act.wait_ge(m_late, LATE1 // LPG * LGT)
                    for n, c, tok, _b in pv_blocks(pp):
                        ins = act.activation(oT[:, TURNS[pp][0], tok:tok + n],
                                             B7[:, 256 + c:256 + c + n], ACT.Copy)
                    ins.then_inc(t_otev, 1)
                if t is not None:
                    act.wait_ge(t_ttr, t + 1)
                    st = stats[:, t % 4, :]
                    for np_, _pc, sc, n, _tc, _e, _q, _k, i in segments(t):
                        n += 0 if is_a(t) else 1
                        sb = scores[t % 2][0:np_, sc:sc + n]
                        ins = act.activation(sb, sb, ACT.Exp, bias=st[0:np_, 4 + i:5 + i],
                                             accum_out=st[0:np_, 8 + i:9 + i])
                    ins.then_inc(t_exp, 1)
                if hf is not None and part == 0 and hf + 2 < FC0:
                    hi_early(hf + 2)
                begin, end = late_of(hf, part, parts)
                for n in begin:
                    late_mul(n)
                if hf is None:
                    for kt in TAIL_SPLITS[k - TAIL]:
                        act.wait_ge(g_done, ZH)
                        act.wait_ge(t_otev, len(OUTS) if kt == KT - 1 else OUT_COUNT[4 * (kt - 8) + 51] if kt >= 8
                                    else OUT_COUNT[6 * kt + 5])
                        act.activation(x_hi[:, kt, :], oT[:, kt, :], ACT.Copy).then_inc(n_hi, 1)
                if pt is not None:
                    act.wait_ge(t_pv, OUT_COUNT[pt])
                    act.wait_ge(t_comb, OUT_COUNT[pt])
                    st = stats[:, pt % 4, :]
                    if is_a(pt):
                        n = pv_blocks(pt)[0][0]
                        inv = st[0:n, 12:13]
                        act.activation(o_raw[0:n, :], B7[0:n, 0:P], ACT.Copy, scale=inv)
                        act.activation(square[0:n, :], B7[0:n, 0:P], ACT.Square, scale=inv,
                                       accum_out=st[0:n, 17:18]).then_inc(t_o, 1)
                    else:
                        for o, (n, c, _tok, _b) in enumerate(pv_blocks(pt)):
                            for e in range(2):
                                a = c + 64 * e
                                ins = act.activation(o_norm[0:n, a:a + 64], B7[0:n, a:a + 64], ACT.Copy,
                                                     scale=st[0:n, 12 + 2 * o + e:13 + 2 * o + e])
                        ins.then_inc(t_on_b, 1)
                if item:
                    ki, x = item
                    act.wait_ge(b6_done, USE6[("x", ki, x)])
                    if x == "v":
                        if ki >= 2:
                            act.wait_ge(st_v, 32 * (ki - 1))
                        act.activation(v_nat[ki % 2][:, 0:512], B6[:, :], ACT.Copy).then_inc(b6_free, 1)
                    elif x == "s":
                        if ki:
                            act.wait_ge(st_k, 32 * ki)
                        act.activation(v_nat[ki % 2][0:TS, 4 * P:5 * P], B6[0:TS, 0:P], ACT.Copy)
                        act.activation(k_nat[0:TS, 4 * P:5 * P], B6[0:TS, P:2 * P], ACT.Copy).then_inc(b6_free, 1)
                    elif x == "p":
                        n = 4 * P if ki < A_HEADS else P
                        act.activation(past_kT[:, 0:n], B6[:, 0:n], ACT.Copy).then_inc(b6_free, 1)
                    else:
                        c0 = 0 if ki < A_HEADS else 3 * P
                        act.activation(k_nat[:, c0:512], B6[:, c0:512], ACT.Copy).then_inc(b6_free, 1)
                for n in end:
                    late_mul(n)
            for hf in range(ZH, ZH + OH):
                if hf + 2 < FC0:
                    hi_early(hf + 2)
                for x in late_of(hf, 0, 1):
                    for n in x:
                        late_mul(n)

            def hi_ffn(f):
                n, i = f
                count = FFN_RAW[n % NR] + 16 * (n // NR + 1)
                hi(n, n % NR, count if i is None else i * (LOOP_CHUNKS // NR * 16) + count)

            act.wait_ge(g_done, ZH + OH)
            hi_ffn((0, None))
            hi_ffn((1, None))
            root(1, n2[2][:, :])
            for kt in range(KT):
                affine(1, kt, cv[kt % 2], ext[kt % 2], SC_F, SH_F)
            act.wait_ge(x_ok, 3 * KT)

            def u_copy(x, h, count):
                act.wait_ge(u_done, count)
                for a, n, g in PIECES[h]:
                    ins = act.activation(ext[x][:, a + 2 + 2 * g:a + 2 + 2 * g + n],
                                         bank(2 * x + h)[:, a - HALF[h][0]:a - HALF[h][0] + n], ACT.Copy)
                ins.then_inc(u_ev, 1)

            def hidden(J, par, jj, f, has_down, last):
                at = lambda n: (f[0] + n, f[1])
                act.wait_ge(u_done, J * 4 + 1)
                hi_ffn(at(2))
                hi_ffn(at(3))
                if not isinstance(J, int) or J:
                    act.wait_ge(c_gate, J)
                u_copy(0, 0, J * 4 + 1)
                u_copy(0, 1, J * 4 + 2)
                if has_down:
                    hi_ffn(at(4))
                    hi_ffn(at(5))
                if not isinstance(J, int) or J:
                    act.wait_ge(c_val, J)
                u_copy(1, 0, J * 4 + 3)
                u_copy(1, 1, J * 4 + 4)
                if not last:
                    nxt = 6 if has_down else 4
                    hi_ffn(at(nxt))
                    hi_ffn(at(nxt + 1))
                act.wait_ge(c_gate, J + 1)
                act.activation(cv[0][:, :], cv[0][:, :], ACT.Silu).then_inc(c_silu, 1)
                act.wait_ge(y_mul, J + 1)
                for a, n, g in ((0, TP, 0), (TP, TS, 1)):
                    ins = act.activation(y_hi[par][:, jj, a:a + n], cv[1][:, a + 2 * g:a + 2 * g + n], ACT.Copy)
                ins.then_inc(y_hi_ok, 1)

            for jj in range(GRP):
                hidden(jj, 0, jj, (4 * jj, None), False, False)
            with act.Fori(0, (NG - 1) // 2) as i:
                for gg in range(2):
                    for jj in range(GRP):
                        hidden(i * (2 * GRP) + (GRP * (gg + 1) + jj), (gg + 1) % 2, jj,
                               (4 * GRP + 24 * gg + 6 * jj, i), True, False)
            for n in range(2, 8):
                act.wait_ge(d_done, 8 * GRP * (NG - 1) + 4 * (n - 2) - 4 if n < 4 else
                            8 * GRP * (NG - 1) + 4 * (n - 3))
                hi_ffn((LAST_DOWN + n, None))
            act.wait_ge(uc_t, 1)
            act.activation(u_rows[0:2 * FT, :, :].rearrange("p r n -> p (r n)"), bank(3)[0:2 * FT, :], ACT.Copy
                           ).then_inc(uc_ev, 1)
            root(2, ext[0][:, 0:T])
            for kt in range(0, KT, 2):
                act.wait_ge(f_t, kt + 1)
                b = F_BANKS[kt % 3]
                act.activation(y_nat[:, 0:QT, P * kt:P * kt + P],
                               bank(b)[:, :].rearrange("p (t n) -> p t n", n=P), ACT.Copy)
                act.activation(y_nat[0:TS, QT, P * kt:P * kt + P], bank(b + 1)[0:TS, 0:P], ACT.Copy
                               ).then_inc(f_eva, 1)

        @block.vector
        def _(dve):
            own = [0]

            def step(ins):
                own[0] += 1
                ins.then_inc(dve_own, 1)
                dve.wait_ge(dve_own, own[0])

            def row_out(i):
                n = ROW_COUNTS[i]
                dve.wait_ge(rows_t, i + 1)
                dve.tensor_copy(cols[:, i, 0:n], psw[:, 2048 + P * i:2048 + P * i + n]).then_inc(rows_ev, 1)

            row_out(0)
            dve.wait_ge(c_hi, 1)
            dve.tensor_tensor(c_parts[:, :, 2:4], cs[:, :, :], c_parts[:, :, 0:2].bitcast(F32), ALU.subtract
                              ).then_inc(c_lo, 1)

            def add_square(kt, x, sq, acc):
                if kt == 0:
                    step(dve.tensor_tensor(acc, x[:, 0, :], x[:, 0, :], ALU.mult))
                    return
                step(dve.tensor_tensor(sq, x[:, kt, :], x[:, kt, :], ALU.mult))
                ins = dve.tensor_tensor(acc, acc, sq, ALU.add)
                if kt == KT - 1:
                    ins.then_inc(sq_ok, 1)
                else:
                    step(ins)

            def scales(row, g_row, count):
                for g in range(2):
                    ins = dve.scalar_tensor_tensor(out=mod[:, row:row + count, g], in0=mod[:, row:row + count, g],
                                                   scalar=1.0, in1=cols[:, GT, g_row:g_row + count],
                                                   op0=ALU.add, op1=ALU.mult)
                ins.then_inc(mod_ok, 1)

            def inverse(n, x):
                dve.wait_ge(sd_ok, n + 1)
                step(dve.reciprocal(x, x))

            def normalise(n, x, t, h, rstd):
                def mul(kt):
                    dve.tensor_tensor(t[kt % 2], x[:, kt, :], rstd, ALU.mult).then_inc(n_mul, 1)
                mul(0)
                for kt in range(KT):
                    if kt + 1 < KT:
                        mul(kt + 1)
                    dve.wait_ge(n_hi, KT * 2 * n + kt + 1)
                    dve.tensor_tensor(x_lo[:, kt, :], h[kt % 2], x_hi[:, kt, :].bitcast(F32), ALU.subtract
                                      ).then_inc(x_ok, 1)

            def lo(c, raw, nth):
                dve.wait_ge(s_hi, nth + 1)
                dve.tensor_tensor(w_lo[c % NW][:, :], w_raw[raw][:, :], w_hi[c % NW][:, :].bitcast(F32), ALU.subtract
                                  ).then_inc(s_lo, 1)

            def group_mod(g):
                t0 = early_tile(g)
                dve.wait_ge(e_t, g + 1)
                for st in range(2):
                    ins = dve.tensor_tensor(mod[:, t0:t0 + EGT, st], bank(5)[:, 2 * t0 + st:2 * (t0 + EGT):2],
                                            cols[:, BT, t0:t0 + EGT], ALU.add)
                ins.then_inc(e_tev, 1)
                if g % 2:
                    dve.wait_ge(e_tev, g + 1)
                    scales(t0, t0 - SC_A, EGT)

            def h_lo(kt):
                dve.wait_ge(n_hi, kt + 1)
                dve.tensor_tensor(x_lo[:, kt, :], xT[:, kt, :], x_hi[:, kt, :].bitcast(F32), ALU.subtract
                                  ).then_inc(x_ok, 1)

            for e in range(EC):
                lo(e, e % NR, e)
                if e == 4:
                    dve.wait_ge(rows_t, len(ROW_COUNTS))
                    for i in range(1, len(ROW_COUNTS)):
                        row_out(i)
                if e == 5:
                    dve.wait_ge(ld_small, 80)
                    for i in range(2):
                        a, b = lam[2 * i], lam[2 * i + 1]
                        dve.tensor_tensor_reduce(a[:, :], a[:, :], b[:, :], 1.0, 0.0, ALU.mult, ALU.add,
                                                 tiny[:, 6 + i:7 + i]).then_inc(lam_dot, 1)
                if e == X_AT + 2:
                    dve.wait_ge(lam_exp, 1)
                    step(dve.tensor_tensor(tiny[:, 3:4], tiny[:, 5:6], tiny[:, 4:5], ALU.subtract))
                    step(dve.tensor_scalar(neg_lam, tiny[:, 3:4], -LAMBDA_INIT, None, ALU.add))
                kt = e - X_AT - LAG
                if 1 <= kt < KT:
                    dve.wait_ge(sq_mul, kt + 1)
                    if kt > 1:
                        dve.wait_ge(sq_add, kt - 1)
                    ins = dve.tensor_tensor(n0_acc[:, :], n0_sq[0][:, :] if kt == 1 else n0_acc[:, :],
                                            n0_sq[kt % 2][:, :], ALU.add)
                    ins.then_inc(sq_ok if kt == KT - 1 else sq_add, 1)
                if e == SUM_AT + LAG:
                    dve.wait_ge(sd_ok, 1)
                    dve.reciprocal(n0_rstd[:, :], n0_rstd[:, :]).then_inc(rs_ok, 1)
                if e % EPG == LAG + 2 and e >= EPG:
                    group_mod(e // EPG - 1)
                if e in NORM_AT:
                    h_lo(NORM_AT[e])
            group_mod(E_GROUPS - 1)
            for kt in range(len(NORM_AT), KT):
                h_lo(kt)
            dve.wait_ge(ld_sub, 16)
            dve.tensor_scalar(gsub[:, :], gsub[:, :], 1.0 - LAMBDA_INIT, None, ALU.mult).then_inc(small_ok, 1)
            dve.wait_ge(small_ok, 1)

            def lo_early(c):
                lo(c, RAW_OF[("w", c)] % NR, EC + c)

            def late_out(hf):
                if hf not in SUM_OF:
                    return None
                g, t = SUM_OF[hf]
                tile = MOD_EARLY + LGT * g + t
                return dve.tensor_scalar(mod[:, tile, :], out_bank(hf)[:, H0:H0 + 2], cols[:, BT, tile:tile + 1], None,
                                         ALU.add)

            def late_sum(n):
                x = ("mod", n)
                g = n // LPG
                dve.wait_ge(ld_raw[RAW_OF[x] % NR], LOADED[x])
                if n % LPG == 0 and g >= 2:
                    dve.wait_ge(m_late, LGT * (g - 1))
                if n == LATE1:
                    dve.wait_ge(x_ok, 2 * KT)
                for k in range(LK):
                    kt = LK * (n % LPG) + k
                    w, c = w_raw[RAW_OF[x] % NR][:, LG * k:LG * k + LG], cs[:, kt, 0:1]
                    if kt == 0:
                        ins = dve.tensor_scalar(acc_d[g % 2], w, c, None, ALU.mult)
                    else:
                        dve.wait_ge(late_d, KT * g + kt)
                        ins = dve.scalar_tensor_tensor(out=acc_d[g % 2], in0=w, scalar=c, in1=acc_d[g % 2],
                                                       op0=ALU.mult, op1=ALU.add)
                    ins.then_inc(late_d, 1)

            def z_out(hf):
                dve.wait_ge(g_done, hf + 1)
                x, i = SLABS[hf // 2]
                buf = zq[i % 2] if x == "q" else zk[i % 2] if x == "k" else zv
                a, n = HALF[hf % 2]
                ins = dve.tensor_scalar(buf[:, a:a + n], G[hf % 2][:, 0:n], SCALE if x == "q" else 1.0, None, ALU.mult)
                (late_out(hf) or ins).then_inc(g_free, 1)

            def softmax_max(t):
                qi, i = TURNS[t]
                dve.wait_ge(t_score, t + 1)
                dve.wait_ge(tab_ok, qi + 1)
                st, sb, segs = stats[:, t % 4, :], scores[t % 2], segments(t)
                head = lambda e: 8 * ((qi - A_HEADS) // 4) + (qi - A_HEADS) % 4 + 4 * e
                if not is_a(t):
                    for np_, c, w in ((P, 256, 257),) if i < 3 else ((P, P, 129), (TS, 258 + 160, 161)):
                        dve.tensor_copy(sb[0:np_, c:c + w + 1:w], sinks[0:np_, head(0):head(0) + 5:4])
                for np_, pc, sc, n, tc, e, _q, _k, c in segs:
                    first = LOWEST if is_a(t) else sinks[0:np_, head(e):head(e) + 1]
                    ins = dve.tensor_tensor_reduce(sb[0:np_, sc:sc + n], S[t % 2][0:np_, pc:pc + n],
                                                   tab[qi % 2][0:np_, tc:tc + n], 1.0, first, ALU.add, ALU.max,
                                                   st[0:np_, c:c + 1])
                step(ins)
                groups = ([(P, 0, 2)] if i < 4 else [(TS, i - 4, i - 3)]) if is_a(t) else \
                    [(P, 0, 2)] if i < 3 else [(P, 0, 2), (TS, 2, 4)]
                for np_, c0, c1 in groups:
                    ins = dve.tensor_scalar(st[0:np_, 4 + c0:4 + c1], st[0:np_, c0:c1], -1.0, None, ALU.mult)
                ins.then_inc(t_ttr, 1)

            def combine(t):
                qi, i = TURNS[t]
                dve.wait_ge(t_exp, t + 1)
                st = stats[:, t % 4, :]
                if not is_a(t):
                    ins = dve.reciprocal(st[:, 12:14], st[:, 8:10])
                    if i == 3:
                        ins = dve.reciprocal(st[0:TS, 14:16], st[0:TS, 10:12])
                    ins.then_inc(t_comb, 1)
                    return
                if i < 4:
                    n, np_, st0_, p0 = P * (i + 1), P, st, scores[t % 2][:, 0:P * (i + 1)]
                    p1, out = scores[t % 2][:, 512:512 + n], p0
                else:
                    n, np_, st0_, p0 = PAST + TS, TS, stats[:, (t - 1) % 4, :], scores[(t - 1) % 2][0:TS, 0:PAST + TS]
                    p1 = out = scores[t % 2][0:TS, 0:n]
                dve.reciprocal(st[0:np_, 12:13], st0_[0:np_, 8:9])
                step(dve.reciprocal(st[0:np_, 13:14], st[0:np_, 9:10]))
                step(dve.tensor_scalar(st[0:np_, 16:17], st0_[0:np_, 8:9], st[0:np_, 13:14], neg_lam[0:np_, :],
                                       ALU.mult, ALU.mult))
                dve.scalar_tensor_tensor(out=out, in0=p1, scalar=st[0:np_, 16:17], in1=p0, op0=ALU.mult, op1=ALU.add
                                         ).then_inc(t_comb, 1)

            lo_early(0)
            lo_early(1)
            for k, (hf, part, parts, t, item) in enumerate(SLOTS):
                pt = prev_out(k, 1)
                if (hf and part == 0) or k == TAIL:
                    z_out(hf - 1 if hf else ZH - 1)
                if t is not None:
                    softmax_max(t)
                if pt is not None and not is_a(pt):
                    dve.wait_ge(b6_done, USE6[("p", pt)])
                    if TURNS[pt][1] < 3:
                        dve.tensor_copy(probsT[:, :], B6[:, :]).then_inc(b6_free, 1)
                    else:
                        dve.tensor_copy(probsT[:, 0:2 * P], B6[:, 0:2 * P])
                        for e in range(2):
                            c = 256 + 64 * e
                            dve.tensor_copy(probsT[:, c:c + TS], B6[:, c:c + TS])
                            ins = dve.tensor_copy(probsT[0:TS, c + TS:c + 2 * TS], B6[0:TS, c + TS:c + 2 * TS])
                        ins.then_inc(b6_free, 1)
                if hf is not None and part == 0 and hf + 2 < FC0:
                    lo_early(hf + 2)
                if hf is None:
                    for kt in TAIL_SPLITS[k - TAIL]:
                        dve.wait_ge(n_hi, KT + kt + 1)
                        dve.tensor_tensor(x_lo[:, kt, :], oT[:, kt, :], x_hi[:, kt, :].bitcast(F32), ALU.subtract
                                          ).then_inc(x_ok, 1)
                if t is not None and has_out(t):
                    combine(t)
                begin, end = late_of(hf, part, parts)
                for n in begin:
                    late_sum(n)
                if pt is not None and is_a(pt):
                    dve.wait_ge(t_rstd, OUT_A[pt])
                    n = pv_blocks(pt)[0][0]
                    dve.scalar_tensor_tensor(out=o_norm[0:n, 0:P], in0=o_raw[0:n, :], scalar=stats[0:n, pt % 4, 19:20],
                                             in1=gsub[0:n, :], op0=ALU.mult, op1=ALU.mult).then_inc(t_on_a, 1)
                for n in end:
                    late_sum(n)

            def gated(n, h, b, gate):
                for a, m, g in PIECES[h]:
                    ins = dve.scalar_tensor_tensor(out=x1[:, n, a:a + m], in0=b[:, a - HALF[h][0]:a - HALF[h][0] + m],
                                                   scalar=mod[:, gate + n, g:g + 1], in1=x1[:, n, a:a + m],
                                                   op0=ALU.mult, op1=ALU.add)
                return ins

            for hf in range(ZH, ZH + OH):
                if hf + 2 < FC0:
                    lo_early(hf + 2)
                n, h = (hf - ZH) // 2, hf % 2
                if h == 0 and n % 4 == 0:
                    dve.wait_ge(xr[n // 4], 16)
                dve.wait_ge(g_done, hf + 1)
                ins = gated(n, h, out_bank(hf), GT_A)
                (late_out(hf) or ins).then_inc(g_free, 1)
                for x in late_of(hf, 0, 1):
                    for c in x:
                        late_sum(c)
                if h:
                    dve.wait_ge(g_free, hf + 1)
                    add_square(n, x1, n2[0][:, :], n2[1][:, :])

            dve.wait_ge(g_free, ZH + OH)
            scales(SC_F, KT, KT)

            def lo_ffn(f):
                n, i = f
                lo(n, n % NR, SC0 + n if i is None else i * LOOP_CHUNKS + (SC0 + n))

            lo_ffn((0, None))
            lo_ffn((1, None))
            inverse(1, n2[2][:, :])
            dve.wait_ge(mod_ok, KT // EGT + 1)
            normalise(1, x1, [cv[0][:, 0:T], cv[1][:, 0:T]], [ext[0][:, 0:T], ext[1][:, 0:T]], n2[2][:, :])
            dve.wait_ge(x_ok, 3 * KT)
            for x in range(2):
                ins = dve.memset(ext[x][:, 0:2], 0.0)
            ins.then_inc(d_ev, 4)

            def conv(x, J, done):
                tile = J + FT * x
                dve.tensor_copy(ext[x][:, TP + 2:TP + 4], cols[:, STATE:STATE + 2, bass.ds(tile, 1)]
                                .rearrange("p a b -> p (a b)")).then_inc(ext_ok, 1)
                dve.wait_ge(ext_ok, J * 2 + (x + 1))
                dve.tensor_copy(u_last[:, bass.ds(tile, 1), :].rearrange("p o (a b) -> p (o a) b", b=2),
                                ext[x][:, TP:TP + 2 * (TS + 2)].rearrange("p (a b) -> p a b", b=TS + 2)[:, :, 0:2])
                w = lambda i: cols[:, CONV_W + i, bass.ds(tile, 1)]
                dve.tensor_scalar(cv[x][:, :], ext[x][:, 2:T + 4], w(2), cols[:, CONV_B, bass.ds(tile, 1)],
                                  ALU.mult, ALU.add).then_inc(cv_ok, 1)
                dve.wait_ge(cv_ok, J * 4 + (2 * x + 1))
                dve.scalar_tensor_tensor(out=cv[x][:, :], in0=ext[x][:, 1:T + 3], scalar=w(1), in1=cv[x][:, :],
                                         op0=ALU.mult, op1=ALU.add).then_inc(cv_ok, 1)
                dve.wait_ge(cv_ok, J * 4 + (2 * x + 2))
                dve.scalar_tensor_tensor(out=cv[x][:, :], in0=ext[x][:, 0:T + 2], scalar=w(0), in1=cv[x][:, :],
                                         op0=ALU.mult, op1=ALU.add).then_inc(done, 1)

            def down_out(q, jj, Jd):
                dve.wait_ge(d_done, Jd * 8 + (q + 1))
                gated(4 * jj + q // 2, q % 2, bank(4 + q % 4), GT_F).then_inc(d_ev, 1)

            def hidden(J, par, jj, f, has_down, last):
                at = lambda n: (f[0] + n, f[1])
                lo_ffn(at(2))
                lo_ffn(at(3))
                dve.wait_ge(u_ev, J * 4 + 2)
                conv(0, J, c_gate)
                if has_down:
                    lo_ffn(at(4))
                    lo_ffn(at(5))
                dve.wait_ge(u_ev, J * 4 + 4)
                conv(1, J, c_val)
                out = (lambda q: down_out(q, jj, J - GRP)) if has_down else (lambda q: None)
                out(0)
                dve.wait_ge(c_val, J + 1)
                dve.wait_ge(c_silu, J + 1)
                dve.tensor_tensor(cv[1][:, :], cv[0][:, :], cv[1][:, :], ALU.mult).then_inc(y_mul, 1)
                out(1)
                nxt = 6 if has_down else 4
                if not last:
                    lo_ffn(at(nxt))
                    lo_ffn(at(nxt + 1))
                out(2)
                out(3)
                dve.wait_ge(y_hi_ok, J + 1)
                for a, n, g in ((0, TP, 0), (TP, TS, 1)):
                    ins = dve.tensor_tensor(y_lo[par][:, jj, a:a + n], cv[1][:, a + 2 * g:a + 2 * g + n],
                                            y_hi[par][:, jj, a:a + n].bitcast(F32), ALU.subtract)
                ins.then_inc(y_ok, 1)
                for q in range(4, 8):
                    out(q)

            for jj in range(GRP):
                hidden(jj, 0, jj, (4 * jj, None), False, False)
            with dve.Fori(0, (NG - 1) // 2) as i:
                for gg in range(2):
                    for jj in range(GRP):
                        hidden(i * (2 * GRP) + (GRP * (gg + 1) + jj), (gg + 1) % 2, jj,
                               (4 * GRP + 24 * gg + 6 * jj, i), True, False)
            for n in range(8):
                if n >= 2:
                    lo_ffn((LAST_DOWN + n, None))
                for q in range(4 * (n % 2), 4 * (n % 2) + 4):
                    down_out(q, n // 2, GRP * (NG - 1) + n // 2)
                    if q % 2:
                        dve.wait_ge(d_ev, 4 + 8 * (GRP * (NG - 1) + n // 2) + q + 1)
                        add_square(4 * (n // 2) + q // 2, x1, cv[0][:, 0:T], cv[1][:, 0:T])
            inverse(2, ext[0][:, 0:T])
            for kt in range(KT):
                if kt >= 2:
                    dve.wait_ge(f_t, kt - 1)
                dve.scalar_tensor_tensor(out=cv[kt % 2][:, 0:T], in0=x1[:, kt, :], scalar=cols[:, GT, 2 * KT + kt:2 * KT + kt + 1],
                                         in1=ext[0][:, 0:T], op0=ALU.mult, op1=ALU.mult).then_inc(f_mul, 1)
                if kt >= 2 and kt % 2 == 0 or kt == KT - 1:
                    for o in ([kt - 1] if kt < KT - 1 else [kt]):
                        dve.wait_ge(f_t, o + 1)
                        b = F_BANKS[o % 3]
                        dve.tensor_copy(y_nat[:, 0:QT, P * o:P * o + P],
                                        bank(b)[:, :].rearrange("p (t n) -> p t n", n=P))
                        dve.tensor_copy(y_nat[0:TS, QT, P * o:P * o + P], bank(b + 1)[0:TS, 0:P]).then_inc(f_evd, 1)

        @block.tensor
        def _(pe):
            def row(i):
                n = ROW_COUNTS[i]
                pe.transpose(psw[:, 2048 + P * i:2048 + P * i + n], rows[0:n, i, :], ident[0:n, 0:n]).then_inc(rows_t, 1)

            pe.wait_ge(consts, 5)
            pe.wait_ge(ld_c, 32)
            row(0)

            def sum_squares(n, acc):
                pe.wait_ge(sq_ok, n + 1)
                b = 4 if n else 0
                pe.matmul(bank(b), ones[:, :], acc[:, 0:TP], start=True, stop=True)
                pe.matmul(bank(b + 1)[:, 0:TS], ones[:, :], acc[:, TP:T], start=True, stop=True).then_inc(ss_ok, 1)

            def group_columns(g):
                pe.wait_ge(e_ev, g + 1)
                if g:
                    pe.wait_ge(e_tev, g)
                for t in range(EGT):
                    col = 2 * (early_tile(g) + t)
                    mm = pe.matmul(bank(5)[:, col:col + 2], mod_rows[g % 2][0:4, P * t:P * t + P], pair[0:4, :],
                                   start=True, stop=True)
                mm.then_inc(e_t, 1)

            pe.wait_ge(c_lo, 1)
            for e in range(EC):
                g, first = e // EPG, e % EPG == 0
                if first and g >= 2:
                    pe.wait_ge(e_ev, g - 1)
                if e == EPG:
                    pe.wait_ge(rows_ev, len(ROW_COUNTS))
                pe.wait_ge(s_lo, e + 1)
                for k in range(EK):
                    kt = EK * (e % EPG) + k
                    for part in (w_hi, w_lo):
                        mm = pe.matmul(bank(7 - g % 2)[0:4, :], c_parts[:, kt, :], part[e % NW][:, EG * k:EG * k + EG],
                                       start=(kt == 0 and part is w_hi), stop=(kt == KT - 1 and part is w_lo))
                mm.then_inc(m_used, 1)
                if e == 3:
                    pe.wait_ge(ld_rows, 16 * 10)
                    for i in range(1, len(ROW_COUNTS)):
                        row(i)
                kt = e - X_AT
                if 0 <= kt < KT:
                    if kt == 0:
                        pe.wait_ge(ld_x, 16 * (QT + 1))
                    if kt >= 2:
                        pe.wait_ge(xt_ev, kt - 1)
                    b = bank(2 * (kt % 2), 2)
                    for t in range(QT):
                        pe.transpose(b[:, P * t:P * t + P], x_nat[t][:, P * kt:P * kt + P], ident[:, :])
                    pe.transpose(b[:, TP:T], x_nat[QT][0:TS, P * kt:P * kt + P], ident[0:TS, 0:TS]).then_inc(xt_t, 1)
                if e == SUM_AT + 2:
                    pe.wait_ge(xt_ev, KT)
                    sum_squares(0, n0_acc)
                if e % EPG == LAG and e >= EPG:
                    group_columns(g - 1)
            group_columns(E_GROUPS - 1)

            def products(out, n, hi_w, lo_w, hi_x, lo_x, first, last):
                pe.matmul(out[:, 0:n], hi_w, hi_x, start=first, stop=False)
                pe.matmul(out[:, 0:n], hi_w, lo_x, start=False, stop=False)
                return pe.matmul(out[:, 0:n], lo_w, hi_x, start=False, stop=last)

            def late_tile(g, t, hf):
                pe.wait_ge(late_d, KT * (g + 1))
                pe.wait_ge(late_p, LPG * (g + 1))
                for st, acc in enumerate((acc_d, acc_p)):
                    mm = pe.matmul(out_bank(hf)[:, H0 + st:H0 + st + 1], acc[g % 2][:, P * t:P * t + P], ones[:, 0:1],
                                   start=True, stop=True)
                mm.then_inc(m_late, 1)

            def tiles(hf, kts):
                s, h = hf // 2, hf % 2
                a, n = HALF[h]
                for kt in kts:
                    c = 2 * s + kt // BLK
                    if kt == 0:
                        if hf >= 2:
                            pe.wait_ge(g_free, hf - 1 if hf < ZH + 2 else max(hf - 3, ZH))
                        if hf == ZH + 2:
                            pe.wait_ge(t_ttr, len(TURNS))
                        if hf in SUM_OF:
                            late_tile(*SUM_OF[hf], hf)
                    if kt % BLK == 0 and h == 0:
                        pe.wait_ge(s_lo, EC + c + 1)
                    if hf in (0, ZH):
                        pe.wait_ge(x_ok, (KT if hf else 0) + kt + 1)
                    w = slice(P * (kt % BLK), P * (kt % BLK) + P)
                    mm = products(out_bank(hf), n, w_hi[c % NW][:, w], w_lo[c % NW][:, w], x_hi[:, kt, a:a + n],
                                  x_lo[:, kt, a:a + n], kt == 0, kt == KT - 1)
                    if kt == KT - 1:
                        mm.then_inc(g_done, 1)

            def z_ready(ki_or_qi, what):
                pe.wait_ge(g_free, 2 * SLAB_OF[(what, ki_or_qi)] + 2)

            def score(t):
                qi, i = TURNS[t]
                ki = kv_of(qi)
                z_ready(qi, "q")
                z_ready(ki, "k")
                if t >= 2:
                    pe.wait_ge(t_ttr, t - 1)
                for np_, pc, _sc, _n, _tc, e, q0, keys, _c in segments(t):
                    r = slice(64 * e, 64 * e + 64)
                    for src, k0, n in keys:
                        if src == "past":
                            pe.wait_ge(b6_free, USE6[("x", ki, "p")])
                        kk = (past_kT if src == "past" else zk[ki % 2])[r, k0:k0 + n]
                        mm = pe.matmul(S[t % 2][0:np_, pc:pc + n], zq[qi % 2][r, q0:q0 + np_], kk, start=True, stop=True)
                        pc += n
                mm.then_inc(t_score, 1)

            def bank6(use):
                if use > 1:
                    pe.wait_ge(b6_free, use - 1)

            def turn_probs(t):
                if is_a(t):
                    pe.wait_ge(t_comb, OUT_COUNT[t])
                else:
                    pe.wait_ge(t_exp, t + 1)
                bank6(USE6[("p", t)])
                for np_, _c, _tok, blocks in pv_blocks(t):
                    for sc, n, _src, _tile, _vc, _vn, _oc, tc in blocks:
                        mm = pe.transpose(B6[0:n, tc:tc + np_], scores[t % 2][0:np_, sc:sc + n], ident[0:np_, 0:np_])
                mm.then_inc(b6_done, 1)

            def values(t):
                ki = kv_of(TURNS[t][0])
                pe.wait_ge(b6_free, max(USE6[("p", t)], USE6[("x", ki, "s" if TURNS[t][1] >= 3 else "v")]))
                prev = OUT_COUNT[t] - 1
                if prev:
                    pe.wait_ge(t_otev, prev)
                for np_, _c, tok, blocks in pv_blocks(t):
                    if tok == TP:
                        pe.wait_ge(ld_pv, 16 * (ki + 1))
                    for j, (_sc, n, src, tile, vc, vn, oc, tc) in enumerate(blocks):
                        v = (past_v if src == "past" else v_nat[ki % 2])[0:n, P * tile + vc:P * tile + vc + vn]
                        first = j == 0 or blocks[j - 1][6] != oc
                        last = j == len(blocks) - 1 or blocks[j + 1][6] != oc
                        mm = pe.matmul(B7[0:np_, oc:oc + vn], probsT[0:n, tc:tc + np_], v, start=first, stop=last)
                mm.then_inc(t_pv, 1)

            def turn_output(t):
                if is_a(t):
                    pe.wait_ge(t_on_a, OUT_A[t])
                else:
                    pe.wait_ge(t_on_b, OUT_B[t])
                for np_, c, _tok, _b in pv_blocks(t):
                    mm = pe.transpose(B7[:, 256 + c:256 + c + np_], o_norm[0:np_, c:c + P], ident[0:np_, 0:np_])
                mm.then_inc(t_ot, 1)

            def kv_item(ki, x):
                z_ready(ki, "v" if x in "vs" else "k")
                bank6(USE6[("x", ki, x)])
                if x == "v":
                    for t in range(QT):
                        mm = pe.transpose(B6[:, P * t:P * t + P], zv[:, P * t:P * t + P], ident[:, :])
                elif x == "s":
                    pe.transpose(B6[0:TS, 0:P], zv[:, TP:T], ident[:, :])
                    mm = pe.transpose(B6[0:TS, P:2 * P], zk[ki % 2][:, TP:T], ident[:, :])
                elif x == "p":
                    pe.wait_ge(ld_pk, 16 * (ki + 1))
                    for t in range(4 if ki < A_HEADS else 1):
                        mm = pe.transpose(B6[:, P * t:P * t + P], past_k[:, P * t:P * t + P], ident[:, :])
                else:
                    for t in range(0 if ki < A_HEADS else 3, QT):
                        mm = pe.transpose(B6[:, P * t:P * t + P], zk[ki % 2][:, P * t:P * t + P], ident[:, :])
                mm.then_inc(b6_done, 1)

            for k, (hf, part, parts, t, item) in enumerate(SLOTS):
                pt, pp = prev_out(k, 1), prev_out(k, 2)
                n = KT // parts
                cut = [n * part + c for c in (0, n // 4, 5 * n // 8, n)]
                if t is not None:
                    score(t)
                if hf is not None:
                    tiles(hf, range(cut[0], cut[1]))
                if pt is not None:
                    turn_probs(pt)
                if pp is not None:
                    turn_output(pp)
                if hf is not None:
                    tiles(hf, range(cut[1], cut[2]))
                if pt is not None:
                    values(pt)
                if item:
                    kv_item(*item)
                if hf is not None:
                    tiles(hf, range(cut[2], cut[3]))
            for hf in range(ZH, ZH + OH):
                tiles(hf, range(KT))
            sum_squares(1, n2[1])
            pe.wait_ge(g_free, ZH + OH)

            def lo_ready(f):
                n, i = f
                pe.wait_ge(s_lo, SC0 + n + 1 if i is None else i * LOOP_CHUNKS + (SC0 + n + 1))

            def up(J, f, x):
                for h, (a, n) in enumerate(HALF):
                    if not isinstance(J, int) or J:
                        pe.wait_ge(u_ev, J * 4 + (2 * x + h - 3))
                    for kt in range(KT):
                        c = f[0] + 2 * x + kt // BLK
                        if kt % BLK == 0 and h == 0:
                            lo_ready((c, f[1]))
                        if isinstance(J, int) and J == 0 and x == 0 and h == 0:
                            pe.wait_ge(x_ok, 2 * KT + kt + 1)
                        w = slice(P * (kt % BLK), P * (kt % BLK) + P)
                        mm = products(bank(2 * x + h), n, w_hi[c % NW][:, w], w_lo[c % NW][:, w], x_hi[:, kt, a:a + n],
                                      x_lo[:, kt, a:a + n], kt == 0, kt == KT - 1)
                    mm.then_inc(u_done, 1)

            def down(Jd, f, par):
                for q in range(8):
                    c, nn, h = f[0] + q // 4, q % 4 // 2, q % 2
                    if q % 4 == 0:
                        lo_ready((c, f[1]))
                    pe.wait_ge(d_ev, Jd * 8 + (q + 1))
                    a, n = HALF[h]
                    for kt in range(GRP):
                        w = slice(256 * kt + P * nn, 256 * kt + P * nn + P)
                        mm = products(bank(4 + q % 4), n, w_hi[c % NW][:, w], w_lo[c % NW][:, w], y_hi[par][:, kt, a:a + n],
                                      y_lo[par][:, kt, a:a + n], kt == 0, kt == GRP - 1)
                    mm.then_inc(d_done, 1)

            for jj in range(GRP):
                up(jj, (4 * jj, None), 0)
                up(jj, (4 * jj, None), 1)
            with pe.Fori(0, (NG - 1) // 2) as i:
                for gg in range(2):
                    for jj in range(GRP):
                        J = i * (2 * GRP) + (GRP * (gg + 1) + jj)
                        f = (4 * GRP + 24 * gg + 6 * jj, i)
                        up(J, f, 0)
                        up(J, f, 1)
                        if jj == 0:
                            pe.wait_ge(y_ok, J)
                        down(J - GRP, (f[0] + 4, i), gg % 2)
            pe.wait_ge(y_ok, FT)
            for jj in range(GRP):
                down(GRP * (NG - 1) + jj, (LAST_DOWN + 2 * jj, None), (NG - 1) % 2)
            pe.wait_ge(c_val, FT)
            pe.wait_ge(u_ev, 4 * FT)
            for r in range(4):
                mm = pe.transpose(bank(3)[0:2 * FT, P * r:P * r + P], u_last[:, :, r], ident[:, :])
            mm.then_inc(uc_t, 1)
            sum_squares(2, cv[1])
            for kt in range(KT):
                pe.wait_ge(f_mul, kt + 1)
                if kt == 2:
                    pe.wait_ge(sd_ok, 3)
                if kt >= 3:
                    o = kt - 3
                    pe.wait_ge(f_evd if o % 2 else f_eva, o // 2 + 1)
                b = bank(F_BANKS[kt % 3], 2)
                for t in range(QT):
                    pe.transpose(b[:, P * t:P * t + P], cv[kt % 2][:, P * t:P * t + P], ident[:, :])
                pe.transpose(b[0:TS, 512:512 + P], cv[kt % 2][:, TP:T], ident[:, :]).then_inc(f_t, 1)


_INS = ["x_prompt", "x_sample", "cache_a_k", "cache_a_v", "cache_b_k", "cache_b_v", "state_conv", "c_prompt",
        "c_sample", "w_mod", "b_mod", "g_attn", "w_in", "lambda_q1", "lambda_k1", "lambda_q2", "lambda_k2",
        "subln_g", "sinks", "w_out", "g_ffn", "w_up", "conv_w", "conv_b", "w_down", "g_final"]
_OUTS = [("y_p", (1, TP, D)), ("y_s", (1, TS, D)), ("ak_p", (1, 1, TP, A_HEADS, 2 * A_DK)),
         ("av_p", (1, 1, TP, A_HEADS, A_DV)), ("bk_p", (1, 1, P, 4, B_DH)), ("bv_p", (1, 1, P, 4, B_DH)),
         ("conv_p", (1, 1, 2, 2 * DFF)), ("ak_s", (1, 1, TS, A_HEADS, 2 * A_DK)),
         ("av_s", (1, 1, TS, A_HEADS, A_DV)), ("bk_s", (1, 1, P, 4, B_DH)), ("bv_s", (1, 1, P, 4, B_DH)),
         ("conv_s", (1, 1, 2, 2 * DFF))]


def kernel(**inputs):
    import numpy as np
    import concourse.bacc as bacc
    from concourse.bass_utils import run_bass_kernel_spmd

    nc = bacc.Bacc("TRN2", target_bir_lowering=False, num_devices=1)
    arrays, A, O = {}, {}, {}
    for name in _INS:
        a = np.ascontiguousarray(inputs[name])
        arrays[f"in_{name}"] = a
        A[name] = nc.dram_tensor(f"in_{name}", a.shape, mybir.dt.from_np(a.dtype), kind="ExternalInput").ap()
    for name, shape in _OUTS:
        O[name] = nc.dram_tensor(f"out_{name}", shape, F32, kind="ExternalOutput").ap()
    build(nc, A, O)
    r = run_bass_kernel_spmd(nc, [arrays], core_ids=[0])
    return tuple(r.results[0][f"out_{name}"] for name, _ in _OUTS)
```

```python
from contextlib import ExitStack

import concourse.bass as bass
from concourse import mybir

F32 = mybir.dt.float32
F32R = mybir.dt.float32r
ALU = mybir.AluOpType
ACT = mybir.ActivationFunctionType

P = 128
D = 2048
KT = D // P
TP, TS = 512, 32
T = TP + TS
QT = TP // P
H0 = T // 2
HALF = [(0, H0), (H0, T - H0)]
PIECES = [[(0, H0, 0)], [(H0, TP - H0, 0), (TP, TS, 1)]]
BLK = 8
CW = BLK * P
NR = 4
NW = 4
PAST = 512
CHUNK = 64
A_HEADS, A_DK, A_DV = 8, 64, 128
B_HEADS, B_DH, B_GROUP = 16, 64, 4
SCALE = A_DK ** -0.5
A_QW = A_HEADS * 2 * A_DK
DFF = 5632
FT = DFF // P
GRP = 4
NG = FT // GRP
EPS = 1e-6
LAMBDA_INIT = 0.2
NEG_LARGE = -2.0 ** 110
LOWEST = -3.0e38
ZSLABS = 36
ZH = 2 * ZSLABS
OH = 2 * KT
MOD_EARLY = 32
MOD_TILES = 96
SH_A, SC_A, GT_A, SH_F, SC_F, GT_F = range(0, MOD_TILES, KT)
LG = 256
LGT = LG // P
LK = CW // LG
LPG = KT // LK
EG = 512
EGT = EG // P
E_GROUPS = MOD_EARLY // EGT
EK = CW // EG
EPG = KT // EK
EC = E_GROUPS * EPG
TAB = 640


def slope_a(h):
    return 2.0 ** (-8.0 * (h + 1) / A_HEADS)


def slope_b(h):
    return 2.0 ** (-8.0 * (h + 1) / B_HEADS)


SLABS = [(x, h) for h in range(A_HEADS) for x in "qkv"]
for _m in range(2):
    SLABS += [("k", A_HEADS + _m), ("v", A_HEADS + _m)]
    SLABS += [("q", A_HEADS + 4 * _m + i) for i in range(4)]
SLAB_OF = {x: s for s, x in enumerate(SLABS)}


def kv_of(qi):
    return qi if qi < A_HEADS else A_HEADS + (qi - A_HEADS) // 4


TURNS = [(h, i) for h in range(A_HEADS) for i in range(6)]
TURNS += [(A_HEADS + u, i) for u in range(8) for i in range(4)]


def is_a(t):
    return TURNS[t][0] < A_HEADS


def has_out(t):
    return not (is_a(t) and TURNS[t][1] == 4)


def make_slots():
    turns = {6 * (h + 1) + i: [6 * h + i] for h in range(A_HEADS) for i in range(6)}
    items = {6 * (h + 1) + i: [(h, x)] for h in range(A_HEADS) for i, x in enumerate("vspk")}
    b = 6 * A_HEADS
    for u, first in ((0, 54), (1, 56), (2, 58), (4, 66), (5, 68), (6, 70)):
        for n in range(2):
            turns[first + n] = [b + 4 * u + 2 * n, b + 4 * u + 2 * n + 1]
    for n in range(4):
        turns[60 + n] = [b + 12 + n]
    items[52], items[53], items[54] = [(8, "v")], [(8, "s")], [(8, "p"), (8, "k")]
    items[64], items[65] = [(9, "v"), (9, "s")], [(9, "p"), (9, "k")]
    slots = []
    for hf in range(ZH):
        tt, ii = turns.get(hf, []), items.get(hf, [])
        n = max(1, len(tt), len(ii))
        for p in range(n):
            slots.append((hf, p, n, tt[p] if p < len(tt) else None, ii[p] if p < len(ii) else None))
    for t in range(b + 28, b + 32):
        slots.append((None, 0, 1, t, None))
    slots += [(None, 0, 1, None, None)] * 2
    return slots


SLOTS = make_slots()
TAIL = len(SLOTS) - 6
TAIL_SPLITS = [range(0, 4), range(4, 8), range(8, 11), range(11, 14), range(14, 15), range(15, 16)]


def segments(t):
    qi, i = TURNS[t]
    if qi < A_HEADS:
        if i < 4:
            n = P * (i + 1)
            return [(P, 512 * m, 512 * m, n, 512 - P * i, m, P * i, [("new", 0, n)], m) for m in range(2)]
        return [(TS, 0, 0, PAST + TS, 0, i - 4, TP, [("past", 0, PAST), ("new", TP, TS)], i - 4)]
    if i < 3:
        q0 = P * (i + 1)
        return [(P, 512 * e, 257 * e, 256, 256 * e, e, q0, [("new", q0 - P, 256)], e) for e in range(2)]
    out = [(P, 512 * e, 129 * e, P, 256 * e + P, e, 0, [("new", 0, P)], e) for e in range(2)]
    out += [(TS, 512 * e + P, 258 + 161 * e, P + TS, 256 * e, e, TP, [("past", 0, P), ("new", TP, TS)], 2 + e)
            for e in range(2)]
    return out


def pv_blocks(t):
    qi, i = TURNS[t]
    if qi < A_HEADS:
        if i < 4:
            return [(P, 0, P * i, [(P * j, P, "new", j, 0, P, 0, P * j) for j in range(i + 1)])]
        blocks = [(P * j, P, "past", j, 0, P, 0, TS * j) for j in range(4)]
        return [(TS, 0, TP, blocks + [(PAST, TS, "new", 4, 0, P, 0, P)])]
    if i < 3:
        return [(P, 0, P * (i + 1), [(257 * e + P * j, P, "new", i + j, 64 * e, 64, 64 * e, P * (2 * e + j))
                                     for e in range(2) for j in range(2)])]
    first = (P, 0, 0, [(129 * e, P, "new", 0, 64 * e, 64, 64 * e, P * e) for e in range(2)])
    blocks = []
    for e in range(2):
        blocks.append((258 + 161 * e, P, "past", 0, 64 * e, 64, P + 64 * e, 256 + 64 * e))
        blocks.append((258 + 161 * e + P, TS, "new", 4, 64 * e, 64, P + 64 * e, 256 + 64 * e + TS))
    return [first, (TS, P, TP, blocks)]


BANK6 = []
for _k, (_hf, _p, _n, _t, _x) in enumerate(SLOTS):
    if _k and SLOTS[_k - 1][3] is not None and has_out(SLOTS[_k - 1][3]):
        BANK6.append(("p", SLOTS[_k - 1][3]))
    if _x:
        BANK6.append(("x",) + _x)
USE6 = {x: n + 1 for n, x in enumerate(BANK6)}
OUTS = [t for t in range(len(TURNS)) if has_out(t)]
OUT_COUNT = {t: n + 1 for n, t in enumerate(OUTS)}
OUT_A = {t: n + 1 for n, t in enumerate([t for t in OUTS if is_a(t)])}
OUT_B = {t: n + 1 for n, t in enumerate([t for t in OUTS if not is_a(t)])}


def scored_ahead(t):
    return is_a(t) or TURNS[t][1] > 0


def next_ahead(k):
    t = SLOTS[k + 1][3] if k + 1 < len(SLOTS) else None
    return t if t is not None and scored_ahead(t) else None


def prev_out(k, back):
    t = SLOTS[k - back][3] if k >= back else None
    return t if t is not None and has_out(t) else None


X_AT = 8
SUM_AT = X_AT + KT + 2
LAG = NW
NORM_AT = {34 + 2 * k if k < 8 else 57 + 2 * (k - 8): k for k in range(12)}


LATE1 = 24 * LPG
LATE2 = (MOD_TILES - MOD_EARLY) // LGT * LPG - LATE1
LATE_AT = [3 + n * 60 // LATE1 for n in range(LATE1)] + [ZH + 1 + n * 28 // LATE2 for n in range(LATE2)]
SUM_OF = {LATE_AT[LPG * g + LPG - 1] + 2 + t: (g, t) for g in range((LATE1 + LATE2) // LPG) for t in range(LGT)}
assert len(SUM_OF) == (LATE1 + LATE2) // LPG * LGT and max(SUM_OF) < ZH + OH


def late_of(hf, part, parts):
    if hf is None:
        return [], []
    c = [n for n, h in enumerate(LATE_AT) if h == hf]
    if parts == 1:
        return c[:1], c[1:]
    return (c[:1] if part == 0 else c[1:] if part == 1 else []), []


def early_tile(g):
    return (SC_A if g % 2 else SH_A) + EGT * (g // 2)


STREAM = [("e", _e) for _e in range(EC)] + [("w", 0), ("w", 1)]
for _hf in range(ZH + OH):
    _late = [("mod", _n) for _n, _h in enumerate(LATE_AT) if _h == _hf]
    STREAM += _late[:1]
    if _hf + 2 < ZH + OH:
        STREAM.append(("w", _hf + 2))
    STREAM += _late[1:]
RAW_OF = {x: r for r, x in enumerate(STREAM)}


def chunk_dmas(c):
    if c < ZH:
        x, qi = SLABS[c // 2]
        return 2 if x == "q" and qi >= A_HEADS else 1
    return 4 if c % 2 else 1


LOADED = {}
_count = [0] * NR
for _r, _x in enumerate(STREAM):
    _count[_r % NR] += 16 * (chunk_dmas(_x[1]) if _x[0] == "w" else 1)
    LOADED[_x] = _count[_r % NR]
FFN_RAW = list(_count)
FC0 = ZH + OH
SC0 = EC + FC0
assert len(STREAM) % NR == FC0 % NR == EC % NR == 0
LOOP_CHUNKS = 2 * GRP * 6
LAST_DOWN = 4 * GRP + LOOP_CHUNKS * (NG - 1) // 2
ROW_COUNTS = [2 * KT, MOD_TILES, 3 * KT] + [2 * FT] * 6


def build(nc, A, O):
    w_in, w_out, w_mod = A["w_in"][0], A["w_out"][0], A["w_mod"][0]
    w_up, w_down = A["w_up"][0], A["w_down"][0]
    scratch = nc.dram_tensor("x_transposed", (KT, P, T), F32, kind="Internal").ap()

    ctx = ExitStack()
    with ctx:
        def on(stack, name, shape, dt=F32):
            return stack.enter_context(nc.sbuf_tensor(name, shape, dt))

        def sem(name):
            return ctx.enter_context(nc.semaphore(name))

        w_raw = [on(ctx, f"w_raw{i}", [P, CW]) for i in range(NR)]
        w_hi = [on(ctx, f"w_hi{i}", [P, CW], F32R) for i in range(NW)]
        w_lo = [on(ctx, f"w_lo{i}", [P, CW], F32R) for i in range(NW)]
        cols = on(ctx, "cols", [P, 9, P])
        mod = on(ctx, "mod", [P, MOD_TILES, 2])
        cs = on(ctx, "cs", [P, KT, 2])
        ident = on(ctx, "ident", [P, P])
        ones = on(ctx, "ones", [P, P])
        tiny = on(ctx, "tiny", [P, 16])
        sinks = on(ctx, "sinks", [P, B_HEADS])
        stats = on(ctx, "stats", [P, 4, 20])
        eps, minus_half, neg_lam = tiny[:, 0:1], tiny[:, 1:2], tiny[:, 2:3]
        CT, BT, GT, CONV_W, CONV_B, STATE = 0, 1, 2, 3, 6, 7
        early = ExitStack()
        x_nat = [on(early, f"x_nat{i}", [P, D]) for i in range(QT + 1)]
        early.close()
        y_nat = on(early, "y_nat", [P, QT + 1, D])
        early.close()
        x_hi = on(ctx, "x_hi", [P, KT, T], F32R)
        x_lo = on(ctx, "x_lo", [P, KT, T], F32R)
        st0 = ExitStack()
        xT = on(st0, "xT", [P, KT, T])
        n0_sq = [on(st0, f"n0_sq{i}", [P, T]) for i in range(2)]
        n0_acc, n0_rstd = on(st0, "n0_acc", [P, T]), on(st0, "n0_rstd", [P, T])
        lam = [on(st0, f"lambda{i}", [P, A_DK]) for i in range(4)]
        c_parts = on(st0, "c_parts", [P, KT, 4], F32R)
        mod_rows = [on(st0, f"mod_rows{i}", [P, EG]) for i in range(2)]
        pair = on(st0, "pair", [P, 2])
        rows = on(st0, "rows", [P, 9, P])
        st0.close()
        st1 = ExitStack()
        zq = [on(st1, f"zq{i}", [P, T]) for i in range(2)]
        zk = [on(st1, f"zk{i}", [P, T]) for i in range(2)]
        zv = on(st1, "zv", [P, T])
        v_nat = [on(st1, f"v_nat{i}", [P, 5 * P]) for i in range(2)]
        k_nat = on(st1, "k_nat", [P, 5 * P])
        past_k = on(st1, "past_k", [P, 4 * P])
        past_v = on(st1, "past_v", [P, 4 * P])
        past_kT = on(st1, "past_kT", [P, 4 * P])
        scores = [on(st1, f"scores{i}", [P, 1024]) for i in range(2)]
        probsT = on(st1, "probsT", [P, 512])
        o_raw = on(st1, "o_raw", [P, P])
        o_norm = on(st1, "o_norm", [P, 2 * P])
        square = on(st1, "square", [P, P])
        oT = on(st1, "oT", [P, KT, T])
        late = oT[:, KT - 4:KT, :].rearrange("p k n -> p (k n)")
        acc_d, acc_p = ([late[:, LG * (2 * x + i):LG * (2 * x + i) + LG] for i in range(2)] for x in range(2))
        late_prod = late[:, 4 * LG:4 * LG + CW]
        tab_a = on(st1, "tab_a", [P, TAB])
        tab_b = on(st1, "tab_b", [P, 256])
        tab = [on(st1, f"tab{i}", [P, TAB]) for i in range(2)]
        gsub = on(st1, "gsub", [P, P])
        st1.close()
        st2 = ExitStack()
        x1 = on(st2, "x1", [P, KT, T])
        st3 = st2
        ext = [on(st3, f"ext{i}", [P, TP + 2 * (TS + 2)]) for i in range(2)]
        cv = [on(st3, f"cv{i}", [P, T + 2]) for i in range(2)]
        n2_st = ExitStack()
        n2_sq, n2_acc, n2_rstd = [on(n2_st, f"n2_{x}", [P, T]) for x in ("sq", "acc", "rstd")]
        n2_st.close()
        y_hi = [on(st3, "y_hi0", [P, GRP, T], F32R)]
        y_lo = [on(st3, "y_lo0", [P, GRP, T], F32R)]
        fin_st = ExitStack()
        xg = [on(fin_st, f"xg{i}", [P, T]) for i in range(2)]
        fin_st.close()
        y_hi.append(on(st3, "y_hi1", [P, GRP, T], F32R))
        y_lo.append(on(st3, "y_lo1", [P, GRP, T], F32R))
        u_last = on(st3, "u_last", [P, 2 * FT, 4])
        u_rows = on(st3, "u_rows", [P, 4, P])
        st3.close()
        h2_t, h2_h = (lambda i, b=b: b[i % 2][:, H0 * (i // 2 % 2):H0 * (i // 2 % 2) + H0] for b in (cv, ext))
        f_sq, f_sum = cv, ext[1][:, 0:T]

        ps = ctx.enter_context(nc.psum_tensor("ps", [P, 8, 512], F32))
        psw = ps[:, :, :].rearrange("p b n -> p (b n)")

        def bank(b, n=1):
            return psw[:, 512 * b:512 * (b + n)]

        G = [bank(0), bank(1)]
        S = [bank(2, 2), bank(4, 2)]

        def out_bank(hf):
            return bank(hf % (2 if hf < ZH else 4))

        B6, B7 = bank(6), bank(7)

        ld_x, ld_rows, ld_small, scratch_out = sem("ld_x"), sem("ld_rows"), sem("ld_small"), sem("scratch_out")
        ld_c, c_hi, c_lo = sem("ld_c"), sem("c_hi"), sem("c_lo")
        e_ev, e_t, e_tev = sem("e_ev"), sem("e_t"), sem("e_tev")
        sq_mul, sq_add = sem("sq_mul"), sem("sq_add")
        ld_raw = [sem(f"ld_raw{i}") for i in range(NR)]
        consts, rows_t, rows_ev, cs_ok = sem("consts"), sem("rows_t"), sem("rows_ev"), sem("cs_ok")
        xt_t, xt_ev = sem("xt_t"), sem("xt_ev")
        sq_ok, ss_ok, sd_ok, rs_ok = sem("sq_ok"), sem("ss_ok"), sem("sd_ok"), sem("rs_ok")
        m_used, m_late, mod_ok = sem("m_used"), sem("m_late"), sem("mod_ok")
        late_d, late_act, late_p, n_aff2 = sem("late_d"), sem("late_act"), sem("late_p"), sem("n_aff2")
        n_mul, n_aff, n_hi, x_ok = sem("n_mul"), sem("n_aff"), sem("n_hi"), sem("x_ok")
        act_own, dve_own, pool_own = sem("act_own"), sem("dve_own"), sem("pool_own")
        s_hi, s_lo = sem("s_hi"), sem("s_lo")
        g_done, g_free = sem("g_done"), sem("g_free")
        lam_dot, lam_exp, small_ok = sem("lam_dot"), sem("lam_exp"), sem("small_ok")
        tab_ok = sem("tab_ok")
        t_score, t_ttr, t_exp, t_comb = sem("t_score"), sem("t_ttr"), sem("t_exp"), sem("t_comb")
        b6_done, b6_free = sem("b6_done"), sem("b6_free")
        t_pv, t_o, t_rstd, t_on_a, t_on_b = sem("t_pv"), sem("t_o"), sem("t_rstd"), sem("t_on_a"), sem("t_on_b")
        t_ot, t_otev = sem("t_ot"), sem("t_otev")
        st_k, st_v, ld_pk, ld_pv = sem("st_k"), sem("st_v"), sem("ld_pk"), sem("ld_pv")
        xr = [sem(f"xr{i}") for i in range(4)]
        u_done, u_ev, c_gate, c_val, c_silu, y_mul, y_hi_ok, y_ok = (
            sem(x) for x in ("u_done", "u_ev", "c_gate", "c_val", "c_silu", "y_mul", "y_hi_ok", "y_ok"))
        d_done, d_ev = sem("d_done"), sem("d_ev")
        f_mul, f_t, f_ev, store = sem("f_mul"), sem("f_t"), sem("f_ev"), sem("store")
        uc_t, uc_ev = sem("uc_t"), sem("uc_ev")
        f_square, f_add, f_sum_t, f_sd, f_rs = (sem(x) for x in ("f_square", "f_add", "f_sum_t", "f_sd", "f_rs"))
        f_sca, f_scd = sem("f_sca"), sem("f_scd")
        h2_ok, h2_sample = sem("h2_ok"), sem("h2_sample")
        ld_sub, st_win, st_conv = sem("ld_sub"), sem("st_win"), sem("st_conv")
        ext_ok, cv_ok = sem("ext_ok"), sem("cv_ok")

        block = ctx.enter_context(nc.Block())

        def w_in_cols(s):
            x, i = SLABS[s]
            if i < A_HEADS:
                return [("qkv".index(x) * A_QW + P * i, P)]
            m, base = (i - A_HEADS) // 4 if x == "q" else i - A_HEADS, 3 * A_QW
            if x == "q":
                head = 2 * B_GROUP * m + (i - A_HEADS) % 4
                return [(base + B_DH * head, B_DH), (base + B_DH * (head + B_GROUP), B_DH)]
            return [(base + B_HEADS * B_DH + (256 if x == "v" else 0) + P * m, P)]

        @block.sync
        def _(sp):
            def slot_free(old):
                if old[0] != "mod":
                    sp.wait_ge(s_lo, old[1] + 1 + (EC if old[0] == "w" else 0))
                else:
                    sp.wait_ge(late_d, LK * (old[1] + 1))
                    sp.wait_ge(late_act, old[1] + 1)

            for r, x in enumerate(STREAM):
                slot = r % NR
                q = (r - X_AT - NR - 5) // 4
                if r % 4 == 1 and 0 <= q < 4:
                    sp.wait_ge(xt_ev, 4 * q + 4)
                    sp.dma_start(scratch[4 * q:4 * q + 4].rearrange("k p t -> p k t"), xT[:, 4 * q:4 * q + 4, :]
                                 ).then_inc(scratch_out, 16)
                if r >= NR:
                    slot_free(STREAM[r - NR])
                dst = w_raw[slot][:, :].rearrange("p (k n) -> p k n", n=P)
                if x[0] == "e":
                    c0, r0 = P * early_tile(x[1] // EPG), EK * P * (x[1] % EPG)
                    sp.dma_start(w_raw[slot][:, :].rearrange("p (k n) -> p k n", n=EG),
                                 w_mod[r0:r0 + EK * P, c0:c0 + EG].rearrange("(k p) n -> p k n", p=P)
                                 ).then_inc(ld_raw[slot], 16)
                elif x[0] == "mod":
                    c0, r0 = P * MOD_EARLY + LG * (x[1] // LPG), LK * P * (x[1] % LPG)
                    sp.dma_start(w_raw[slot][:, :].rearrange("p (k n) -> p k n", n=LG),
                                 w_mod[r0:r0 + LK * P, c0:c0 + LG].rearrange("(k p) n -> p k n", p=P)
                                 ).then_inc(ld_raw[slot], 16)
                elif x[1] < ZH:
                    s, half = x[1] // 2, x[1] % 2
                    at = 0
                    for c0, n in w_in_cols(s):
                        src = w_in[1024 * half:1024 * half + 1024, c0:c0 + n]
                        sp.dma_start(dst[:, :, at:at + n], src.rearrange("(k p) n -> p k n", p=P)
                                     ).then_inc(ld_raw[slot], 16)
                        at += n
                else:
                    n, half = (x[1] - ZH) // 2, x[1] % 2
                    if half == 0:
                        sp.dma_start(dst, w_out[0:1024, P * n:P * n + P].rearrange("(k p) n -> p k n", p=P)
                                     ).then_inc(ld_raw[slot], 16)
                    else:
                        for u in range(2):
                            for m in range(2):
                                r0 = 1024 + 512 * m + 256 * u
                                src = w_out[r0:r0 + 256, P * n:P * n + P]
                                sp.dma_start(dst[64 * u:64 * u + 64, 4 * m:4 * m + 4, :],
                                             src.rearrange("(i p) n -> p i n", p=64)
                                             ).then_inc(ld_raw[slot], 16)

            def up(c, nth, j, k, base):
                slot = c % NR
                if isinstance(nth, int) and nth - SC0 < NR:
                    slot_free(STREAM[nth - SC0 - NR])
                else:
                    sp.wait_ge(s_lo, nth - NR + 1)
                sp.dma_start(w_raw[slot][:, :].rearrange("p (k n) -> p k n", n=P),
                             w_up[1024 * k:1024 * k + 1024, bass.ds(base + P * j, P)]
                             .rearrange("(k p) n -> p k n", p=P)).then_inc(ld_raw[slot], 16)

            def down(c, nth, g, n0_):
                slot = c % NR
                sp.wait_ge(s_lo, nth - NR + 1)
                sp.dma_start(w_raw[slot][:, :].rearrange("p (k n) -> p k n", n=256),
                             w_down[bass.ds(g * (GRP * P), GRP * P), P * n0_:P * n0_ + 256]
                             .rearrange("(k p) n -> p k n", p=P)).then_inc(ld_raw[slot], 16)

            for j in range(GRP):
                for n in range(4):
                    up(4 * j + n, SC0 + 4 * j + n, j, n % 2, DFF * (n // 2))
            with sp.Fori(0, NG - 1) as i:
                for jj in range(GRP):
                    for n in range(4):
                        up(6 * jj + n, i * 24 + (SC0 + 16 + 6 * jj + n), (i + 1) * GRP + jj, n % 2, DFF * (n // 2))
                    for n in range(2):
                        down(6 * jj + 4 + n, i * 24 + (SC0 + 16 + 6 * jj + 4 + n), i, 4 * jj + 2 * n)
            for n in range(8):
                down(n, SC0 + 16 + 24 * (NG - 1) + n, NG - 1, 2 * n)
            for t, ready, n in ((0, f_scd, 1), (2, f_sca, 1), (1, f_scd, 2), (3, f_sca, 2)):
                sp.wait_ge(ready, n)
                sp.dma_start(O["y_p"][0, P * t:P * t + P, :], y_nat[:, t, :]).then_inc(store, 16)
            sp.wait_ge(f_scd, 3)
            sp.dma_start(O["y_s"][0], y_nat[0:TS, QT, :]).then_inc(store, 16)
            sp.wait_ge(store, 16 * (QT + 1))

        @block.gpsimd
        def _(pool):
            own = [0]

            def step(ins):
                own[0] += 1
                ins.then_inc(pool_own, 1)
                pool.wait_ge(pool_own, own[0])

            pool.memset(ones[:, :], 1.0).then_inc(consts, 1)
            step(pool.memset(ident[:, :], 0.0))
            pool.affine_select(out=ident[:, :], in_=ident[:, :], compare_op=ALU.not_equal, fill=1.0, base=0,
                               pattern=[[-1, P]], channel_multiplier=1).then_inc(consts, 1)
            pool.memset(eps, EPS).then_inc(consts, 1)
            pool.memset(minus_half, -0.5).then_inc(consts, 1)
            pool.wait_ge(consts, 4)
            pool.tensor_tensor(pair[0:4, :], ident[0:4, 0:2], ident[0:4, 2:4], ALU.add).then_inc(consts, 1)
            tiled = lambda a: a.rearrange("(k p) -> k p", p=P)
            pool.dma_start(rows[0:MOD_TILES, BT, :], tiled(A["b_mod"][0])).then_inc(ld_rows, 16)
            pool.dma_start(rows[0:KT, GT, :], tiled(A["g_attn"][0])).then_inc(ld_rows, 16)
            pool.dma_start(rows[KT:2 * KT, GT, :], tiled(A["g_ffn"][0])).then_inc(ld_rows, 16)
            pool.dma_start(rows[2 * KT:3 * KT, GT, :], tiled(A["g_final"])).then_inc(ld_rows, 16)
            for i in range(3):
                pool.dma_start(rows[0:2 * FT, CONV_W + i, :], tiled(A["conv_w"][0, i])).then_inc(ld_rows, 16)
            pool.dma_start(rows[0:2 * FT, CONV_B, :], tiled(A["conv_b"][0])).then_inc(ld_rows, 16)
            for i in range(2):
                pool.dma_start(rows[0:2 * FT, STATE + i, :], tiled(A["state_conv"][0, 0, i])).then_inc(ld_rows, 16)
            bc = lambda a: a.partition_broadcast(P).rearrange("p a n -> p (a n)")
            pool.dma_start(sinks[:, :], bc(A["sinks"])).then_inc(ld_small, 16)
            for i, x in enumerate(("q1", "k1", "q2", "k2")):
                pool.dma_start(lam[i][:, :], bc(A[f"lambda_{x}"])).then_inc(ld_small, 16)
            for kt in range(KT):
                pool.wait_ge(xt_ev, kt + 1)
                if kt >= 2:
                    pool.wait_ge(sq_add, max(1, kt - 2))
                pool.tensor_tensor(n0_sq[kt % 2][:, :], xT[:, kt, :], xT[:, kt, :], ALU.mult).then_inc(sq_mul, 1)
            pool.wait_ge(scratch_out, 16 * 4)
            pool.wait_ge(rs_ok, 1)
            def scale_shift(kt):
                pool.wait_ge(mod_ok, kt // EGT + 1)
                pool.wait_ge(n_mul, kt + 1)
                for a, c, g in ((0, TP, 0), (TP, TS, 1)):
                    ins = pool.tensor_scalar(xT[:, kt, a:a + c], xT[:, kt, a:a + c], mod[:, SC_A + kt, g:g + 1],
                                             mod[:, SH_A + kt, g:g + 1], ALU.mult, ALU.add)
                ins.then_inc(n_aff, 1)

            for kt in range(KT):
                pool.tensor_tensor(xT[:, kt, :], xT[:, kt, :], n0_rstd[:, :], ALU.mult).then_inc(n_mul, 1)
                if kt < 2 * EGT:
                    scale_shift(kt)
            for kt in range(2 * EGT, 3 * EGT):
                scale_shift(kt)

            def natural(ki, item):
                sem_, buf = (st_v, v_nat[ki % 2]) if item == "v" else (st_k, k_nat)
                pool.wait_ge(b6_free, USE6[("x", ki, item)])
                if item == "p":
                    return
                if item == "s":
                    lo = 0 if ki < A_HEADS else P - TS
                    for x, b, sm in (("v", v_nat[ki % 2], st_v), ("k", k_nat, st_k)):
                        if ki < A_HEADS:
                            dst = O[f"a{x}_s"][0, 0, :, ki, :]
                        else:
                            m = ki - A_HEADS
                            dst = O[f"b{x}_s"][0, 0, lo:, 2 * m:2 * m + 2, :].rearrange("t h d -> t (h d)")
                        pool.dma_start(dst, b[0:TS, 4 * P:5 * P]).then_inc(sm, 16)
                elif ki < A_HEADS:
                    dst = O[f"a{item}_p"][0, 0, :, ki, :].rearrange("(t p) d -> p t d", p=P)
                    pool.dma_start(dst, buf[:, 0:512].rearrange("p (t d) -> p t d", d=P)).then_inc(sem_, 16)
                else:
                    m = ki - A_HEADS
                    dst = O[f"b{item}_p"][0, 0, :, 2 * m:2 * m + 2, :].rearrange("t h d -> t (h d)")
                    pool.dma_start(dst, buf[:, 384:512]).then_inc(sem_, 16)

            def load_past(which, ki):
                buf, sm = (past_k, ld_pk) if which == "k" else (past_v, ld_pv)
                if ki < A_HEADS:
                    src = A[f"cache_a_{which}"][0, 0, :, ki, :].rearrange("(t p) d -> p t d", p=P)
                    pool.dma_start(buf[:, :].rearrange("p (t d) -> p t d", d=P), src).then_inc(sm, 16)
                else:
                    m = ki - A_HEADS
                    src = A[f"cache_b_{which}"][0, 0, :, 2 * m:2 * m + 2, :].rearrange("t h d -> t (h d)")
                    pool.dma_start(buf[:, 0:P], src).then_inc(sm, 16)

            for x in "kv":
                pool.dma_start(O[f"b{x}_s"][0, 0, 0:P - TS], A[f"cache_b_{x}"][0, 0, TS:P]).then_inc(st_win, 16)

            pool.wait_ge(x_ok, KT)
            pool.wait_ge(scratch_out, 16 * 4)
            load_past("k", 0)
            load_past("v", 0)
            pool.dma_start(gsub[:, :], A["subln_g"].partition_broadcast(P).rearrange("p a n -> p (a n)")
                           ).then_inc(ld_sub, 16)
            step(pool.iota(tab_a[:, :], pattern=[[1, TAB]], base=-512, channel_multiplier=-1,
                           allow_small_or_imprecise_dtypes=True))
            step(pool.tensor_scalar(tab[0][:, :], tab_a[:, :], -1.0, None, ALU.mult))
            step(pool.tensor_scalar(tab[1][:, :], tab_a[:, :], 0.0, -2.0, ALU.max, ALU.mult))
            step(pool.tensor_tensor(tab_a[:, :], tab_a[:, :], tab[1][:, :], ALU.add))
            step(pool.memset(tab_a[0:CHUNK, 512 + CHUNK:TAB], NEG_LARGE))
            step(pool.tensor_copy(tab_b[:, :], tab_a[:, 384:TAB]))
            step(pool.memset(tab_b[CHUNK:P, 0:CHUNK], NEG_LARGE))

            def table(qi):
                if qi >= 2:
                    last = max(t for t in range(len(TURNS)) if TURNS[t][0] == qi - 2)
                    pool.wait_ge(t_ttr, last + 1)
                if qi < A_HEADS:
                    pool.tensor_scalar(tab[qi % 2][:, :], tab_a[:, :], slope_a(qi), None, ALU.mult
                                       ).then_inc(tab_ok, 1)
                else:
                    m, i = (qi - A_HEADS) // 4, (qi - A_HEADS) % 4
                    for e in range(2):
                        ins = pool.tensor_scalar(tab[qi % 2][:, 256 * e:256 * e + 256], tab_b[:, :],
                                                 slope_b(8 * m + 4 * e + i), None, ALU.mult)
                    ins.then_inc(tab_ok, 1)

            def rstd(t):
                pool.wait_ge(t_o, OUT_A[t])
                n = pv_blocks(t)[0][0]
                s = stats[0:n, t % 4, :]
                step(pool.tensor_scalar(s[:, 18:19], s[:, 17:18], 1.0 / A_DV, EPS, ALU.mult, ALU.add))
                pool.tensor_tensor(s[:, 19:20], s[:, 18:19], minus_half[0:n, :], ALU.pow).then_inc(t_rstd, 1)

            def late_add(n):
                g, p = n // LPG, n % LPG
                if p == 0 and g >= 2:
                    pool.wait_ge(m_late, LGT * (g - 1))
                if n == LATE1:
                    pool.wait_ge(x_ok, 2 * KT)
                pool.wait_ge(late_act, n + 1)
                acc, prod = acc_p[g % 2], lambda k: late_prod[:, LG * k:LG * k + LG]
                if n:
                    pool.wait_ge(late_p, n)
                for k in range(1 if p == 0 else 0, LK):
                    ins = pool.tensor_tensor(acc, prod(0) if p == 0 and k == 1 else acc, prod(k), ALU.add)
                    if k < LK - 1:
                        step(ins)
                ins.then_inc(late_p, 1)

            table(0)
            next_table, next_pk, next_pv = 1, 1, 1
            for k, (hf, part, parts, t, item) in enumerate(SLOTS):
                pt = prev_out(k, 1)
                begin, end = late_of(hf, part, parts)
                for n in begin:
                    late_add(n)
                if pt is not None and is_a(pt):
                    rstd(pt)
                if t is not None and TURNS[t][1] == 0 and next_table < 16:
                    table(next_table)
                    next_table += 1
                if item:
                    natural(*item)
                    if item[1] == "p" and next_pk < 10:
                        load_past("k", next_pk)
                        next_pk += 1
                if pt is not None and TURNS[pt][1] == (5 if is_a(pt) else 3):
                    last_of_kv = pt + 1 == len(TURNS) or kv_of(TURNS[pt + 1][0]) != kv_of(TURNS[pt][0])
                    if last_of_kv and next_pv < 10:
                        pool.wait_ge(t_pv, OUT_COUNT[pt])
                        load_past("v", next_pv)
                        next_pv += 1
                for n in end:
                    late_add(n)
            def x_back(q):
                pool.dma_start(x1[:, 4 * q:4 * q + 4, :], scratch[4 * q:4 * q + 4].rearrange("k p t -> p k t")
                               ).then_inc(xr[q], 16)

            pool.wait_ge(t_score, len(TURNS))
            x_back(0)
            pool.wait_ge(t_pv, len(OUTS))
            pool.wait_ge(st_k, 16 * 20)
            pool.wait_ge(st_v, 16 * 20)
            x_back(1)
            pool.wait_ge(t_otev, len(OUTS))
            x_back(2)
            x_back(3)
            for n in range(LATE1, LATE1 + LATE2):
                late_add(n)
            for kt in range(KT):
                i = KT + kt
                pool.wait_ge(n_mul, KT + i + 1)
                pool.wait_ge(x_ok, 2 * KT + i - 3)
                pool.tensor_scalar(h2_h(i)[:, TP - H0:T - H0], h2_t(i)[:, TP - H0:T - H0], mod[:, SC_F + kt, 1:2],
                                   mod[:, SH_F + kt, 1:2], ALU.mult, ALU.add).then_inc(h2_sample, 1)
            for kt in range(KT):
                pool.wait_ge(f_square, kt + 1)
                if kt == 1:
                    pool.tensor_tensor(f_sum, f_sq[0][:, 0:T], f_sq[1][:, 0:T], ALU.add).then_inc(f_add, 1)
                elif kt > 1:
                    pool.wait_ge(f_add, kt - 1)
                    pool.tensor_tensor(f_sum, f_sum, f_sq[kt % 2][:, 0:T], ALU.add).then_inc(f_add, 1)
            pool.wait_ge(uc_ev, 1)
            for r in range(4):
                dst = O["conv_p" if r < 2 else "conv_s"][0, 0, r % 2, :].rearrange("(j p) -> j p", p=P)
                pool.dma_start(dst, u_rows[0:2 * FT, r, :]).then_inc(st_conv, 16)
            pool.wait_ge(st_conv, 64)
            pool.wait_ge(st_win, 32)

        @block.scalar
        def _(act):
            own = [0]

            def step(ins):
                own[0] += 1
                ins.then_inc(act_own, 1)
                act.wait_ge(act_own, own[0])

            tiled = lambda a: a.rearrange("(k p) -> k p", p=P)
            act.dma_start(rows[0:KT, 0, :], tiled(A["c_prompt"][0])).then_inc(ld_c, 16)
            act.dma_start(rows[KT:2 * KT, 0, :], tiled(A["c_sample"][0])).then_inc(ld_c, 16)
            for t in range(QT):
                act.dma_start(x_nat[t][:, :], A["x_prompt"][0, P * t:P * t + P, :]).then_inc(ld_x, 16)
            act.dma_start(x_nat[QT][0:TS, :], A["x_sample"][0]).then_inc(ld_x, 16)
            act.wait_ge(rows_ev, 1)
            act.activation(cs[:, :, :].rearrange("p k g -> p g k"),
                           cols[:, CT, 0:2 * KT].rearrange("p (g k) -> p g k", g=2), ACT.Silu).then_inc(cs_ok, 1)
            act.wait_ge(cs_ok, 1)
            act.activation(c_parts[:, :, 0:2], cs[:, :, :], ACT.Copy).then_inc(c_hi, 1)
            act.wait_ge(consts, 5)

            def root(n, dst):
                act.wait_ge(ss_ok, n + 1)
                act.activation(dst, bank(4 if n else 0, 2)[:, 0:T], ACT.Sqrt, bias=eps, scale=1.0 / D).then_inc(sd_ok, 1)

            def hi(c, raw, count):
                act.wait_ge(ld_raw[raw], count)
                act.activation(w_hi[c % NW][:, :], w_raw[raw][:, :], ACT.Copy).then_inc(s_hi, 1)

            def hi_early(c):
                if c >= NW:
                    act.wait_ge(g_done, 2 * ((c - NW) // 2) + 2)
                else:
                    act.wait_ge(m_used, EC - NW + c + 1)
                hi(c, RAW_OF[("w", c)] % NR, LOADED[("w", c)])

            def group_out(g):
                act.wait_ge(m_used, EPG * (g + 1))
                if g >= 2:
                    act.wait_ge(e_t, g - 1)
                act.activation(mod_rows[g % 2][0:4, :], bank(7 - g % 2)[0:4, :], ACT.Copy).then_inc(e_ev, 1)

            def scale_shift(kt):
                act.wait_ge(n_mul, kt + 1)
                act.wait_ge(mod_ok, kt // EGT + 1)
                for a, c, g in ((0, TP, 0), (TP, TS, 1)):
                    ins = act.activation(xT[:, kt, a:a + c], xT[:, kt, a:a + c], ACT.Identity,
                                         bias=mod[:, SH_A + kt, g:g + 1], scale=mod[:, SC_A + kt, g:g + 1])
                ins.then_inc(n_aff2, 1)

            def h_hi(kt):
                if kt < len(NORM_AT):
                    act.wait_ge(n_aff, kt + 1)
                else:
                    act.wait_ge(n_aff2, kt - len(NORM_AT) + 1)
                act.activation(x_hi[:, kt, :], xT[:, kt, :], ACT.Copy).then_inc(n_hi, 1)

            for e in range(EC):
                if e >= NW:
                    act.wait_ge(m_used, e - NW + 1)
                hi(e, e % NR, LOADED[("e", e)])
                if e % EPG == LAG - 1 and e >= EPG:
                    group_out(e // EPG - 1)
                kt = e - X_AT - LAG + 1
                if 0 <= kt < KT:
                    act.wait_ge(xt_t, kt + 1)
                    act.activation(xT[:, kt, :], bank(2 * (kt % 2), 2)[:, 0:T], ACT.Copy).then_inc(xt_ev, 1)
                if e == X_AT:
                    act.wait_ge(lam_dot, 2)
                    act.activation(tiny[:, 4:6], tiny[:, 6:8], ACT.Exp).then_inc(lam_exp, 1)
                if e == SUM_AT + LAG:
                    root(0, n0_rstd[:, :])
                if e in NORM_AT:
                    h_hi(NORM_AT[e])
            def late_mul(n):
                x = ("mod", n)
                act.wait_ge(ld_raw[RAW_OF[x] % NR], LOADED[x])
                if n:
                    act.wait_ge(late_p, n)
                if n == LATE1:
                    act.wait_ge(x_ok, 2 * KT)
                for k in range(LK):
                    kt = LK * (n % LPG) + k
                    ins = act.activation(late_prod[:, LG * k:LG * k + LG], w_raw[RAW_OF[x] % NR][:, LG * k:LG * k + LG],
                                         ACT.Copy, scale=cs[:, kt, 1:2])
                ins.then_inc(late_act, 1)

            def softmax_exp(t):
                act.wait_ge(t_ttr, t + 1)
                st = stats[:, t % 4, :]
                for np_, _pc, sc, n, _tc, _e, _q, _k, i in segments(t):
                    n += 0 if is_a(t) else 1
                    sb = scores[t % 2][0:np_, sc:sc + n]
                    ins = act.activation(sb, sb, ACT.Exp, bias=st[0:np_, 4 + i:5 + i],
                                         accum_out=st[0:np_, 8 + i:9 + i])
                ins.then_inc(t_exp, 1)

            hi_early(0)
            hi_early(1)
            group_out(E_GROUPS - 1)
            for kt in range(len(NORM_AT), KT):
                scale_shift(kt)
                if kt > len(NORM_AT):
                    h_hi(kt - 1)
            h_hi(KT - 1)
            for k, (hf, part, parts, t, item) in enumerate(SLOTS):
                pt, pp = prev_out(k, 1), prev_out(k, 2)
                if t is not None and scored_ahead(t):
                    softmax_exp(t)
                if pt is not None and is_a(pt):
                    act.wait_ge(b6_done, USE6[("p", pt)])
                    if pv_blocks(pt)[0][0] == P:
                        n = P * len(pv_blocks(pt)[0][3])
                        act.activation(probsT[:, 0:n], B6[:, 0:n], ACT.Copy).then_inc(b6_free, 1)
                    else:
                        act.activation(probsT[:, 0:P], B6[:, 0:P], ACT.Copy)
                        act.activation(probsT[0:TS, P:P + TS], B6[0:TS, P:P + TS], ACT.Copy).then_inc(b6_free, 1)
                if pp is not None:
                    act.wait_ge(t_ot, OUT_COUNT[pp])
                    if TURNS[pp][0] >= KT - 4:
                        act.wait_ge(m_late, LATE1 // LPG * LGT)
                    for n, c, tok, _b in pv_blocks(pp):
                        ins = act.activation(oT[:, TURNS[pp][0], tok:tok + n],
                                             B7[:, 256 + c:256 + c + n], ACT.Copy)
                    ins.then_inc(t_otev, 1)
                if t is not None and not scored_ahead(t):
                    softmax_exp(t)
                if hf is not None and part == 0 and hf + 2 < FC0:
                    hi_early(hf + 2)
                begin, end = late_of(hf, part, parts)
                for n in begin:
                    late_mul(n)
                if hf is None:
                    for kt in TAIL_SPLITS[k - TAIL]:
                        act.wait_ge(g_done, ZH)
                        act.wait_ge(t_otev, len(OUTS) if kt == KT - 1 else OUT_COUNT[4 * (kt - 8) + 51] if kt >= 8
                                    else OUT_COUNT[6 * kt + 5])
                        act.activation(x_hi[:, kt, :], oT[:, kt, :], ACT.Copy).then_inc(n_hi, 1)
                if pt is not None:
                    act.wait_ge(t_pv, OUT_COUNT[pt])
                    act.wait_ge(t_comb, OUT_COUNT[pt])
                    st = stats[:, pt % 4, :]
                    if is_a(pt):
                        n = pv_blocks(pt)[0][0]
                        inv = st[0:n, 12:13]
                        act.activation(o_raw[0:n, :], B7[0:n, 0:P], ACT.Copy, scale=inv)
                        act.activation(square[0:n, :], B7[0:n, 0:P], ACT.Square, scale=inv,
                                       accum_out=st[0:n, 17:18]).then_inc(t_o, 1)
                    else:
                        for o, (n, c, _tok, _b) in enumerate(pv_blocks(pt)):
                            for e in range(2):
                                a = c + 64 * e
                                ins = act.activation(o_norm[0:n, a:a + 64], B7[0:n, a:a + 64], ACT.Copy,
                                                     scale=st[0:n, 12 + 2 * o + e:13 + 2 * o + e])
                        ins.then_inc(t_on_b, 1)
                if item:
                    ki, x = item
                    act.wait_ge(b6_done, USE6[("x", ki, x)])
                    if x == "v":
                        if ki >= 2:
                            act.wait_ge(st_v, 32 * (ki - 1))
                        act.activation(v_nat[ki % 2][:, 0:512], B6[:, :], ACT.Copy).then_inc(b6_free, 1)
                    elif x == "s":
                        if ki:
                            act.wait_ge(st_k, 32 * ki)
                        act.activation(v_nat[ki % 2][0:TS, 4 * P:5 * P], B6[0:TS, 0:P], ACT.Copy)
                        act.activation(k_nat[0:TS, 4 * P:5 * P], B6[0:TS, P:2 * P], ACT.Copy).then_inc(b6_free, 1)
                    elif x == "p":
                        n = 4 * P if ki < A_HEADS else P
                        act.activation(past_kT[:, 0:n], B6[:, 0:n], ACT.Copy).then_inc(b6_free, 1)
                    else:
                        c0 = 0 if ki < A_HEADS else 3 * P
                        act.activation(k_nat[:, c0:512], B6[:, c0:512], ACT.Copy).then_inc(b6_free, 1)
                for n in end:
                    late_mul(n)
            for hf in range(ZH, ZH + OH):
                if hf + 2 < FC0:
                    hi_early(hf + 2)
                for x in late_of(hf, 0, 1):
                    for n in x:
                        late_mul(n)

            def hi_ffn(f):
                n, i = f
                count = FFN_RAW[n % NR] + 16 * (n // NR + 1)
                hi(n, n % NR, count if i is None else i * (LOOP_CHUNKS // NR * 16) + count)

            act.wait_ge(g_done, ZH + OH - 2)
            hi_ffn((0, None))
            hi_ffn((1, None))
            act.wait_ge(g_done, ZH + OH)
            hi_ffn((2, None))
            hi_ffn((3, None))
            root(1, n2_rstd[:, :])

            def h2_affine(i):
                kt, src, dst = i % KT, h2_t(i), h2_h(i)
                c = PIECES[i // KT][0][1]
                act.wait_ge(n_mul, KT + i + 1)
                if i >= 4:
                    act.wait_ge(x_ok, 2 * KT + i - 3)
                act.activation(dst[:, 0:c], src[:, 0:c], ACT.Identity, bias=mod[:, SH_F + kt, 0:1],
                               scale=mod[:, SC_F + kt, 0:1]).then_inc(h2_ok, 1)

            def h2_hi(i):
                kt, (a, c) = i % KT, HALF[i // KT]
                act.wait_ge(h2_ok, i + 1)
                if i >= KT:
                    act.wait_ge(h2_sample, kt + 1)
                act.activation(x_hi[:, kt, a:a + c], h2_h(i)[:, 0:c], ACT.Copy).then_inc(n_hi, 1)

            for i in range(2 * KT):
                h2_affine(i)
                if i:
                    h2_hi(i - 1)
            h2_hi(2 * KT - 1)
            act.wait_ge(x_ok, 4 * KT)

            def u_copy(x, h, count):
                act.wait_ge(u_done, count)
                for a, n, g in PIECES[h]:
                    ins = act.activation(ext[x][:, a + 2 + 2 * g:a + 2 + 2 * g + n],
                                         bank(2 * x + h)[:, a - HALF[h][0]:a - HALF[h][0] + n], ACT.Copy)
                ins.then_inc(u_ev, 1)

            def hidden(J, par, jj, f, has_down):
                at = lambda n: (f[0] + n, f[1])
                first = isinstance(J, int) and J == 0
                act.wait_ge(u_done, J * 4 + 1)
                if not first:
                    hi_ffn(at(2))
                    hi_ffn(at(3))
                    act.wait_ge(c_gate, J)
                u_copy(0, 0, J * 4 + 1)
                u_copy(0, 1, J * 4 + (3 if first else 2))
                hi_ffn(at(4))
                hi_ffn(at(5))
                if not first:
                    act.wait_ge(c_val, J)
                u_copy(1, 0, J * 4 + (2 if first else 3))
                u_copy(1, 1, J * 4 + 4)
                if has_down:
                    hi_ffn(at(6))
                    hi_ffn(at(7))
                act.wait_ge(c_gate, J + 1)
                act.activation(cv[0][:, :], cv[0][:, :], ACT.Silu).then_inc(c_silu, 1)
                act.wait_ge(y_mul, J + 1)
                for a, n, g in ((0, TP, 0), (TP, TS, 1)):
                    ins = act.activation(y_hi[par][:, jj, a:a + n], cv[1][:, a + 2 * g:a + 2 * g + n], ACT.Copy)
                ins.then_inc(y_hi_ok, 1)

            for jj in range(GRP):
                hidden(jj, 0, jj, (4 * jj, None), False)
            with act.Fori(0, (NG - 1) // 2) as i:
                for gg in range(2):
                    for jj in range(GRP):
                        hidden(i * (2 * GRP) + (GRP * (gg + 1) + jj), (gg + 1) % 2, jj,
                               (4 * GRP + 24 * gg + 6 * jj, i), True)
            def squares(kts):
                for kt in kts:
                    act.wait_ge(d_ev, 4 + 8 * GRP * (NG - 1) + 2 * kt + 2)
                    if kt >= 2:
                        act.wait_ge(f_add, kt - 1)
                    act.activation(f_sq[kt % 2][:, 0:T], x1[:, kt, :], ACT.Square).then_inc(f_square, 1)

            def y_out(kts):
                for kt in kts:
                    act.wait_ge(f_t, kt + 1)
                    b = 2 * (kt % 2)
                    act.activation(y_nat[:, 0:QT, P * kt:P * kt + P],
                                   bank(b)[:, :].rearrange("p (t n) -> p t n", n=P), ACT.Copy)
                    act.activation(y_nat[0:TS, QT, P * kt:P * kt + P], bank(b + 1)[0:TS, 0:P], ACT.Copy
                                   ).then_inc(f_ev, 1)

            base = 8 * GRP * (NG - 1)
            act.wait_ge(d_done, base - 4)
            hi_ffn((LAST_DOWN + 2, None))
            act.wait_ge(d_done, base)
            hi_ffn((LAST_DOWN + 3, None))
            for n in range(8):
                if n + 4 < 8:
                    act.wait_ge(d_done, base + 4 * (n + 1))
                    hi_ffn((LAST_DOWN + n + 4, None))
                squares(range(2 * n, 2 * n + 2))
                if n:
                    y_out(range(2 * n - 2, 2 * n))
            y_out(range(KT - 2, KT))
            act.wait_ge(f_sum_t, 1)
            act.activation(tiny[:, 8:8 + QT], bank(0)[:, 0:QT], ACT.Sqrt, bias=eps, scale=1.0 / D)
            act.activation(tiny[0:TS, 8 + QT:9 + QT], bank(0)[0:TS, QT:QT + 1], ACT.Sqrt, bias=eps[0:TS, :],
                           scale=1.0 / D).then_inc(f_sd, 1)
            act.wait_ge(f_rs, 1)
            act.wait_ge(f_ev, KT)
            for t in (2, 3):
                act.activation(y_nat[:, t, :], y_nat[:, t, :], ACT.Copy, scale=tiny[:, 8 + t:9 + t]).then_inc(f_sca, 1)
            act.wait_ge(uc_t, 1)
            act.activation(u_rows[0:2 * FT, :, :].rearrange("p r n -> p (r n)"), bank(3)[0:2 * FT, :], ACT.Copy
                           ).then_inc(uc_ev, 1)

        @block.vector
        def _(dve):
            own = [0]

            def step(ins):
                own[0] += 1
                ins.then_inc(dve_own, 1)
                dve.wait_ge(dve_own, own[0])

            def row_out(i):
                n = ROW_COUNTS[i]
                dve.wait_ge(rows_t, i + 1)
                dve.tensor_copy(cols[:, i, 0:n], psw[:, 2048 + P * i:2048 + P * i + n]).then_inc(rows_ev, 1)

            row_out(0)
            dve.wait_ge(c_hi, 1)
            dve.tensor_tensor(c_parts[:, :, 2:4], cs[:, :, :], c_parts[:, :, 0:2].bitcast(F32), ALU.subtract
                              ).then_inc(c_lo, 1)

            def add_square(kt, x, sq, acc):
                if kt == 0:
                    step(dve.tensor_tensor(acc, x[:, 0, :], x[:, 0, :], ALU.mult))
                    return
                step(dve.tensor_tensor(sq, x[:, kt, :], x[:, kt, :], ALU.mult))
                ins = dve.tensor_tensor(acc, acc, sq, ALU.add)
                if kt == KT - 1:
                    ins.then_inc(sq_ok, 1)
                else:
                    step(ins)

            def scales(row, g_row, count):
                for g in range(2):
                    ins = dve.scalar_tensor_tensor(out=mod[:, row:row + count, g], in0=mod[:, row:row + count, g],
                                                   scalar=1.0, in1=cols[:, GT, g_row:g_row + count],
                                                   op0=ALU.add, op1=ALU.mult)
                ins.then_inc(mod_ok, 1)

            def inverse(n, x):
                dve.wait_ge(sd_ok, n + 1)
                step(dve.reciprocal(x, x))

            def normalise():
                def mul(i):
                    kt, (a, n) = i % KT, HALF[i // KT]
                    dve.tensor_tensor(h2_t(i)[:, 0:n], x1[:, kt, a:a + n], n2_rstd[:, a:a + n], ALU.mult
                                      ).then_inc(n_mul, 1)
                for i in range(3):
                    mul(i)
                for i in range(2 * KT):
                    kt, (a, n) = i % KT, HALF[i // KT]
                    dve.wait_ge(n_hi, 2 * KT + i + 1)
                    dve.tensor_tensor(x_lo[:, kt, a:a + n], h2_h(i)[:, 0:n], x_hi[:, kt, a:a + n].bitcast(F32),
                                      ALU.subtract).then_inc(x_ok, 1)
                    if i + 3 < 2 * KT:
                        mul(i + 3)

            def lo(c, raw, nth):
                dve.wait_ge(s_hi, nth + 1)
                dve.tensor_tensor(w_lo[c % NW][:, :], w_raw[raw][:, :], w_hi[c % NW][:, :].bitcast(F32), ALU.subtract
                                  ).then_inc(s_lo, 1)

            def group_mod(g):
                t0 = early_tile(g)
                dve.wait_ge(e_t, g + 1)
                for st in range(2):
                    ins = dve.tensor_tensor(mod[:, t0:t0 + EGT, st], bank(5)[:, 2 * t0 + st:2 * (t0 + EGT):2],
                                            cols[:, BT, t0:t0 + EGT], ALU.add)
                ins.then_inc(e_tev, 1)
                if g % 2:
                    dve.wait_ge(e_tev, g + 1)
                    scales(t0, t0 - SC_A, EGT)

            def h_lo(kt):
                dve.wait_ge(n_hi, kt + 1)
                dve.tensor_tensor(x_lo[:, kt, :], xT[:, kt, :], x_hi[:, kt, :].bitcast(F32), ALU.subtract
                                  ).then_inc(x_ok, 1)

            for e in range(EC):
                lo(e, e % NR, e)
                if e == 6:
                    dve.wait_ge(rows_t, len(ROW_COUNTS))
                    for i in range(1, len(ROW_COUNTS)):
                        row_out(i)
                if e == 7:
                    dve.wait_ge(ld_small, 80)
                    for i in range(2):
                        a, b = lam[2 * i], lam[2 * i + 1]
                        dve.tensor_tensor_reduce(a[:, :], a[:, :], b[:, :], 1.0, 0.0, ALU.mult, ALU.add,
                                                 tiny[:, 6 + i:7 + i]).then_inc(lam_dot, 1)
                if e == X_AT + 2:
                    dve.wait_ge(lam_exp, 1)
                    step(dve.tensor_tensor(tiny[:, 3:4], tiny[:, 5:6], tiny[:, 4:5], ALU.subtract))
                    step(dve.tensor_scalar(neg_lam, tiny[:, 3:4], -LAMBDA_INIT, None, ALU.add))
                kt = e - X_AT - LAG
                if 1 <= kt < KT:
                    dve.wait_ge(sq_mul, kt + 1)
                    if kt > 1:
                        dve.wait_ge(sq_add, kt - 1)
                    ins = dve.tensor_tensor(n0_acc[:, :], n0_sq[0][:, :] if kt == 1 else n0_acc[:, :],
                                            n0_sq[kt % 2][:, :], ALU.add)
                    ins.then_inc(sq_ok if kt == KT - 1 else sq_add, 1)
                if e == SUM_AT + LAG:
                    dve.wait_ge(sd_ok, 1)
                    dve.reciprocal(n0_rstd[:, :], n0_rstd[:, :]).then_inc(rs_ok, 1)
                if e % EPG == LAG + 2 and e >= EPG:
                    group_mod(e // EPG - 1)
                if e in NORM_AT:
                    h_lo(NORM_AT[e])
            lo(0, RAW_OF[("w", 0)] % NR, EC)
            lo(1, RAW_OF[("w", 1)] % NR, EC + 1)
            group_mod(E_GROUPS - 1)
            for kt in range(len(NORM_AT), KT):
                h_lo(kt)

            def lo_early(c):
                lo(c, RAW_OF[("w", c)] % NR, EC + c)

            def late_out(hf):
                if hf not in SUM_OF:
                    return None
                g, t = SUM_OF[hf]
                tile = MOD_EARLY + LGT * g + t
                return dve.tensor_scalar(mod[:, tile, :], out_bank(hf)[:, H0:H0 + 2], cols[:, BT, tile:tile + 1], None,
                                         ALU.add)

            def late_sum(n):
                x = ("mod", n)
                g = n // LPG
                dve.wait_ge(ld_raw[RAW_OF[x] % NR], LOADED[x])
                if n % LPG == 0 and g >= 2:
                    dve.wait_ge(m_late, LGT * (g - 1))
                if n == LATE1:
                    dve.wait_ge(x_ok, 2 * KT)
                for k in range(LK):
                    kt = LK * (n % LPG) + k
                    w, c = w_raw[RAW_OF[x] % NR][:, LG * k:LG * k + LG], cs[:, kt, 0:1]
                    if kt == 0:
                        ins = dve.tensor_scalar(acc_d[g % 2], w, c, None, ALU.mult)
                    else:
                        dve.wait_ge(late_d, KT * g + kt)
                        ins = dve.scalar_tensor_tensor(out=acc_d[g % 2], in0=w, scalar=c, in1=acc_d[g % 2],
                                                       op0=ALU.mult, op1=ALU.add)
                    ins.then_inc(late_d, 1)

            def z_out(hf):
                dve.wait_ge(g_done, hf + 1)
                x, i = SLABS[hf // 2]
                buf = zq[i % 2] if x == "q" else zk[i % 2] if x == "k" else zv
                a, n = HALF[hf % 2]
                ins = dve.tensor_scalar(buf[:, a:a + n], G[hf % 2][:, 0:n], SCALE if x == "q" else 1.0, None, ALU.mult)
                (late_out(hf) or ins).then_inc(g_free, 1)

            def softmax_max(t):
                qi, i = TURNS[t]
                dve.wait_ge(t_score, t + 1)
                if any(x < t for x in OUTS):
                    dve.wait_ge(t_comb, max(OUT_COUNT[x] for x in OUTS if x < t))
                dve.wait_ge(tab_ok, qi + 1)
                st, sb, segs = stats[:, t % 4, :], scores[t % 2], segments(t)
                head = lambda e: 8 * ((qi - A_HEADS) // 4) + (qi - A_HEADS) % 4 + 4 * e
                if not is_a(t):
                    for np_, c, w in ((P, 256, 257),) if i < 3 else ((P, P, 129), (TS, 258 + 160, 161)):
                        dve.tensor_copy(sb[0:np_, c:c + w + 1:w], sinks[0:np_, head(0):head(0) + 5:4])
                for np_, pc, sc, n, tc, e, _q, _k, c in segs:
                    first = LOWEST if is_a(t) else sinks[0:np_, head(e):head(e) + 1]
                    ins = dve.tensor_tensor_reduce(sb[0:np_, sc:sc + n], S[t % 2][0:np_, pc:pc + n],
                                                   tab[qi % 2][0:np_, tc:tc + n], 1.0, first, ALU.add, ALU.max,
                                                   st[0:np_, c:c + 1])
                step(ins)
                groups = ([(P, 0, 2)] if i < 4 else [(TS, i - 4, i - 3)]) if is_a(t) else \
                    [(P, 0, 2)] if i < 3 else [(P, 0, 2), (TS, 2, 4)]
                for np_, c0, c1 in groups:
                    ins = dve.tensor_scalar(st[0:np_, 4 + c0:4 + c1], st[0:np_, c0:c1], -1.0, None, ALU.mult)
                ins.then_inc(t_ttr, 1)

            def combine(t):
                qi, i = TURNS[t]
                dve.wait_ge(t_exp, t + 1)
                st = stats[:, t % 4, :]
                if not is_a(t):
                    ins = dve.reciprocal(st[:, 12:14], st[:, 8:10])
                    if i == 3:
                        ins = dve.reciprocal(st[0:TS, 14:16], st[0:TS, 10:12])
                    ins.then_inc(t_comb, 1)
                    return
                if i < 4:
                    n, np_, st0_, p0 = P * (i + 1), P, st, scores[t % 2][:, 0:P * (i + 1)]
                    p1, out = scores[t % 2][:, 512:512 + n], p0
                else:
                    n, np_, st0_, p0 = PAST + TS, TS, stats[:, (t - 1) % 4, :], scores[(t - 1) % 2][0:TS, 0:PAST + TS]
                    p1 = out = scores[t % 2][0:TS, 0:n]
                dve.reciprocal(st[0:np_, 12:13], st0_[0:np_, 8:9])
                step(dve.reciprocal(st[0:np_, 13:14], st[0:np_, 9:10]))
                step(dve.tensor_scalar(st[0:np_, 16:17], st0_[0:np_, 8:9], st[0:np_, 13:14], neg_lam[0:np_, :],
                                       ALU.mult, ALU.mult))
                dve.scalar_tensor_tensor(out=out, in0=p1, scalar=st[0:np_, 16:17], in1=p0, op0=ALU.mult, op1=ALU.add
                                         ).then_inc(t_comb, 1)

            for k, (hf, part, parts, t, item) in enumerate(SLOTS):
                pt = prev_out(k, 1)
                if (hf and part == 0) or k == TAIL:
                    z_out(hf - 1 if hf else ZH - 1)
                if hf == 5:
                    dve.wait_ge(ld_sub, 16)
                    dve.tensor_scalar(gsub[:, :], gsub[:, :], 1.0 - LAMBDA_INIT, None, ALU.mult).then_inc(small_ok, 1)
                    dve.wait_ge(small_ok, 1)
                if t is not None and not scored_ahead(t):
                    softmax_max(t)
                if pt is not None and not is_a(pt):
                    dve.wait_ge(b6_done, USE6[("p", pt)])
                    if TURNS[pt][1] < 3:
                        dve.tensor_copy(probsT[:, :], B6[:, :]).then_inc(b6_free, 1)
                    else:
                        dve.tensor_copy(probsT[:, 0:2 * P], B6[:, 0:2 * P])
                        for e in range(2):
                            c = 256 + 64 * e
                            dve.tensor_copy(probsT[:, c:c + TS], B6[:, c:c + TS])
                            ins = dve.tensor_copy(probsT[0:TS, c + TS:c + 2 * TS], B6[0:TS, c + TS:c + 2 * TS])
                        ins.then_inc(b6_free, 1)
                if hf is not None and part == 0 and hf + 2 < FC0:
                    lo_early(hf + 2)
                if hf is None:
                    for kt in TAIL_SPLITS[k - TAIL]:
                        dve.wait_ge(n_hi, KT + kt + 1)
                        dve.tensor_tensor(x_lo[:, kt, :], oT[:, kt, :], x_hi[:, kt, :].bitcast(F32), ALU.subtract
                                          ).then_inc(x_ok, 1)
                if t is not None and has_out(t):
                    combine(t)
                if next_ahead(k) is not None:
                    softmax_max(next_ahead(k))
                begin, end = late_of(hf, part, parts)
                for n in begin:
                    late_sum(n)
                if pt is not None and is_a(pt):
                    dve.wait_ge(t_rstd, OUT_A[pt])
                    n = pv_blocks(pt)[0][0]
                    dve.scalar_tensor_tensor(out=o_norm[0:n, 0:P], in0=o_raw[0:n, :], scalar=stats[0:n, pt % 4, 19:20],
                                             in1=gsub[0:n, :], op0=ALU.mult, op1=ALU.mult).then_inc(t_on_a, 1)
                for n in end:
                    late_sum(n)

            def gated(n, h, b, gate):
                for a, m, g in PIECES[h]:
                    ins = dve.scalar_tensor_tensor(out=x1[:, n, a:a + m], in0=b[:, a - HALF[h][0]:a - HALF[h][0] + m],
                                                   scalar=mod[:, gate + n, g:g + 1], in1=x1[:, n, a:a + m],
                                                   op0=ALU.mult, op1=ALU.add)
                return ins

            for hf in range(ZH, ZH + OH):
                if hf + 2 < FC0:
                    lo_early(hf + 2)
                n, h = (hf - ZH) // 2, hf % 2
                if h == 0 and n % 4 == 0:
                    dve.wait_ge(xr[n // 4], 16)
                dve.wait_ge(g_done, hf + 1)
                ins = gated(n, h, out_bank(hf), GT_A)
                (late_out(hf) or ins).then_inc(g_free, 1)
                for x in late_of(hf, 0, 1):
                    for c in x:
                        late_sum(c)
                if h:
                    dve.wait_ge(g_free, hf + 1)
                    add_square(n, x1, n2_sq[:, :], n2_acc[:, :])

            dve.wait_ge(g_free, ZH + OH)
            scales(SC_F, KT, KT)

            def lo_ffn(f):
                n, i = f
                lo(n, n % NR, SC0 + n if i is None else i * LOOP_CHUNKS + (SC0 + n))

            for n in range(4):
                lo_ffn((n, None))
            inverse(1, n2_rstd[:, :])
            dve.wait_ge(mod_ok, KT // EGT + 1)
            normalise()
            dve.wait_ge(x_ok, 4 * KT)
            for x in range(2):
                ins = dve.memset(ext[x][:, 0:2], 0.0)
            ins.then_inc(d_ev, 4)

            def conv(x, J, done):
                tile = J + FT * x
                dve.tensor_copy(ext[x][:, TP + 2:TP + 4], cols[:, STATE:STATE + 2, bass.ds(tile, 1)]
                                .rearrange("p a b -> p (a b)")).then_inc(ext_ok, 1)
                dve.wait_ge(ext_ok, J * 2 + (x + 1))
                dve.tensor_copy(u_last[:, bass.ds(tile, 1), :].rearrange("p o (a b) -> p (o a) b", b=2),
                                ext[x][:, TP:TP + 2 * (TS + 2)].rearrange("p (a b) -> p a b", b=TS + 2)[:, :, 0:2])
                w = lambda i: cols[:, CONV_W + i, bass.ds(tile, 1)]
                dve.tensor_scalar(cv[x][:, :], ext[x][:, 2:T + 4], w(2), cols[:, CONV_B, bass.ds(tile, 1)],
                                  ALU.mult, ALU.add).then_inc(cv_ok, 1)
                dve.wait_ge(cv_ok, J * 4 + (2 * x + 1))
                dve.scalar_tensor_tensor(out=cv[x][:, :], in0=ext[x][:, 1:T + 3], scalar=w(1), in1=cv[x][:, :],
                                         op0=ALU.mult, op1=ALU.add).then_inc(cv_ok, 1)
                dve.wait_ge(cv_ok, J * 4 + (2 * x + 2))
                dve.scalar_tensor_tensor(out=cv[x][:, :], in0=ext[x][:, 0:T + 2], scalar=w(0), in1=cv[x][:, :],
                                         op0=ALU.mult, op1=ALU.add).then_inc(done, 1)

            def down_out(q, jj, Jd):
                dve.wait_ge(d_done, Jd * 8 + (q + 1))
                gated(4 * jj + q // 2, q % 2, bank(4 + q % 4), GT_F).then_inc(d_ev, 1)

            def hidden(J, par, jj, f, has_down):
                at = lambda n: (f[0] + n, f[1])
                if not isinstance(J, int) or J:
                    lo_ffn(at(2))
                    lo_ffn(at(3))
                dve.wait_ge(u_ev, J * 4 + 2)
                conv(0, J, c_gate)
                lo_ffn(at(4))
                lo_ffn(at(5))
                dve.wait_ge(u_ev, J * 4 + 4)
                conv(1, J, c_val)
                out = (lambda q: down_out(q, jj, J - GRP)) if has_down else (lambda q: None)
                out(0)
                dve.wait_ge(c_val, J + 1)
                dve.wait_ge(c_silu, J + 1)
                dve.tensor_tensor(cv[1][:, :], cv[0][:, :], cv[1][:, :], ALU.mult).then_inc(y_mul, 1)
                out(1)
                if has_down:
                    lo_ffn(at(6))
                    lo_ffn(at(7))
                out(2)
                out(3)
                dve.wait_ge(y_hi_ok, J + 1)
                for a, n, g in ((0, TP, 0), (TP, TS, 1)):
                    ins = dve.tensor_tensor(y_lo[par][:, jj, a:a + n], cv[1][:, a + 2 * g:a + 2 * g + n],
                                            y_hi[par][:, jj, a:a + n].bitcast(F32), ALU.subtract)
                ins.then_inc(y_ok, 1)
                for q in range(4, 8):
                    out(q)

            for jj in range(GRP):
                hidden(jj, 0, jj, (4 * jj, None), False)
            with dve.Fori(0, (NG - 1) // 2) as i:
                for gg in range(2):
                    for jj in range(GRP):
                        hidden(i * (2 * GRP) + (GRP * (gg + 1) + jj), (gg + 1) % 2, jj,
                               (4 * GRP + 24 * gg + 6 * jj, i), True)
            lo_ffn((LAST_DOWN + 2, None))
            lo_ffn((LAST_DOWN + 3, None))
            for n in range(8):
                for q in range(4 * (n % 2), 4 * (n % 2) + 4):
                    down_out(q, n // 2, GRP * (NG - 1) + n // 2)
                for kt in (2 * n, 2 * n + 1):
                    dve.wait_ge(d_ev, 4 + 8 * GRP * (NG - 1) + 2 * kt + 2)
                    if kt >= 2:
                        dve.wait_ge(f_t, kt - 1)
                    dve.tensor_scalar(xg[kt % 2][:, :], x1[:, kt, :], cols[:, GT, 2 * KT + kt:2 * KT + kt + 1], None,
                                      ALU.mult).then_inc(f_mul, 1)
                if n + 4 < 8:
                    lo_ffn((LAST_DOWN + n + 4, None))
            dve.wait_ge(f_sd, 1)
            dve.reciprocal(tiny[:, 8:8 + QT], tiny[:, 8:8 + QT])
            dve.reciprocal(tiny[0:TS, 8 + QT:9 + QT], tiny[0:TS, 8 + QT:9 + QT]).then_inc(f_rs, 1)
            dve.wait_ge(f_rs, 1)
            dve.wait_ge(f_ev, KT)
            for t in (0, 1, QT):
                n = P if t < QT else TS
                dve.tensor_scalar(y_nat[0:n, t, :], y_nat[0:n, t, :], tiny[0:n, 8 + t:9 + t], None, ALU.mult
                                  ).then_inc(f_scd, 1)

        @block.tensor
        def _(pe):
            def row(i):
                n = ROW_COUNTS[i]
                pe.transpose(psw[:, 2048 + P * i:2048 + P * i + n], rows[0:n, i, :], ident[0:n, 0:n]).then_inc(rows_t, 1)

            pe.wait_ge(consts, 5)
            pe.wait_ge(ld_c, 32)
            row(0)

            def sum_squares(n, acc):
                pe.wait_ge(sq_ok, n + 1)
                b = 4 if n else 0
                pe.matmul(bank(b), ones[:, :], acc[:, 0:TP], start=True, stop=True)
                pe.matmul(bank(b + 1)[:, 0:TS], ones[:, :], acc[:, TP:T], start=True, stop=True).then_inc(ss_ok, 1)

            def group_columns(g):
                pe.wait_ge(e_ev, g + 1)
                if g:
                    pe.wait_ge(e_tev, g)
                for t in range(EGT):
                    col = 2 * (early_tile(g) + t)
                    mm = pe.matmul(bank(5)[:, col:col + 2], mod_rows[g % 2][0:4, P * t:P * t + P], pair[0:4, :],
                                   start=True, stop=True)
                mm.then_inc(e_t, 1)

            pe.wait_ge(c_lo, 1)
            for e in range(EC):
                g, first = e // EPG, e % EPG == 0
                if first and g >= 2:
                    pe.wait_ge(e_ev, g - 1)
                if e == EPG:
                    pe.wait_ge(rows_ev, len(ROW_COUNTS))
                pe.wait_ge(s_lo, e + 1)
                for k in range(EK):
                    kt = EK * (e % EPG) + k
                    for part in (w_hi, w_lo):
                        mm = pe.matmul(bank(7 - g % 2)[0:4, :], c_parts[:, kt, :], part[e % NW][:, EG * k:EG * k + EG],
                                       start=(kt == 0 and part is w_hi), stop=(kt == KT - 1 and part is w_lo))
                mm.then_inc(m_used, 1)
                if e == 5:
                    pe.wait_ge(ld_rows, 16 * 10)
                    for i in range(1, len(ROW_COUNTS)):
                        row(i)
                kt = e - X_AT
                if 0 <= kt < KT:
                    if kt == 0:
                        pe.wait_ge(ld_x, 16 * (QT + 1))
                    if kt >= 2:
                        pe.wait_ge(xt_ev, kt - 1)
                    b = bank(2 * (kt % 2), 2)
                    for t in range(QT):
                        pe.transpose(b[:, P * t:P * t + P], x_nat[t][:, P * kt:P * kt + P], ident[:, :])
                    pe.transpose(b[:, TP:T], x_nat[QT][0:TS, P * kt:P * kt + P], ident[0:TS, 0:TS]).then_inc(xt_t, 1)
                if e == SUM_AT + 2:
                    pe.wait_ge(xt_ev, KT)
                    sum_squares(0, n0_acc)
                if e % EPG == LAG and e >= EPG:
                    group_columns(g - 1)
            group_columns(E_GROUPS - 1)

            def products(out, n, hi_w, lo_w, hi_x, lo_x, first, last):
                pe.matmul(out[:, 0:n], hi_w, hi_x, start=first, stop=False)
                pe.matmul(out[:, 0:n], hi_w, lo_x, start=False, stop=False)
                return pe.matmul(out[:, 0:n], lo_w, hi_x, start=False, stop=last)

            def late_tile(g, t, hf):
                pe.wait_ge(late_d, KT * (g + 1))
                pe.wait_ge(late_p, LPG * (g + 1))
                for st, acc in enumerate((acc_d, acc_p)):
                    mm = pe.matmul(out_bank(hf)[:, H0 + st:H0 + st + 1], acc[g % 2][:, P * t:P * t + P], ones[:, 0:1],
                                   start=True, stop=True)
                mm.then_inc(m_late, 1)

            def tiles(hf, kts):
                s, h = hf // 2, hf % 2
                a, n = HALF[h]
                for kt in kts:
                    c = 2 * s + kt // BLK
                    if kt == 0:
                        if hf >= 2:
                            pe.wait_ge(g_free, hf - 1 if hf < ZH + 2 else max(hf - 3, ZH))
                        if hf == ZH + 2:
                            pe.wait_ge(t_ttr, len(TURNS))
                        if hf in SUM_OF:
                            late_tile(*SUM_OF[hf], hf)
                    if kt % BLK == 0 and h == 0:
                        pe.wait_ge(s_lo, EC + c + 1)
                    if hf in (0, ZH):
                        pe.wait_ge(x_ok, (KT if hf else 0) + kt + 1)
                    w = slice(P * (kt % BLK), P * (kt % BLK) + P)
                    mm = products(out_bank(hf), n, w_hi[c % NW][:, w], w_lo[c % NW][:, w], x_hi[:, kt, a:a + n],
                                  x_lo[:, kt, a:a + n], kt == 0, kt == KT - 1)
                    if kt == KT - 1:
                        mm.then_inc(g_done, 1)

            def z_ready(ki_or_qi, what):
                pe.wait_ge(g_free, 2 * SLAB_OF[(what, ki_or_qi)] + 2)

            def score(t):
                qi, i = TURNS[t]
                ki = kv_of(qi)
                z_ready(qi, "q")
                z_ready(ki, "k")
                if t >= 2:
                    pe.wait_ge(t_ttr, t - 1)
                for np_, pc, _sc, _n, _tc, e, q0, keys, _c in segments(t):
                    r = slice(64 * e, 64 * e + 64)
                    for src, k0, n in keys:
                        if src == "past":
                            pe.wait_ge(b6_free, USE6[("x", ki, "p")])
                        kk = (past_kT if src == "past" else zk[ki % 2])[r, k0:k0 + n]
                        mm = pe.matmul(S[t % 2][0:np_, pc:pc + n], zq[qi % 2][r, q0:q0 + np_], kk,
                                       start=True, stop=True)
                        pc += n
                mm.then_inc(t_score, 1)

            def bank6(use):
                if use > 1:
                    pe.wait_ge(b6_free, use - 1)

            def turn_probs(t):
                if is_a(t):
                    pe.wait_ge(t_comb, OUT_COUNT[t])
                else:
                    pe.wait_ge(t_exp, t + 1)
                bank6(USE6[("p", t)])
                for np_, _c, _tok, blocks in pv_blocks(t):
                    for sc, n, _src, _tile, _vc, _vn, _oc, tc in blocks:
                        mm = pe.transpose(B6[0:n, tc:tc + np_], scores[t % 2][0:np_, sc:sc + n], ident[0:np_, 0:np_])
                mm.then_inc(b6_done, 1)

            def values(t):
                ki = kv_of(TURNS[t][0])
                pe.wait_ge(b6_free, max(USE6[("p", t)], USE6[("x", ki, "s" if TURNS[t][1] >= 3 else "v")]))
                prev = OUT_COUNT[t] - 1
                if prev:
                    pe.wait_ge(t_otev, prev)
                for np_, _c, tok, blocks in pv_blocks(t):
                    if tok == TP:
                        pe.wait_ge(ld_pv, 16 * (ki + 1))
                    for j, (_sc, n, src, tile, vc, vn, oc, tc) in enumerate(blocks):
                        v = (past_v if src == "past" else v_nat[ki % 2])[0:n, P * tile + vc:P * tile + vc + vn]
                        first = j == 0 or blocks[j - 1][6] != oc
                        last = j == len(blocks) - 1 or blocks[j + 1][6] != oc
                        mm = pe.matmul(B7[0:np_, oc:oc + vn], probsT[0:n, tc:tc + np_], v, start=first, stop=last)
                mm.then_inc(t_pv, 1)

            def turn_output(t):
                if is_a(t):
                    pe.wait_ge(t_on_a, OUT_A[t])
                else:
                    pe.wait_ge(t_on_b, OUT_B[t])
                for np_, c, _tok, _b in pv_blocks(t):
                    mm = pe.transpose(B7[:, 256 + c:256 + c + np_], o_norm[0:np_, c:c + P], ident[0:np_, 0:np_])
                mm.then_inc(t_ot, 1)

            def kv_item(ki, x):
                z_ready(ki, "v" if x in "vs" else "k")
                bank6(USE6[("x", ki, x)])
                if x == "v":
                    for t in range(QT):
                        mm = pe.transpose(B6[:, P * t:P * t + P], zv[:, P * t:P * t + P], ident[:, :])
                elif x == "s":
                    pe.transpose(B6[0:TS, 0:P], zv[:, TP:T], ident[:, :])
                    mm = pe.transpose(B6[0:TS, P:2 * P], zk[ki % 2][:, TP:T], ident[:, :])
                elif x == "p":
                    pe.wait_ge(ld_pk, 16 * (ki + 1))
                    for t in range(4 if ki < A_HEADS else 1):
                        mm = pe.transpose(B6[:, P * t:P * t + P], past_k[:, P * t:P * t + P], ident[:, :])
                else:
                    for t in range(0 if ki < A_HEADS else 3, QT):
                        mm = pe.transpose(B6[:, P * t:P * t + P], zk[ki % 2][:, P * t:P * t + P], ident[:, :])
                mm.then_inc(b6_done, 1)

            for k, (hf, part, parts, t, item) in enumerate(SLOTS):
                pt, pp = prev_out(k, 1), prev_out(k, 2)
                n = KT // parts
                cut = [n * part + n * c // 4 for c in range(5)]

                def products_between(c):
                    if hf is not None:
                        tiles(hf, range(cut[c], cut[c + 1]))
                    elif k > TAIL and c in (1, 2):
                        tiles(ZH + c - 1, TAIL_SPLITS[k - TAIL - 1])

                if t is not None and not scored_ahead(t):
                    score(t)
                products_between(0)
                if pt is not None:
                    turn_probs(pt)
                products_between(1)
                if pp is not None:
                    turn_output(pp)
                products_between(2)
                if pt is not None:
                    values(pt)
                if next_ahead(k) is not None:
                    score(next_ahead(k))
                if item:
                    kv_item(*item)
                products_between(3)
            tiles(ZH, TAIL_SPLITS[-1])
            tiles(ZH + 1, TAIL_SPLITS[-1])
            for hf in range(ZH + 2, ZH + OH):
                tiles(hf, range(KT))
            sum_squares(1, n2_acc)
            pe.wait_ge(g_free, ZH + OH)

            def lo_ready(f):
                n, i = f
                pe.wait_ge(s_lo, SC0 + n + 1 if i is None else i * LOOP_CHUNKS + (SC0 + n + 1))

            def up(J, f, x, halves=(0, 1)):
                for h in halves:
                    a, n = HALF[h]
                    if not isinstance(J, int) or J:
                        pe.wait_ge(u_ev, J * 4 + (2 * x + h - 3))
                    for kt in range(KT):
                        c = f[0] + 2 * x + kt // BLK
                        if kt % BLK == 0 and h == 0:
                            lo_ready((c, f[1]))
                        if isinstance(J, int) and J == 0 and x == 0:
                            pe.wait_ge(x_ok, 2 * KT + KT * h + kt + 1)
                        w = slice(P * (kt % BLK), P * (kt % BLK) + P)
                        mm = products(bank(2 * x + h), n, w_hi[c % NW][:, w], w_lo[c % NW][:, w], x_hi[:, kt, a:a + n],
                                      x_lo[:, kt, a:a + n], kt == 0, kt == KT - 1)
                    mm.then_inc(u_done, 1)

            def down(Jd, f, par, halves=range(8)):
                for q in halves:
                    c, nn, h = f[0] + q // 4, q % 4 // 2, q % 2
                    if q % 4 == 0:
                        lo_ready((c, f[1]))
                    pe.wait_ge(d_ev, Jd * 8 + (q + 1))
                    a, n = HALF[h]
                    for kt in range(GRP):
                        w = slice(256 * kt + P * nn, 256 * kt + P * nn + P)
                        mm = products(bank(4 + q % 4), n, w_hi[c % NW][:, w], w_lo[c % NW][:, w], y_hi[par][:, kt, a:a + n],
                                      y_lo[par][:, kt, a:a + n], kt == 0, kt == GRP - 1)
                    mm.then_inc(d_done, 1)

            for h in range(2):
                up(0, (0, None), 0, (h,))
                up(0, (0, None), 1, (h,))
            for jj in range(1, GRP):
                up(jj, (4 * jj, None), 0)
                up(jj, (4 * jj, None), 1)
            with pe.Fori(0, (NG - 1) // 2) as i:
                for gg in range(2):
                    for jj in range(GRP):
                        J = i * (2 * GRP) + (GRP * (gg + 1) + jj)
                        f = (4 * GRP + 24 * gg + 6 * jj, i)
                        up(J, f, 0)
                        up(J, f, 1)
                        if jj == 0:
                            pe.wait_ge(y_ok, J)
                        down(J - GRP, (f[0] + 4, i), gg % 2)
            pe.wait_ge(y_ok, FT)

            def y_turn(kts):
                for kt in kts:
                    pe.wait_ge(f_mul, kt + 1)
                    if kt >= 2:
                        pe.wait_ge(f_ev, kt - 1)
                    b = bank(2 * (kt % 2), 2)
                    for t in range(QT):
                        pe.transpose(b[:, P * t:P * t + P], xg[kt % 2][:, P * t:P * t + P], ident[:, :])
                    pe.transpose(b[0:TS, 512:512 + P], xg[kt % 2][:, TP:T], ident[:, :]).then_inc(f_t, 1)

            pe.wait_ge(u_ev, 4 * FT)
            for n in range(8):
                down(GRP * (NG - 1) + n // 2, (LAST_DOWN + 2 * (n // 2), None), (NG - 1) % 2,
                     range(4 * (n % 2), 4 * (n % 2) + 4))
                if n:
                    y_turn(range(2 * n - 2, 2 * n))
            y_turn(range(KT - 2, KT))
            pe.wait_ge(f_ev, KT)
            pe.wait_ge(f_add, KT - 1)
            for t in range(QT + 1):
                n = P if t < QT else TS
                mm = pe.matmul(bank(0)[0:n, t:t + 1], f_sum[:, P * t:P * t + n], ones[:, 0:1], start=True, stop=True)
            mm.then_inc(f_sum_t, 1)
            pe.wait_ge(c_val, FT)
            for r in range(4):
                mm = pe.transpose(bank(3)[0:2 * FT, P * r:P * r + P], u_last[:, :, r], ident[:, :])
            mm.then_inc(uc_t, 1)


_INS = ["x_prompt", "x_sample", "cache_a_k", "cache_a_v", "cache_b_k", "cache_b_v", "state_conv", "c_prompt",
        "c_sample", "w_mod", "b_mod", "g_attn", "w_in", "lambda_q1", "lambda_k1", "lambda_q2", "lambda_k2",
        "subln_g", "sinks", "w_out", "g_ffn", "w_up", "conv_w", "conv_b", "w_down", "g_final"]
_OUTS = [("y_p", (1, TP, D)), ("y_s", (1, TS, D)), ("ak_p", (1, 1, TP, A_HEADS, 2 * A_DK)),
         ("av_p", (1, 1, TP, A_HEADS, A_DV)), ("bk_p", (1, 1, P, 4, B_DH)), ("bv_p", (1, 1, P, 4, B_DH)),
         ("conv_p", (1, 1, 2, 2 * DFF)), ("ak_s", (1, 1, TS, A_HEADS, 2 * A_DK)),
         ("av_s", (1, 1, TS, A_HEADS, A_DV)), ("bk_s", (1, 1, P, 4, B_DH)), ("bv_s", (1, 1, P, 4, B_DH)),
         ("conv_s", (1, 1, 2, 2 * DFF))]


def kernel(**inputs):
    import numpy as np
    import concourse.bacc as bacc
    from concourse.bass_utils import run_bass_kernel_spmd

    nc = bacc.Bacc("TRN2", target_bir_lowering=False, num_devices=1)
    arrays, A, O = {}, {}, {}
    for name in _INS:
        a = np.ascontiguousarray(inputs[name])
        arrays[f"in_{name}"] = a
        A[name] = nc.dram_tensor(f"in_{name}", a.shape, mybir.dt.from_np(a.dtype), kind="ExternalInput").ap()
    for name, shape in _OUTS:
        O[name] = nc.dram_tensor(f"out_{name}", shape, F32, kind="ExternalOutput").ap()
    build(nc, A, O)
    r = run_bass_kernel_spmd(nc, [arrays], core_ids=[0])
    return tuple(r.results[0][f"out_{name}"] for name, _ in _OUTS)
```
